# Optimizing a Trainium2 kernel written in Bass

```python
import jax
import jax.numpy as jnp
from jax import lax
import numpy as np

D_MODEL = 1024
BATCH = 1
SEQ = 512
DEPTH = 1

LRU_WIDTH = D_MODEL // 2
LRU_BLOCKS = 8
LRU_BLOCK = LRU_WIDTH // LRU_BLOCKS
CONV_WIDTH = 4
LRU_C = 8.0
NSA_HEADS = 8
HEAD_DIM = 64
NSA_WIDTH = NSA_HEADS * HEAD_DIM
NSA_KV_HEADS = 2
NSA_GROUP = NSA_HEADS // NSA_KV_HEADS
KV_WIDTH = NSA_KV_HEADS * HEAD_DIM
N_BRANCH = 3
CMP_STRIDE = 16
CMP_BLOCK = 2 * CMP_STRIDE
CMP_HIDDEN = 256
SEL_BLOCK = 64
SEL_TOPK = 16
WINDOW = 512
Q_BLOCK = 128
SEL_Q_CHUNK = 16
MIX_WIDTH = LRU_WIDTH + NSA_WIDTH
IN_SPLITS = (LRU_WIDTH, LRU_WIDTH, NSA_WIDTH, KV_WIDTH, KV_WIDTH, KV_WIDTH, KV_WIDTH, KV_WIDTH, KV_WIDTH, N_BRANCH * NSA_HEADS, NSA_WIDTH)
IN_WIDTH = sum(IN_SPLITS)
ATTN_SCALE = HEAD_DIM ** -0.5
NEG_INF = -1e30
FORCE = 1e6
EPS = 1e-6

kernel_name = 'hymba_rglru_nsa_alibi_adaln_block'

def rms_norm(x, g):
    xf = x.astype(jnp.float32)
    y = xf * lax.rsqrt(jnp.mean(xf * xf, axis=-1, keepdims=True) + EPS)
    return (y * g.astype(jnp.float32)).astype(x.dtype)

def alibi_slopes():
    h = jnp.arange(1, NSA_HEADS + 1, dtype=jnp.float32)
    return (2.0 ** (-8.0 * h / NSA_HEADS)).reshape(NSA_KV_HEADS, NSA_GROUP)

def masked_softmax(s, mask):
    return jax.nn.softmax(jnp.where(mask, s, NEG_INF), axis=-1)

def causal_depthwise_conv(x, w, b):
    y = lax.conv_general_dilated(x, w[:, None, :].astype(x.dtype), window_strides=(1,), padding=[(CONV_WIDTH - 1, 0)], dimension_numbers=('NWC', 'WIO', 'NWC'), feature_group_count=x.shape[-1])
    return y + b

def rg_lru(xc, w_a, b_a, w_x, b_x, lam):
    bsz, seq, _ = xc.shape
    xb = xc.reshape(bsz, seq, LRU_BLOCKS, LRU_BLOCK)
    r = jax.nn.sigmoid(jnp.einsum('bsni,nij->bsnj', xb, w_a).reshape(bsz, seq, LRU_WIDTH) + b_a)
    i = jax.nn.sigmoid(jnp.einsum('bsni,nij->bsnj', xb, w_x).reshape(bsz, seq, LRU_WIDTH) + b_x)
    log_a = -LRU_C * r.astype(jnp.float32) * jax.nn.softplus(-lam.astype(jnp.float32))
    a = jnp.exp(log_a)
    u = jnp.sqrt(-jnp.expm1(2.0 * log_a)) * (i * xc).astype(jnp.float32)

    def combine(left, right):
        a_l, h_l = left
        a_r, h_r = right
        return a_l * a_r, a_r * h_l + h_r

    _, h = lax.associative_scan(combine, (a, u), axis=1)
    return h.astype(xc.dtype)

def compress_blocks(kv, pos, w1, w2):
    bsz, seq, hk, dh = kv.shape
    chunks = kv.reshape(bsz, seq // CMP_STRIDE, CMP_STRIDE, hk, dh)
    blocks = jnp.concatenate([chunks[:, :-1], chunks[:, 1:]], axis=2) + pos[None, None, :, None, :]
    flat = jnp.moveaxis(blocks, 3, 2).reshape(bsz, seq // CMP_STRIDE - 1, hk, CMP_BLOCK * dh)
    return jax.nn.gelu(flat @ w1) @ w2

def nsa_branches(q, kc, vc, ks, vs, kw, vw, gate_logits):
    bsz, seq = q.shape[:2]
    n_cmp = kc.shape[1]
    n_sel = seq // SEL_BLOCK
    n_top = min(SEL_TOPK, n_sel)
    slopes = alibi_slopes()
    cmp_end = CMP_STRIDE * jnp.arange(n_cmp) + CMP_BLOCK - 1
    cmp_ids = jnp.arange(n_cmp)
    ratio = SEL_BLOCK // CMP_STRIDE
    overlap = jax.nn.one_hot(cmp_ids // ratio, n_sel, dtype=jnp.float32) + jax.nn.one_hot((cmp_ids + 1) // ratio, n_sel, dtype=jnp.float32)
    sel_ids = jnp.arange(n_sel)
    n_qb = seq // Q_BLOCK

    def cmp_step(i):
        t = i * Q_BLOCK + jnp.arange(Q_BLOCK)
        qb = lax.dynamic_slice_in_dim(q, i * Q_BLOCK, Q_BLOCK, axis=1)
        dist = (t[:, None] - cmp_end[None, :]).astype(jnp.float32)
        mask = dist >= 0
        s = jnp.einsum('bqhgd,bchd->bhgqc', qb, kc).astype(jnp.float32) * ATTN_SCALE - slopes[:, :, None, None] * dist
        p = jnp.where(mask, masked_softmax(s, mask), 0.0)
        o = jnp.einsum('bhgqc,bchd->bqhgd', p.astype(vc.dtype), vc)
        imp = jnp.einsum('bhgqc,cn->bqhn', p, overlap)
        cur = (t // SEL_BLOCK)[:, None, None]
        forced = (sel_ids == 0) | (sel_ids == cur) | (sel_ids == cur - 1)
        imp = jnp.where(forced, FORCE, jnp.where(sel_ids > cur, -FORCE, imp))
        _, idx = lax.top_k(imp, n_top)
        return o, idx

    o_cmp, sel_idx = lax.map(cmp_step, jnp.arange(n_qb))
    o_cmp = jnp.moveaxis(o_cmp, 0, 1).reshape(q.shape)
    sel_idx = jnp.moveaxis(sel_idx, 0, 1).reshape(bsz, seq, NSA_KV_HEADS, n_top)

    ks_b = ks.reshape(bsz, n_sel, SEL_BLOCK, NSA_KV_HEADS, HEAD_DIM).transpose(0, 3, 1, 2, 4)
    vs_b = vs.reshape(bsz, n_sel, SEL_BLOCK, NSA_KV_HEADS, HEAD_DIM).transpose(0, 3, 1, 2, 4)
    b_ix = jnp.arange(bsz)[:, None, None, None]
    h_ix = jnp.arange(NSA_KV_HEADS)[None, None, :, None]
    offs = jnp.arange(SEL_BLOCK)
    n_keys = n_top * SEL_BLOCK

    def slc_step(i):
        t = i * SEL_Q_CHUNK + jnp.arange(SEL_Q_CHUNK)
        qb = lax.dynamic_slice_in_dim(q, i * SEL_Q_CHUNK, SEL_Q_CHUNK, axis=1)
        ib = lax.dynamic_slice_in_dim(sel_idx, i * SEL_Q_CHUNK, SEL_Q_CHUNK, axis=1)
        kg = ks_b[b_ix, h_ix, ib]
        vg = vs_b[b_ix, h_ix, ib]
        kpos = ib[..., None] * SEL_BLOCK + offs
        dist = (t[None, :, None, None, None] - kpos).astype(jnp.float32)
        s = jnp.einsum('bqhgd,bqhnkd->bqhgnk', qb, kg).astype(jnp.float32) * ATTN_SCALE - slopes[None, None, :, :, None, None] * dist[:, :, :, None]
        mask = (dist >= 0)[:, :, :, None].reshape(bsz, SEL_Q_CHUNK, NSA_KV_HEADS, 1, n_keys)
        p = masked_softmax(s.reshape(bsz, SEL_Q_CHUNK, NSA_KV_HEADS, NSA_GROUP, n_keys), mask)
        return jnp.einsum('bqhgm,bqhmd->bqhgd', p.astype(vg.dtype), vg.reshape(bsz, SEL_Q_CHUNK, NSA_KV_HEADS, n_keys, HEAD_DIM))

    o_slc = lax.map(slc_step, jnp.arange(seq // SEL_Q_CHUNK))
    o_slc = jnp.moveaxis(o_slc, 0, 1).reshape(q.shape)

    pad = ((0, 0), (WINDOW, 0), (0, 0), (0, 0))
    kw_p = jnp.pad(kw, pad)
    vw_p = jnp.pad(vw, pad)
    span = WINDOW + Q_BLOCK

    def win_step(i):
        t = i * Q_BLOCK + jnp.arange(Q_BLOCK)
        spos = i * Q_BLOCK - WINDOW + jnp.arange(span)
        qb = lax.dynamic_slice_in_dim(q, i * Q_BLOCK, Q_BLOCK, axis=1)
        kb = lax.dynamic_slice_in_dim(kw_p, i * Q_BLOCK, span, axis=1)
        vb = lax.dynamic_slice_in_dim(vw_p, i * Q_BLOCK, span, axis=1)
        dist = (t[:, None] - spos[None, :]).astype(jnp.float32)
        mask = (dist >= 0) & (dist < WINDOW) & (spos[None, :] >= 0)
        s = jnp.einsum('bqhgd,bkhd->bhgqk', qb, kb).astype(jnp.float32) * ATTN_SCALE - slopes[:, :, None, None] * dist
        p = masked_softmax(s, mask)
        return jnp.einsum('bhgqk,bkhd->bqhgd', p.astype(vb.dtype), vb)

    o_win = lax.map(win_step, jnp.arange(n_qb))
    o_win = jnp.moveaxis(o_win, 0, 1).reshape(q.shape)

    g = jax.nn.sigmoid(gate_logits.astype(jnp.float32)).reshape(bsz, seq, N_BRANCH, NSA_KV_HEADS, NSA_GROUP, 1).astype(q.dtype)
    o = g[:, :, 0] * o_cmp + g[:, :, 1] * o_slc + g[:, :, 2] * o_win
    return o.reshape(bsz, seq, NSA_WIDTH)

def hybrid_layer(x, c, w_ada, b_ada, norm_g, w_in, conv_w, conv_b, w_rg_a, b_rg_a, w_rg_x, b_rg_x, lru_lambda, cmp_pos_k, cmp_w1_k, cmp_w2_k, cmp_pos_v, cmp_w1_v, cmp_w2_v, g_q, g_k_cmp, g_k_slc, g_k_win, g_out_lru, g_out_nsa, w_out):
    bsz, seq, _ = x.shape
    mod = jax.nn.silu(c) @ w_ada + b_ada
    shift, scale, gate = jnp.split(mod, 3, axis=-1)
    h = rms_norm(x, norm_g) * (1.0 + scale[:, None, :]) + shift[:, None, :]
    proj = h @ w_in
    offsets = [int(o) for o in np.cumsum(IN_SPLITS)[:-1]]
    x_lru, z_lru, q, k_cmp, v_cmp, k_slc, v_slc, k_win, v_win, gate_logits, z_nsa = jnp.split(proj, offsets, axis=-1)

    h_lru = rg_lru(causal_depthwise_conv(x_lru, conv_w, conv_b), w_rg_a, b_rg_a, w_rg_x, b_rg_x, lru_lambda)
    y_lru = rms_norm(h_lru, g_out_lru) * jax.nn.silu(z_lru)

    kv_shape = (bsz, seq, NSA_KV_HEADS, HEAD_DIM)
    qh = rms_norm(q.reshape(bsz, seq, NSA_KV_HEADS, NSA_GROUP, HEAD_DIM), g_q)
    kc = rms_norm(compress_blocks(k_cmp.reshape(kv_shape), cmp_pos_k, cmp_w1_k, cmp_w2_k), g_k_cmp)
    vc = compress_blocks(v_cmp.reshape(kv_shape), cmp_pos_v, cmp_w1_v, cmp_w2_v)
    ks = rms_norm(k_slc.reshape(kv_shape), g_k_slc)
    kw = rms_norm(k_win.reshape(kv_shape), g_k_win)
    o_nsa = nsa_branches(qh, kc, vc, ks, v_slc.reshape(kv_shape), kw, v_win.reshape(kv_shape), gate_logits)
    y_nsa = rms_norm(o_nsa, g_out_nsa) * jax.nn.silu(z_nsa)

    out = jnp.concatenate([y_lru, y_nsa], axis=-1) @ w_out
    return x + gate[:, None, :] * out

def setup_inputs(seed: int = 0) -> dict:
    key = jax.random.key(seed)
    ks = jax.random.split(key, 26)
    L = DEPTH

    def nrm(k, shape, s):
        return s * jax.random.normal(k, shape, jnp.float32)

    u = jax.random.uniform(ks[12], (L, LRU_WIDTH), jnp.float32, 0.9, 0.999)
    a0 = u ** (1.0 / LRU_C)
    lam = jnp.log(a0) - jnp.log1p(-a0)
    return {
        'x': nrm(ks[0], (BATCH, SEQ, D_MODEL), 1.0),
        'c': nrm(ks[1], (BATCH, D_MODEL), 1.0),
        'w_ada': nrm(ks[2], (L, D_MODEL, 3 * D_MODEL), 0.5 * D_MODEL ** -0.5),
        'b_ada': nrm(ks[3], (L, 3 * D_MODEL), 0.02),
        'norm_g': 1.0 + nrm(ks[4], (L, D_MODEL), 0.02),
        'w_in': nrm(ks[5], (L, D_MODEL, IN_WIDTH), D_MODEL ** -0.5),
        'conv_w': nrm(ks[6], (L, CONV_WIDTH, LRU_WIDTH), CONV_WIDTH ** -0.5),
        'conv_b': nrm(ks[7], (L, LRU_WIDTH), 0.02),
        'w_rg_a': nrm(ks[8], (L, LRU_BLOCKS, LRU_BLOCK, LRU_BLOCK), LRU_BLOCK ** -0.5),
        'b_rg_a': nrm(ks[9], (L, LRU_WIDTH), 0.02),
        'w_rg_x': nrm(ks[10], (L, LRU_BLOCKS, LRU_BLOCK, LRU_BLOCK), LRU_BLOCK ** -0.5),
        'b_rg_x': nrm(ks[11], (L, LRU_WIDTH), 0.02),
        'lru_lambda': lam,
        'cmp_pos_k': nrm(ks[13], (L, CMP_BLOCK, HEAD_DIM), 0.1),
        'cmp_w1_k': nrm(ks[14], (L, CMP_BLOCK * HEAD_DIM, CMP_HIDDEN), (CMP_BLOCK * HEAD_DIM) ** -0.5),
        'cmp_w2_k': nrm(ks[15], (L, CMP_HIDDEN, HEAD_DIM), CMP_HIDDEN ** -0.5),
        'cmp_pos_v': nrm(ks[16], (L, CMP_BLOCK, HEAD_DIM), 0.1),
        'cmp_w1_v': nrm(ks[17], (L, CMP_BLOCK * HEAD_DIM, CMP_HIDDEN), (CMP_BLOCK * HEAD_DIM) ** -0.5),
        'cmp_w2_v': nrm(ks[18], (L, CMP_HIDDEN, HEAD_DIM), CMP_HIDDEN ** -0.5),
        'g_q': 1.0 + nrm(ks[19], (L, HEAD_DIM), 0.02),
        'g_k_cmp': 1.0 + nrm(ks[20], (L, HEAD_DIM), 0.02),
        'g_k_slc': 1.0 + nrm(ks[21], (L, HEAD_DIM), 0.02),
        'g_k_win': 1.0 + nrm(ks[22], (L, HEAD_DIM), 0.02),
        'g_out_lru': 1.0 + nrm(ks[23], (L, LRU_WIDTH), 0.02),
        'g_out_nsa': 1.0 + nrm(ks[24], (L, NSA_WIDTH), 0.02),
        'w_out': nrm(ks[25], (L, MIX_WIDTH, D_MODEL), MIX_WIDTH ** -0.5),
    }

def reference(x, c, w_ada, b_ada, norm_g, w_in, conv_w, conv_b, w_rg_a, b_rg_a, w_rg_x, b_rg_x, lru_lambda, cmp_pos_k, cmp_w1_k, cmp_w2_k, cmp_pos_v, cmp_w1_v, cmp_w2_v, g_q, g_k_cmp, g_k_slc, g_k_win, g_out_lru, g_out_nsa, w_out):
    for layer in range(DEPTH):
        x = hybrid_layer(x, c, w_ada[layer], b_ada[layer], norm_g[layer], w_in[layer], conv_w[layer], conv_b[layer], w_rg_a[layer], b_rg_a[layer], w_rg_x[layer], b_rg_x[layer], lru_lambda[layer], cmp_pos_k[layer], cmp_w1_k[layer], cmp_w2_k[layer], cmp_pos_v[layer], cmp_w1_v[layer], cmp_w2_v[layer], g_q[layer], g_k_cmp[layer], g_k_slc[layer], g_k_win[layer], g_out_lru[layer], g_out_nsa[layer], w_out[layer])
    return x


_drawn_inputs = setup_inputs


def setup_inputs(seed=0):
    import zlib

    import numpy as np

    out = dict(_drawn_inputs(seed))
    spreads = {}
    factors = {'b_ada': 3.284,
     'norm_g': 8.0,
     'conv_b': 6.417,
     'b_rg_a': 46.828,
     'b_rg_x': 37.747,
     'cmp_pos_k': 8.0,
     'cmp_pos_v': 5.839,
     'g_q': 8.0,
     'g_k_cmp': 8.0,
     'g_k_slc': 8.0,
     'g_k_win': 8.0,
     'g_out_lru': 33.279,
     'g_out_nsa': 33.062}
    for name, (base, spread) in spreads.items():
        noise = np.random.default_rng([zlib.crc32(name.encode()), seed]).standard_normal(out[name].shape)
        drawn = base * np.exp(spread * noise) if base else spread * noise
        out[name] = jnp.asarray(drawn.astype(out[name].dtype))
    for name, factor in factors.items():
        out[name] = (out[name] * factor).astype(out[name].dtype)
    return out
```

```python
import concourse.bass as bass
from concourse import mybir

ALU = mybir.AluOpType
ACT = mybir.ActivationFunctionType
AX = mybir.AxisListType
F32 = mybir.dt.float32
F32R = mybir.dt.float32r
I32 = mybir.dt.int32

P = 128
S = 512
D = 1024
T = S // P
KC = D // P
LRU = 512
CT = LRU // P
H = 8
KV = 2
G = H // KV
HD = 64
TAPS = 4
LRU_C = 8.0
CW = 32
NCMP = 31
MASKED = -1e30
EPS = 1e-6
SCALE = HD ** -0.5
SLOPES = [2.0 ** (-8.0 * (h + 1) / H) for h in range(H)]
UNITS = T * 2 * H
GELU_A, GELU_B = 0.7978845608028654, 0.044715
MAGIC = float(0x5F3759DF)

C_XLRU, C_ZLRU, C_Q, C_KCMP, C_KSLC, C_VSLC, C_KWIN, C_VWIN, C_GATE, C_ZNSA = 0, 512, 1024, 1536, 1792, 1920, 2048, 2176, 2304, 2328
NG = 24

R_CW, R_CB, R_BA, R_BX, R_LAM, R_GL, R_GN, ROWS = 0, 4, 5, 6, 7, 8, 9, 10
Q_GQ, Q_GS, Q_GW, Q_GC, Q_POSK, Q_POSV, QROWS = 0, 1, 2, 3, 4, 20, 36

PIECES = ([("in", C_XLRU, 512, k) for k in (0, 4)] + [("in", C_KCMP, 256, 0)]
          + [("in", c, 512, k) for c in (C_KSLC, C_Q, C_ZLRU, C_ZNSA) for k in (0, 4)]
          + [("out", 512 * half, 512, ct) for ct in (0, 4) for half in (0, 1)])
NP = len(PIECES)
PX, PC, PKV, PQ, PZL, PZN, PO = 0, 2, 3, 5, 7, 9, 11
RAW, HL = 3, 2
ITEMS = [("ada", k) for k in range(KC)] + [("w", p) for p in range(5)] + [("gate", 0), ("w", 5), ("gate", 1),
         ("w", 6), ("gate", 2), ("w", 7), ("gate", 3)] + [("w", p) for p in range(8, NP)]
ITEM_OF = {it: n for n, it in enumerate(ITEMS)}


def build(nc, x, c, w_ada, b_ada, norm_g, w_in, conv_w, conv_b, w_rg_a, b_rg_a, w_rg_x, b_rg_x, lru_lambda,
          cmp_pos_k, cmp_w1_k, cmp_w2_k, cmp_pos_v, cmp_w1_v, cmp_w2_v, g_q, g_k_cmp, g_k_slc, g_k_win,
          g_out_lru, g_out_nsa, w_out, out):
    x, out = x[0], out[0]
    w_ada, w_in, w_out = w_ada[0], w_in[0], w_out[0]
    w1_dram = (cmp_w1_k[0], cmp_w1_v[0])
    w2_dram = (cmp_w2_k[0], cmp_w2_v[0])

    top = [(nc.sbuf_base + 63) // 64 * 64]

    def region(size):
        at = top[0]
        top[0] = at + (size + 31) // 32 * 32
        return at

    def sb(name, shape, at, dt=F32):
        return nc.alloc_sbuf_tensor_at(name, shape, dt, offset=at)

    r_raw, r_hl, r_ht = region(RAW * 8192), region(HL * 16384), region(32768)
    r_x1, r_x2, r_w1 = region(8256 + 8192), region(16384), region(16384)
    r_kt, r_v, r_qn, r_qs = region(16384), region(8192), region(8192), region(8192)
    r_sb, r_pt, r_xo, r_bc = region(4096), region(8192), region(4096), region(4096)
    r_cs, r_vb, r_gb = region(2048), region(2048), region(4096)

    raw = [sb(f"raw{n}", [P, 2048], r_raw + 8192 * n) for n in range(RAW)]
    w_hi = [sb(f"w_hi{n}", [P, 2048], r_hl + 16384 * n, F32R) for n in range(HL)]
    w_lo = [sb(f"w_lo{n}", [P, 2048], r_hl + 16384 * n + 8192, F32R) for n in range(HL)]
    h_hi = sb("h_hi", [P, KC, S], r_ht, F32R)
    h_lo = sb("h_lo", [P, KC, S], r_ht + 16384, F32R)
    x_res = sb("x_res", [P, T, D], r_ht)
    yn_hi = sb("yn_hi", [P, CT, S], r_ht + 16384, F32R)
    yn_lo = sb("yn_lo", [P, CT, S], r_ht + 24576, F32R)
    xn = sb("xn", [P, T, D], r_x1)
    lru_x = sb("lru_x", [P, CT, S + 3], r_x1)
    lru_h = sb("lru_h", [P, CT, S], r_x1 + 8256)
    z_silu = sb("z_silu", [P, T, S], r_x1)
    xT = sb("xT", [P, KC, S], r_x2)
    lru_c = sb("lru_c", [P, CT, S], r_x2)
    lru_d = sb("lru_d", [P, CT, S], r_x2 + 8192)
    yl_hi = sb("yl_hi", [P, CT, S], r_x2, F32R)
    yl_lo = sb("yl_lo", [P, CT, S], r_x2 + 8192, F32R)
    w1 = sb("w1", [P, 16, 256], r_w1)
    bias = sb("bias", [P, H, S], r_w1)
    out_sb = sb("out_sb", [P, 2 * T, 512], r_w1)
    k_st = sb("k_st", [P, 2, KV, 2, S], r_kt, F32R)
    junk = sb("junk", [P, D], r_kt)
    v_hl = sb("v_hl", [P, 2, KV, T, P], r_v, F32R)
    qn = sb("qn", [P, T, S], r_qn)
    kn = sb("kn", [P, T, 256], r_pt + 4096)
    q_st = [sb(f"q_st{n}", [P, H, P], r_qs + 4096 * n, F32R) for n in range(2)]
    bd = sb("bd", [P, 2, CT, P], r_qs)
    w24 = sb("w24", [P, KC, NG], r_qs + 4096)
    w24_hi = sb("w24_hi", [P, KC, NG], r_qs + 4864, F32R)
    w24_lo = sb("w24_lo", [P, KC, NG], r_qs + 5632, F32R)
    sc_sb = [sb(f"sc_sb{n}", [P, S], r_sb + 2048 * n) for n in range(2)]
    gacc = sb("gacc", [P, D], r_sb)
    pt_hi = [sb(f"pt_hi{n}", [P, S], r_pt + 4096 * n, F32R) for n in range(2)]
    pt_lo = [sb(f"pt_lo{n}", [P, S], r_pt + 4096 * n + 2048, F32R) for n in range(2)]
    rows_a = sb("rows_a", [ROWS, LRU], r_gb)
    rows_b = sb("rows_b", [QROWS, P], r_gb + 2048)
    cmp_x = [sb(f"cmp_x{w}", [P, 2, 8, KV, CW], r_pt if w == 0 else r_bc) for w in range(2)]
    bias_c = sb("bias_c", [P, T, H, CW], r_bc)
    xo = [sb(f"xo{n}", [P, G, P], r_xo + 2048 * n) for n in range(2)]
    sq = [sb(f"sq{n}", [P, S], r_xo + 2048 * n) for n in range(2)]
    c_s = sb("c_s", [P, H, CW], r_cs)
    c_pt = sb("c_pt", [P, KV, P], r_cs + 1024)
    gl_q = sb("gl_q", [P, 2, 2 * CW], r_cs)
    gl_g = sb("gl_g", [P, 2, 2 * CW], r_cs + 512)
    gl_t = sb("gl_t", [P, 2 * CW], r_cs + 1024)
    gl_r = sb("gl_r", [P, 2 * CW], r_cs + 1280)
    v_blk = sb("v_blk", [P, KV, G * HD], r_vb)
    g_bc = sb("g_bc", [P, D], r_gb)
    y_b = sb("y_b", [P, S], r_xo)

    def small(name, shape, dt=F32):
        n = 1
        for d in shape[1:]:
            n *= d
        return sb(name, shape, region(4 * n), dt)

    early = [r_v]

    def start_small(name, shape):
        at, n = early[0], 1
        for d in shape[1:]:
            n *= d
        early[0] = at + (4 * n + 31) // 32 * 32
        return sb(name, shape, at)

    ident, ones = small("ident", [P, P]), small("ones", [P, P])
    w2k, w2v = sb("w2k", [P, 2, P], r_kt + 4096), sb("w2v", [P, 2, HD], r_cs + 1536)
    bg_row = sb("bg_row", [1, D], r_pt)
    diag = sb("diag", [P, T, P], r_cs)
    kc_st = small("kc_st", [P, 2, KV, CW], F32R)
    cols_a, cols_b = small("cols_a", [P, CT, ROWS]), small("cols_b", [P, QROWS])
    den, negmax = small("den", [P, UNITS]), small("negmax", [P, UNITS])
    gates = small("gates", [P, T, NG])
    c_col, c_t, c_silu = start_small("c_col", [P, KC]), start_small("c_t", [P, KC]), small("c_silu", [P, KC])
    b_mod, ng_col, mod, s1 = [start_small(n, sh) for n, sh in (("b_mod", [P, 2, KC]), ("ng_col", [P, KC]), ("mod", [P, 2, KC]), ("s1", [P, KC]))]
    ss_x, rs_x = start_small("ss_x", [P, T]), start_small("rs_x", [P, T])
    gk = small("gk", [P, 3])
    hb, sp, n4sp, p4sp, gl_half = small("hb", [P, 2, CT]), small("sp", [P, CT]), small("n4sp", [P, CT]), small("p4sp", [P, CT]), small("gl_half", [P, CT])
    lam_abs, lam_e, lam_s, lam_2 = [start_small(n, [P, CT]) for n in ("lam_abs", "lam_e", "lam_s", "lam_2")]
    gn_half = small("gn_half", [P, CT])
    ss_q, rs_q = sb("ss_q", [P, T, H], r_vb), sb("rs_q", [P, T, H], r_vb + 128)
    ss_k, rs_k = sb("ss_k", [P, T, 4], r_vb + 256), sb("rs_k", [P, T, 4], r_vb + 320)
    nt1 = small("nt1", [P, 64])
    c_max, c_den, c_f = small("c_max", [P, H]), small("c_den", [P, H]), small("c_f", [P, H])
    f_u = small("f_u", [P, 2, G])
    valid = small("valid", [P, 1])
    ss_l, rs_l, ss_n, rs_n = [small(n, [P, T]) for n in ("ss_l", "rs_l", "ss_n", "rs_n")]

    ps = nc.alloc_psum_tensor("ps", [P, 8, 512], F32)

    names = {}

    def sem(name):
        names[name] = nc.alloc_semaphore(name)
        return names[name]

    rows_in, c_in, small_in, w24_in, bd_in, w2_in, bg_in, w1_in, xres_in, stored = [sem(n) for n in (
        "rows_in", "c_in", "small_in", "w24_in", "bd_in", "w2_in", "bg_in", "w1_in", "xres_in", "stored")]
    x_in = [sem(f"x_in{t}") for t in range(T)]
    raw_in = [sem(f"raw_in{n}") for n in range(RAW)]
    (pool_setup, dve_setup, c_tanh, c_ready, cols_done, cols_ready, ssx_ready, xn_ready, xt_psum, xt_ready,
     ada_mm, mod_ready, h_full, h_hi_ready, h_ready, hi_done, lo_done, piece_done, gate_used) = [sem(n) for n in (
        "pool_setup", "dve_setup", "c_tanh", "c_ready", "cols_done", "cols_ready", "ssx_ready", "xn_ready", "xt_psum",
        "xt_ready", "ada_mm", "mod_ready", "h_full", "h_hi_ready", "h_ready", "hi_done", "lo_done", "piece_done",
        "gate_used")]
    (w24_hi_ready, w24_ready, g24_done, g24_tanh, gates_ready, lam_exp, lam_ready, lru_x_ready, xc_ready, rg_mm,
     rg_tanh, ix_ready, a_ready, one_less_a2, sqrt_ready, lru_h_ready, lru_sq, lru_ss, diag_ready, rbc_mm, rbc_ready,
     hr_ready, zl_tanh, yl_full, yl_hi_ready, yl_ready) = [sem(n) for n in (
        "w24_hi_ready", "w24_ready", "g24_done", "g24_tanh", "gates_ready", "lam_exp", "lam_ready", "lru_x_ready",
        "xc_ready", "rg_mm", "rg_tanh", "ix_ready", "a_ready", "one_less_a2", "sqrt_ready", "lru_h_ready", "lru_sq",
        "lru_ss", "diag_ready", "rbc_mm", "rbc_ready", "hr_ready", "zl_tanh", "yl_full", "yl_hi_ready", "yl_ready")]
    (cx_ready, hid_mm, gl_sq, gl_poly, gl_tanh, gl_ready, cw2_mm, kc_sq, kc_ss, kc_full, kc_hi, kc_ready, vc_ready,
     kv_sq, kn_ready, v_hi, v_ready, kt_mm, k_hi, k_ready, q_sq, qn_ready, gate_mm, gate_bc) = [sem(n) for n in (
        "cx_ready", "hid_mm", "gl_sq", "gl_poly", "gl_tanh", "gl_ready", "cw2_mm", "kc_sq", "kc_ss", "kc_full", "kc_hi",
        "kc_ready", "vc_ready", "kv_sq", "kn_ready", "v_hi", "v_ready", "kt_mm", "k_hi", "k_ready", "q_sq",
        "qn_ready", "gate_mm", "gate_bc")]
    (bias_d, bias_s, bias_ready, qt_mm, q_hi, q_st_ready, cs_mm, cs_sub, cs_biased, cp_ready, ct_mm, cpt_ready, cpv_mm, o_init,
     scores_done, biased, probs, pt_done, pt_hi_done, pt_lo_done, pv_done, o_scaled, o_added,
     zn_tanh, zn_ready, n_sq, y_ready, yt_mm, yn_hi_done, yn_ready, out_mm, out_gated, out_added,
     pchain, dchain, achain) = [sem(n) for n in (
        "bias_d", "bias_s", "bias_ready", "qt_mm", "q_hi", "q_st_ready", "cs_mm", "cs_sub", "cs_biased", "cp_ready", "ct_mm",
        "cpt_ready", "cpv_mm", "o_init", "scores_done", "biased", "probs", "pt_done", "pt_hi_done", "pt_lo_done",
        "pv_done", "o_scaled", "o_added", "zn_tanh", "zn_ready", "n_sq", "y_ready", "yt_mm", "yn_hi_done",
        "yn_ready", "out_mm", "out_gated", "out_added", "pchain", "dchain", "achain")]

    def bank(b):
        return ps[:, b, :]

    def item_wait(eng, it):
        n = ITEM_OF[it]
        eng.wait_ge(raw_in[n % RAW], 16 * (n // RAW + 1))

    def raw_of(it):
        return raw[ITEM_OF[it] % RAW]

    def piece_cols(p):
        return PIECES[p][2]

    def wv(t, p):
        return t[:].rearrange("p (k n) -> p k n", n=piece_cols(p))

    def sync_program(sp):
        for t in range(T):
            sp.dma_start(xn[:, t, :], x[t * P:(t + 1) * P, :]).then_inc(x_in[t], 16)
        for n, (kind, p) in enumerate(ITEMS):
            if n >= RAW:
                k0, p0 = ITEMS[n - RAW]
                sp.wait_ge({"ada": ada_mm, "gate": gate_used, "w": lo_done}[k0], p0 + 1)
            slot = raw[n % RAW]
            if kind == "ada":
                src, dst = w_ada.rearrange("(p k) n -> p k n", k=KC)[:, p, 0:2048], slot[:]
            elif kind == "gate":
                src = w_ada.rearrange("(p k) n -> p k n", k=KC)[:, 2 * p:2 * p + 2, 2048:3072]
                dst = slot[:].rearrange("p (k n) -> p k n", k=2)
            else:
                side, c0, n_cols, k0 = PIECES[p]
                if side == "in":
                    src = w_in.rearrange("(p k) n -> p k n", k=KC)[:, k0:k0 + 2048 // n_cols, c0:c0 + n_cols]
                else:
                    src = w_out.rearrange("(k p) n -> p k n", p=P)[:, k0:k0 + 4, c0:c0 + n_cols]
                dst = wv(slot, p)
            sp.dma_start(dst, src).then_inc(raw_in[n % RAW], 16)
            if (kind, p) == ("w", 3):
                sp.dma_start(w1[:], w1_dram[0].rearrange("(k p) n -> p k n", p=P)).then_inc(w1_in, 16)
            if (kind, p) == ("w", 6):
                sp.wait_ge(hid_mm, 1)
                sp.dma_start(bg_row[:], b_ada[0:1, 2048:3072]).then_inc(bg_in, 16)
                sp.dma_start(w1[:], w1_dram[1].rearrange("(k p) n -> p k n", p=P)).then_inc(w1_in, 16)
        sp.wait_ge(piece_done, PZN + 2)
        sp.dma_start(x_res[:], x.rearrange("(t p) n -> p t n", p=P)).then_inc(xres_in, 16)
        for n in range(2 * T):
            half, t = n // T, n % T
            sp.wait_ge(out_added, n + 1)
            sp.dma_start(out[t * P:(t + 1) * P, half * 512:half * 512 + 512], out_sb[:, n, :]).then_inc(stored, 16)
        sp.wait_ge(stored, 16 * 2 * T)

    def pool_program(g):
        gp = nc.gpsimd
        gp.memset(ident[:], 0.0).then_inc(pchain, 1)
        g.wait_ge(pchain, 1)
        gp.affine_select(out=ident[:], in_=ident[:], compare_op=ALU.not_equal, fill=1.0, base=0,
                         pattern=[[-1, P]], channel_multiplier=1).then_inc(pool_setup, 1)
        gp.memset(bd[:], 0.0).then_inc(pool_setup, 1)
        gp.memset(valid[:], 1.0).then_inc(pchain, 1)
        g.wait_ge(pchain, 2)
        gp.affine_select(out=valid[:], in_=valid[:], compare_op=ALU.is_ge, fill=0.0, base=-31,
                         pattern=[[0, 1]], channel_multiplier=1).then_inc(pool_setup, 1)

        def lo(p):
            g.wait_ge(hi_done, p + 1)
            item_wait(g, ("w", p))
            gp.tensor_tensor(w_lo[p % HL][:], raw_of(("w", p))[:], w_hi[p % HL][:].bitcast(F32),
                             ALU.subtract).then_inc(lo_done, 1)

        g.wait_ge(w24_hi_ready, 1)
        gp.tensor_tensor(w24_lo[:], w24[:], w24_hi[:].bitcast(F32), ALU.subtract).then_inc(w24_ready, 1)
        for p in range(PQ + 2):
            lo(p)
        g.wait_ge(hid_mm, 2)
        gp.iota(bias[:, 0, :], pattern=[[1, S]], base=-(S - P), channel_multiplier=-1,
                allow_small_or_imprecise_dtypes=True).then_inc(bias_d, 1)
        gp.iota(bias_c[:, :, 0, :], pattern=[[-P, T], [16, CW]], base=31, channel_multiplier=-1,
                allow_small_or_imprecise_dtypes=True).then_inc(bias_d, 1)
        g.wait_ge(bias_s, 2)
        gp.affine_select(out=bias[:, :, S - P:S], in_=bias[:, :, S - P:S], compare_op=ALU.is_ge, fill=MASKED, base=0,
                         pattern=[[0, H], [-1, P]], channel_multiplier=1).then_inc(bias_ready, 1)
        gp.affine_select(out=bias_c[:], in_=bias_c[:], compare_op=ALU.is_ge, fill=MASKED, base=-31,
                         pattern=[[P, T], [0, H], [-16, CW]], channel_multiplier=1).then_inc(bias_ready, 1)

        def o_add(grp):
            i, b, kv = grp // 4, grp % 4 // 2, grp % 2
            g.wait_ge(o_scaled, grp + 1)
            o = qn[:, i, kv * 256:kv * 256 + 256].rearrange("p (g d) -> p g d", g=G)
            if grp % 4 == 0:
                g.wait_ge(o_init, i + 1)
            n = pool_n[0]
            gp.tensor_tensor(o, o, xo[grp % 2][:, :, 0:HD], ALU.add).then_inc(pchain, 1)
            pool_n[0] += 1
            g.wait_ge(pchain, pool_n[0])
            gp.tensor_tensor(o, o, xo[grp % 2][:, :, HD:P], ALU.add).then_inc(o_added, 1)
            g.wait_ge(o_added, grp + 1)

        pool_n = [2]
        lo(7)
        lo(8)
        for grp in range(4 * T):
            if grp in (4, 8, 14):
                lo({4: 9, 8: 10, 14: 11}[grp])
            o_add(grp)
        for p in range(12, NP):
            lo(p)

    def act_program(act):
        sc = nc.scalar
        act.dma_start(c_col[:], c[0].rearrange("(p k) -> p k", k=KC)).then_inc(c_in, 16)
        act.dma_start(rows_a[R_CW:R_CW + TAPS, :], conv_w[0]).then_inc(rows_in, 16)
        for r, v in ((R_CB, conv_b), (R_BA, b_rg_a), (R_BX, b_rg_x), (R_LAM, lru_lambda), (R_GL, g_out_lru), (R_GN, g_out_nsa)):
            act.dma_start(rows_a[r:r + 1, :], v).then_inc(rows_in, 16)
        for r, v in ((Q_GQ, g_q), (Q_GS, g_k_slc), (Q_GW, g_k_win), (Q_GC, g_k_cmp)):
            act.dma_start(rows_b[r:r + 1, 0:HD], v).then_inc(rows_in, 16)
            act.dma_start(rows_b[r:r + 1, HD:P], v).then_inc(rows_in, 16)
        for r, v in ((Q_POSK, cmp_pos_k), (Q_POSV, cmp_pos_v)):
            act.dma_start(rows_b[r:r + 16, :], v[0].rearrange("(j e) d -> j (e d)", e=2)).then_inc(rows_in, 16)
        act.dma_start(b_mod[:], b_ada[0, 0:2048].rearrange("(s p k) -> p s k", s=2, k=KC)).then_inc(small_in, 16)
        act.dma_start(ng_col[:], norm_g[0].rearrange("(p k) -> p k", k=KC)).then_inc(small_in, 16)
        act.dma_start(w24[:], w_in.rearrange("(p k) n -> p k n", k=KC)[:, :, C_GATE:C_GATE + NG]).then_inc(w24_in, 16)
        for rep in range(2):
            act.dma_start(w2k[:, :, rep * HD:rep * HD + HD], w2_dram[0].rearrange("(k p) n -> p k n", p=P)).then_inc(w2_in, 16)
        act.dma_start(w2v[:], w2_dram[1].rearrange("(k p) n -> p k n", p=P)).then_inc(w2_in, 16)
        act.wait_ge(pool_setup, 2)
        for m, w in enumerate((w_rg_a, w_rg_x)):
            for e in range(2):
                act.dma_start(bd[e * HD:e * HD + HD, m, :, e * HD:e * HD + HD],
                              w[0].rearrange("(t e) i j -> e i t j", e=2)[e]).then_inc(bd_in, 16)
        act.wait_ge(c_in, 16)
        sc.activation(c_t[:], c_col[:], ACT.Tanh, scale=0.5).then_inc(c_tanh, 1)
        for t in range(T):
            act.wait_ge(x_in[t], 16)
            if t >= 1:
                act.wait_ge(ssx_ready, t)
            sc.activation(junk[:], xn[:, t, :], ACT.Square, accum_out=ss_x[:, t:t + 1]).then_inc(ssx_ready, 1)
        act.wait_ge(lam_ready, 1)
        sc.activation(lam_e[:], lam_abs[:], ACT.Exp, scale=-1.0).then_inc(lam_exp, 1)
        act.wait_ge(w24_in, 16)
        sc.activation(w24_hi[:], w24[:], ACT.Copy).then_inc(w24_hi_ready, 1)
        for n in range(2 * T):
            t, j = n // 2, n % 2
            act.wait_ge(xt_psum, n + 1)
            sc.activation(xT[:, 4 * j:4 * j + 4, t * P:(t + 1) * P],
                          bank(n % 4).rearrange("p (k n) -> p k n", k=4), ACT.Copy).then_inc(xt_ready, 1)

        def hi(p):
            item_wait(act, ("w", p))
            if p >= HL:
                act.wait_ge(piece_done, p - HL + 1)
            sc.activation(w_hi[p % HL][:], raw_of(("w", p))[:], ACT.Copy).then_inc(hi_done, 1)

        for k in range(KC):
            act.wait_ge(h_full, k + 1)
            sc.activation(h_hi[:, k, :], xT[:, k, :], ACT.Copy).then_inc(h_hi_ready, 1)
            if k == 2:
                hi(0)
        hi(1)
        act.wait_ge(g24_done, 1)
        sc.activation(gates[:], bank(7)[:, 0:T * NG].rearrange("p (t n) -> p t n", t=T), ACT.Tanh,
                      scale=0.5).then_inc(g24_tanh, 1)
        hi(2)
        act.wait_ge(piece_done, PX + 2)
        for ct in range(CT):
            sc.activation(lru_x[:, ct, 3:S + 3], bank(ct), ACT.Copy).then_inc(lru_x_ready, 1)
        hi(3)

        def gelu_act(w):
            hid = bank(6 + w)[:, 0:4 * CW].rearrange("p (m n) -> p m n", m=2)
            act.wait_ge(hid_mm, w + 1)
            sc.activation(gl_q[:, :, 0:2 * NCMP], hid[:, :, 0:2 * NCMP], ACT.Square).then_inc(gl_sq, 1)
            act.wait_ge(gl_poly, w + 1)
            sc.activation(gl_q[:, :, 0:2 * NCMP], gl_q[:, :, 0:2 * NCMP], ACT.Tanh, scale=GELU_A).then_inc(gl_tanh, 1)

        gelu_act(0)
        hi(4)
        act.wait_ge(cw2_mm, 1)
        sc.activation(gl_t[:, 0:2 * NCMP], bank(6)[:, 0:2 * NCMP], ACT.Square, scale=0.5).then_inc(kc_sq, 1)
        act.wait_ge(piece_done, PKV + 1)
        act.wait_ge(piece_done, PKV + 2)
        for t in range(T):
            row = bank(t).rearrange("p (b s n) -> p b s n", b=2, s=2)
            if t >= 2:
                act.wait_ge(kn_ready, t - 1)
            sc.activation(sq[t % 2][:, 0:256].rearrange("p (b n) -> p b n", b=2), row[:, :, 0, :], ACT.Square).then_inc(kv_sq, 1)
            for b in range(2):
                sc.activation(v_hl[:, b, :, t, 0:HD], row[:, b, 1, :].rearrange("p (k d) -> p k d", k=KV), ACT.Copy).then_inc(v_hi, 1)
        act.wait_ge(kc_full, 1)
        sc.activation(kc_st[:, 0, :, 0:NCMP], gl_t[:, 0:2 * NCMP].rearrange("p (k n) -> p k n", k=KV), ACT.Copy).then_inc(kc_hi, 1)
        hi(5)
        for ct in range(CT):
            for m in range(2):
                act.wait_ge(rg_mm, 2 * ct + m + 1)
                dst = (lru_c, lru_d)[m]
                sc.activation(dst[:, ct, :], bank(6 + m), ACT.Tanh, scale=0.5, bias=hb[:, m, ct:ct + 1]).then_inc(rg_tanh, 1)
        for b in range(2):
            act.wait_ge(kt_mm, b + 1)
            for kv in range(KV):
                src = ps[kv * HD:kv * HD + HD, 4 + b, :]
                for half in (kv, 1 - kv):
                    sc.activation(k_st[half * HD:half * HD + HD, b, kv, 0, :], src, ACT.Identity,
                                  scale=gk[kv * HD:kv * HD + HD, b:b + 1]).then_inc(k_hi, 1)
        hi(6)
        for ct in range(CT):
            act.wait_ge(ix_ready, 1)
            act.wait_ge(rg_tanh, 2 * CT)
            sc.activation(lru_d[:, ct, :], lru_c[:, ct, :], ACT.Exp, scale=n4sp[:, ct:ct + 1], bias=n4sp[:, ct:ct + 1]).then_inc(a_ready, 1)
            sc.activation(lru_x[:, ct, 0:S], lru_c[:, ct, :], ACT.Tanh, scale=p4sp[:, ct:ct + 1], bias=p4sp[:, ct:ct + 1]).then_inc(a_ready, 1)
            act.wait_ge(a_ready, 3 * ct + 2)
            sc.activation(lru_c[:, ct, :], lru_d[:, ct, :], ACT.Square).then_inc(a_ready, 1)
        act.wait_ge(piece_done, PQ + 2)
        for t in range(T):
            if t >= 2:
                act.wait_ge(qn_ready, t - 1)
            sc.activation(sq[t % 2][:], bank(t), ACT.Square).then_inc(q_sq, 1)
        gelu_act(1)
        act.wait_ge(one_less_a2, 1)
        sc.activation(lru_c[:], lru_c[:], ACT.Sqrt, scale=0.25).then_inc(sqrt_ready, 1)
        act.wait_ge(bias_d, 2)
        for h in range(H - 1, -1, -1):
            a = sc.activation(bias[:, h, :], bias[:, 0, :], ACT.Copy, scale=SLOPES[h])
            b = sc.activation(bias_c[:, :, h, :], bias_c[:, :, 0, :], ACT.Copy, scale=SLOPES[h])
        a.then_inc(bias_s, 1)
        b.then_inc(bias_s, 1)
        act.wait_ge(lru_h_ready, CT)
        sc.activation(lru_c[:], lru_h[:], ACT.Square).then_inc(lru_sq, 1)
        act.wait_ge(gate_mm, 2)
        for half in range(2):
            sc.activation(g_bc[:, half * 512:half * 512 + 512], bank(4 + half), ACT.Copy).then_inc(gate_bc, 1)
        act.wait_ge(rbc_mm, 1)
        sc.activation(lru_x[:, 0, 0:S], bank(6), ACT.Copy).then_inc(rbc_ready, 1)

        def q_hi_part(i):
            act.wait_ge(qt_mm, i + 1)
            if i >= 2:
                act.wait_ge(scores_done, 2 * H * (i - 1))
                act.wait_ge(cs_mm, i - 1)
            src = bank(6).rearrange("p (a n) -> p a n", a=H // 2)
            for e in range(2):
                sc.activation(q_st[i % 2][e * HD:e * HD + HD, e:H:2, :], src[e * HD:e * HD + HD], ACT.Copy).then_inc(q_hi, 1)

        def cmp_exp(i):
            act.wait_ge(cs_sub, i + 1)
            sc.activation(c_s[:], c_s[:], ACT.Exp).then_inc(cp_ready, 1)

        def cmp_pt(i):
            act.wait_ge(ct_mm, i + 1)
            sc.activation(c_pt[:], bank(6)[:, 0:256].rearrange("p (k n) -> p k n", k=KV), ACT.Copy).then_inc(cpt_ready, 1)

        def prob(u):
            act.wait_ge(biased, u + 1)
            n = (u // (2 * H) + 1) * P
            sc.activation(sc_sb[u % 2][:, 0:n], sc_sb[u % 2][:, 0:n], ACT.Exp, scale=-1.0, bias=negmax[:, u:u + 1],
                          accum_out=den[:, u:u + 1]).then_inc(probs, 1)

        def pt_hi_part(u):
            act.wait_ge(pt_done, u + 1)
            if u >= 2:
                act.wait_ge(pv_done, u - 1)
            n = (u // (2 * H) + 1) * P
            sc.activation(pt_hi[u % 2][:, 0:n], bank(5)[:, 0:n], ACT.Copy).then_inc(pt_hi_done, 1)

        hi(7)
        q_hi_part(0)
        hi(8)
        cmp_exp(0)
        cmp_pt(0)
        def z_lru(ct):
            act.wait_ge(piece_done, PZL + 2)
            act.wait_ge(hr_ready, 1)
            if ct >= 2:
                act.wait_ge(yl_full, ct - 1)
            sc.activation(lru_x[:, 1 + ct % 2, 0:S], bank(ct), ACT.Tanh, scale=0.5).then_inc(zl_tanh, 1)

        def yl_hi_part(ct):
            act.wait_ge(yl_full, ct + 1)
            sc.activation(yl_hi[:, ct, :], lru_h[:, ct, :], ACT.Copy).then_inc(yl_hi_ready, 1)

        def z_nsa(t):
            act.wait_ge(piece_done, PZN + 2)
            act.wait_ge(yl_ready, CT)
            sc.activation(z_silu[:, t, :], bank(t), ACT.Tanh, scale=0.5).then_inc(zn_tanh, 1)

        hi_at = {16: 9, 32: 10, 56: 11}
        for u in range(UNITS + 1):
            i, r = u // (2 * H), u % (2 * H)
            if u in hi_at:
                hi(hi_at[u])
            if u < UNITS:
                prob(u)
            if u >= 1:
                pt_hi_part(u - 1)
            if i + 1 < T and u < UNITS:
                if r == 6:
                    q_hi_part(i + 1)
                if r == 9:
                    cmp_exp(i + 1)
                if r == 12:
                    cmp_pt(i + 1)
            if ZL_AT <= u < ZL_AT + CT:
                z_lru(u - ZL_AT)
            if ZL_AT + 1 <= u < ZL_AT + 1 + CT:
                yl_hi_part(u - ZL_AT - 1)
        for t in range(T):
            z_nsa(t)
        hi(12)
        for t in range(T):
            act.wait_ge(o_added, 4 * (t + 1))
            if t >= 1:
                act.wait_ge(n_sq, t)
            sc.activation(pt_sq[:], qn[:, t, :], ACT.Square, accum_out=ss_n[:, t:t + 1]).then_inc(n_sq, 1)
        hi(13)
        for t in range(T):
            act.wait_ge(yt_mm, t + 1)
            for ct in range(CT):
                sc.activation(yn_hi[:, ct, t * P:(t + 1) * P], bank(7)[:, ct * P:(ct + 1) * P], ACT.Identity,
                              scale=gn_half[:, ct:ct + 1]).then_inc(yn_hi_done, 1)
        hi(14)

    def dve_program(dve):
        v = nc.vector
        n_link = [0]

        def link(ins):
            n_link[0] += 1
            ins.then_inc(dchain, 1)
            dve.wait_ge(dchain, n_link[0])

        def rsqrt(dst, src, tmp):
            link(v.tensor_scalar(tmp.bitcast(I32), src.bitcast(I32), 1, None, ALU.logical_shift_right))
            link(v.tensor_scalar(dst.bitcast(I32), tmp.bitcast(I32), -1.0, MAGIC, ALU.mult, ALU.add))
            for _ in range(4):
                link(v.tensor_tensor(tmp, dst, dst, ALU.mult))
                link(v.scalar_tensor_tensor(out=tmp, in0=tmp, scalar=-0.5, in1=src, op0=ALU.mult, op1=ALU.mult))
                link(v.scalar_tensor_tensor(out=dst, in0=tmp, scalar=1.5, in1=dst, op0=ALU.add, op1=ALU.mult))

        link(v.memset(ones[:], 1.0))
        link(v.memset(kc_st[:].bitcast(F32), 0.0))
        link(v.memset(gl_g[:], 0.0))
        dve.wait_ge(c_tanh, 1)
        link(v.scalar_tensor_tensor(out=c_silu[:], in0=c_t[:], scalar=1.0, in1=c_col[:], op0=ALU.add, op1=ALU.mult))
        v.tensor_scalar(c_silu[:], c_silu[:], 0.5, None, ALU.mult).then_inc(c_ready, 1)
        dve.wait_ge(cols_done, 1)
        v.tensor_copy(cols_a[:].rearrange("p c r -> p (c r)"), bank(5)[:, 0:CT * ROWS]).then_inc(dchain, 1)
        n_link[0] += 1
        link(v.tensor_copy(cols_b[:], bank(5)[:, CT * ROWS:CT * ROWS + QROWS]))
        lam = cols_a[:, :, R_LAM]
        v.scalar_tensor_tensor(out=lam_abs[:], in0=lam, scalar=-1.0, in1=lam, op0=ALU.mult, op1=ALU.max).then_inc(lam_ready, 1)
        dve.wait_ge(ssx_ready, T)
        link(v.tensor_scalar(ss_x[:], ss_x[:], 1.0 / D, EPS, ALU.mult, ALU.add))
        rsqrt(rs_x[:], ss_x[:], nt1[:, 0:T])
        for t in range(T):
            v.tensor_scalar(xn[:, t, :], xn[:, t, :], rs_x[:, t:t + 1], None, ALU.mult).then_inc(xn_ready, 1)
        dve.wait_ge(lam_exp, 1)
        link(v.tensor_scalar(lam_s[:], lam_e[:], 2.0, None, ALU.add))
        link(v.reciprocal(lam_s[:], lam_s[:]))
        link(v.tensor_tensor(lam_s[:], lam_s[:], lam_e[:], ALU.mult))
        link(v.tensor_tensor(lam_2[:], lam_s[:], lam_s[:], ALU.mult))
        link(v.tensor_scalar(sp[:], lam_2[:], 1.0 / 15, None, ALU.mult))
        for odd in (13, 11, 9, 7, 5, 3):
            link(v.scalar_tensor_tensor(out=sp[:], in0=sp[:], scalar=1.0 / odd, in1=lam_2[:], op0=ALU.add, op1=ALU.mult))
        link(v.scalar_tensor_tensor(out=sp[:], in0=sp[:], scalar=1.0, in1=lam_s[:], op0=ALU.add, op1=ALU.mult))
        link(v.tensor_scalar(lam_2[:], lam, -1.0, 0.0, ALU.mult, ALU.max))
        link(v.scalar_tensor_tensor(out=sp[:], in0=sp[:], scalar=2.0, in1=lam_2[:], op0=ALU.mult, op1=ALU.add))
        link(v.tensor_scalar(p4sp[:], sp[:], LRU_C / 2, None, ALU.mult))
        link(v.tensor_scalar(n4sp[:], sp[:], -LRU_C / 2, None, ALU.mult))
        for m, r in enumerate((R_BA, R_BX)):
            link(v.tensor_scalar(hb[:, m, :], cols_a[:, :, r], 0.5, None, ALU.mult))
        link(v.tensor_scalar(gl_half[:], cols_a[:, :, R_GL], 0.5, None, ALU.mult))
        link(v.tensor_scalar(gn_half[:], cols_a[:, :, R_GN], 0.5, None, ALU.mult))
        for b, r in enumerate((Q_GS, Q_GW, Q_GC)):
            ins = v.scalar_tensor_tensor(out=gk[:, b:b + 1], in0=cols_b[:, Q_GQ:Q_GQ + 1], scalar=SCALE,
                                         in1=cols_b[:, r:r + 1], op0=ALU.mult, op1=ALU.mult)
            if b == 2:
                ins.then_inc(cols_ready, 1)
            else:
                link(ins)
        dve.wait_ge(ada_mm, KC)
        dve.wait_ge(small_in, 32)
        link(v.tensor_tensor(mod[:], bank(4)[:, 0:2 * KC].rearrange("p (s k) -> p s k", s=2), b_mod[:], ALU.add))
        link(v.scalar_tensor_tensor(out=s1[:], in0=mod[:, 1, :], scalar=1.0, in1=ng_col[:], op0=ALU.add, op1=ALU.mult))
        dve.wait_ge(xt_ready, 2 * T)

        def h_lo_part(k):
            dve.wait_ge(h_hi_ready, k + 1)
            v.tensor_tensor(h_lo[:, k, :], xT[:, k, :], h_hi[:, k, :].bitcast(F32), ALU.subtract).then_inc(h_ready, 1)

        for k in range(KC):
            v.tensor_scalar(xT[:, k, :], xT[:, k, :], s1[:, k:k + 1], mod[:, 0, k:k + 1], ALU.mult, ALU.add).then_inc(h_full, 1)
            if k >= 1:
                dve.wait_ge(h_full, k)
                h_lo_part(k - 1)
        dve.wait_ge(h_full, KC)
        h_lo_part(KC - 1)
        dve.wait_ge(h_ready, KC)
        v.memset(lru_x[:, :, 0:3], 0.0).then_inc(dchain, 1)
        n_link[0] += 1
        dve.wait_ge(g24_tanh, 1)
        v.tensor_scalar(gates[:], gates[:], 0.5, 0.5, ALU.mult, ALU.add).then_inc(gates_ready, 1)
        for ct in range(CT):
            dve.wait_ge(lru_x_ready, ct + 1)
            dve.wait_ge(dchain, n_link[0])
            link(v.tensor_scalar(lru_h[:, ct, :], lru_x[:, ct, 0:S], cols_a[:, ct, R_CW:R_CW + 1],
                                 cols_a[:, ct, R_CB:R_CB + 1], ALU.mult, ALU.add))
            for i in range(1, TAPS):
                ins = v.scalar_tensor_tensor(out=lru_h[:, ct, :], in0=lru_x[:, ct, i:i + S],
                                             scalar=cols_a[:, ct, R_CW + i:R_CW + i + 1], in1=lru_h[:, ct, :],
                                             op0=ALU.mult, op1=ALU.add)
                if i == TAPS - 1:
                    ins.then_inc(xc_ready, 1)
                else:
                    link(ins)

        def cmp_stack(w):
            dve.wait_ge(piece_done, PC + 1)
            for kv in range(KV):
                for par in range(2):
                    for var in range(2):
                        src = ps[kv * HD:kv * HD + HD, 4 + w, :].rearrange("p (c j e) -> p e j c", j=8, e=2)[:, par]
                        q0 = (Q_POSK, Q_POSV)[w] + 8 * var
                        pos = cols_b[par * HD:par * HD + HD, q0:q0 + 8].unsqueeze(2).broadcast_to([HD, 8, CW])
                        ins = v.tensor_tensor(cmp_x[w][par * HD:par * HD + HD, var, :, kv, :], src, pos, ALU.add)
                        ins.then_inc(cx_ready, 1)

        cmp_stack(0)
        cmp_stack(1)

        def gate_acc(n):
            item_wait(dve, ("gate", n))
            r = raw_of(("gate", n))[:].rearrange("p (k n) -> p k n", k=2)
            for j in range(2):
                k = 2 * n + j
                if k == 0:
                    ins = v.tensor_scalar(gacc[:], r[:, j, :], c_silu[:, k:k + 1], None, ALU.mult)
                else:
                    ins = v.scalar_tensor_tensor(out=gacc[:], in0=r[:, j, :], scalar=c_silu[:, k:k + 1], in1=gacc[:],
                                                 op0=ALU.mult, op1=ALU.add)
                if j == 0:
                    link(ins)
                else:
                    ins.then_inc(gate_used, 1)
            dve.wait_ge(gate_used, n + 1)

        def gelu_dve(w):
            hid = bank(6 + w)[:, 0:4 * CW].rearrange("p (m n) -> p m n", m=2)[:, :, 0:2 * NCMP]
            q = gl_q[:, :, 0:2 * NCMP]
            dve.wait_ge(gl_sq, w + 1)
            link(v.tensor_scalar(q, q, GELU_B, 1.0, ALU.mult, ALU.add))
            v.tensor_tensor(q, hid, q, ALU.mult).then_inc(gl_poly, 1)
            dve.wait_ge(gl_tanh, w + 1)
            if w == 0:
                o, i0, i1 = gl_g[:, :, 0:2 * NCMP], q, hid
                v.scalar_tensor_tensor(out=o, in0=i0, scalar=1.0, in1=i1, op0=ALU.add, op1=ALU.mult).then_inc(gl_ready, 1)
            else:
                link(v.memset(gl_g[:], 0.0))
                for m in range(2):
                    o = gl_g[:, m, :].rearrange("p (k n) -> p k n", k=KV)[:, :, 0:NCMP]
                    i0 = gl_q[:, m, 0:2 * NCMP].rearrange("p (k n) -> p k n", k=KV)
                    i1 = hid[:, m, :].rearrange("p (k n) -> p k n", k=KV)
                    ins = v.scalar_tensor_tensor(out=o, in0=i0, scalar=1.0, in1=i1, op0=ALU.add, op1=ALU.mult)
                    if m == 0:
                        link(ins)
                    else:
                        ins.then_inc(gl_ready, 1)

        gelu_dve(0)
        gate_acc(0)
        for t in range(T):
            dve.wait_ge(kv_sq, t + 1)
            link(v.tensor_reduce(ss_k[:, t, :], sq[t % 2][:, 0:256].rearrange("p (n d) -> p n d", d=HD), AX.X, ALU.add))
            link(v.tensor_scalar(ss_k[:, t, :], ss_k[:, t, :], 1.0 / HD, EPS, ALU.mult, ALU.add))
            rsqrt(rs_k[:, t, :], ss_k[:, t, :], nt1[:, 0:4])
            row = bank(t).rearrange("p (b s n) -> p b s n", b=2, s=2)
            dve.wait_ge(v_hi, 2 * (t + 1))
            for b in range(2):
                ins = v.tensor_tensor(kn[:, t, b * P:(b + 1) * P].rearrange("p (k d) -> p k d", k=KV),
                                      row[:, b, 0, :].rearrange("p (k d) -> p k d", k=KV),
                                      rs_k[:, t, 2 * b:2 * b + 2].unsqueeze(2).broadcast_to([P, KV, HD]), ALU.mult)
                if b == 0:
                    link(ins)
                else:
                    ins.then_inc(kn_ready, 1)
            for b in range(2):
                ins = v.tensor_tensor(v_hl[:, b, :, t, HD:P], row[:, b, 1, :].rearrange("p (k d) -> p k d", k=KV),
                                      v_hl[:, b, :, t, 0:HD].bitcast(F32), ALU.subtract)
                if b == 0:
                    link(ins)
                else:
                    ins.then_inc(v_ready, 1)
        dve.wait_ge(kc_ss, 1)
        ms, kr = gl_r[:, 0:2 * NCMP], gl_q[:, 0, 0:2 * NCMP]
        link(v.tensor_scalar(ms, bank(6)[:, 64:64 + 2 * NCMP], 1.0 / P, EPS, ALU.mult, ALU.add))
        rsqrt(kr, ms, nt1[:, 0:2 * NCMP])
        link(v.tensor_scalar(kr, kr, 0.5, None, ALU.mult))
        kc = gl_t[:, 0:2 * NCMP]
        v.scalar_tensor_tensor(out=kc, in0=bank(6)[:, 0:2 * NCMP], scalar=gk[:, 2:3], in1=kr, op0=ALU.mult,
                               op1=ALU.mult).then_inc(kc_full, 1)
        dve.wait_ge(kc_hi, 1)
        v.tensor_tensor(kc_st[:, 1, :, 0:NCMP], kc.rearrange("p (k n) -> p k n", k=KV),
                        kc_st[:, 0, :, 0:NCMP].bitcast(F32), ALU.subtract).then_inc(kc_ready, 1)
        gate_acc(1)
        dve.wait_ge(rg_tanh, 2 * CT)
        v.scalar_tensor_tensor(out=lru_h[:], in0=lru_d[:], scalar=1.0, in1=lru_h[:], op0=ALU.add, op1=ALU.mult).then_inc(ix_ready, 1)
        for b in range(2):
            for kv in range(KV):
                for n, half in enumerate((kv, 1 - kv)):
                    dve.wait_ge(k_hi, 4 * b + 2 * kv + 2)
                    v.scalar_tensor_tensor(out=k_st[half * HD:half * HD + HD, b, kv, 1, :],
                                           in0=ps[kv * HD:kv * HD + HD, 4 + b, :], scalar=gk[kv * HD:kv * HD + HD, b:b + 1],
                                           in1=k_st[kv * HD:kv * HD + HD, b, kv, 0, :].bitcast(F32),
                                           op0=ALU.mult, op1=ALU.subtract).then_inc(k_ready, 1)
        gate_acc(2)
        dve.wait_ge(a_ready, 3 * CT)
        v.scalar_tensor_tensor(out=lru_c[:], in0=lru_c[:], scalar=1.0, in1=lru_x[:, :, 0:S], op0=ALU.add, op1=ALU.mult).then_inc(one_less_a2, 1)
        for t in range(T):
            dve.wait_ge(q_sq, t + 1)
            link(v.tensor_reduce(ss_q[:, t, :], sq[t % 2][:].rearrange("p (n d) -> p n d", d=HD), AX.X, ALU.add))
            link(v.tensor_scalar(ss_q[:, t, :], ss_q[:, t, :], 1.0 / HD, EPS, ALU.mult, ALU.add))
            rsqrt(rs_q[:, t, :], ss_q[:, t, :], nt1[:, 0:H])
            v.tensor_tensor(qn[:, t, :].rearrange("p (n d) -> p n d", d=HD), bank(t).rearrange("p (n d) -> p n d", d=HD),
                            rs_q[:, t, :].unsqueeze(2).broadcast_to([P, H, HD]), ALU.mult).then_inc(qn_ready, 1)
        gelu_dve(1)
        gate_acc(3)
        dve.wait_ge(sqrt_ready, 1)
        link(v.tensor_tensor(lru_c[:], lru_c[:], lru_h[:], ALU.mult))
        for ct in range(CT):
            v.tensor_tensor_scan(lru_h[:, ct, :], lru_d[:, ct, :], lru_c[:, ct, :], 0.0, ALU.mult, ALU.add).then_inc(lru_h_ready, 1)
        dve.wait_ge(cw2_mm, 2)
        dve.wait_ge(qn_ready, T)
        link(v.memset(v_blk[:], 0.0))
        for kv in range(KV):
            for g in range(G):
                v.tensor_scalar(v_blk[g * CW:(g + 1) * CW, kv, g * HD:(g + 1) * HD],
                                ps[g * CW:(g + 1) * CW, 7, 256 + kv * HD:256 + (kv + 1) * HD], 0.5, None, ALU.mult).then_inc(vc_ready, 1)
        dve.wait_ge(lru_ss, 1)
        link(v.tensor_scalar(ss_l[:], bank(7)[:, 0:T], 1.0 / LRU, EPS, ALU.mult, ALU.add))
        rsqrt(rs_l[:], ss_l[:], nt1[:, 0:T])
        for t in range(T):
            v.tensor_scalar(diag[:, t, :], ident[:], rs_l[:, t:t + 1], None, ALU.mult).then_inc(diag_ready, 1)
        dve.wait_ge(rbc_ready, 1)
        v.tensor_tensor(lru_h[:], lru_h[:], lru_x[:, 0:1, 0:S].broadcast_to([P, CT, S]), ALU.mult).then_inc(hr_ready, 1)

        def q_lo_part(i):
            src = bank(6).rearrange("p (a n) -> p a n", a=H // 2)
            for e in range(2):
                dve.wait_ge(q_hi, 2 * i + e + 1)
                o = 1 - e
                v.tensor_tensor(q_st[i % 2][o * HD:o * HD + HD, e:H:2, :], src[e * HD:e * HD + HD],
                                q_st[i % 2][e * HD:e * HD + HD, e:H:2, :].bitcast(F32), ALU.subtract).then_inc(q_st_ready, 1)

        def cmp_soft(i):
            dve.wait_ge(cs_mm, i + 1)
            if i >= 1:
                dve.wait_ge(ct_mm, i)
            v.tensor_tensor(c_s[:], bank(6)[:, 0:256].rearrange("p (h n) -> p h n", h=H), bias_c[:, i, :, :], ALU.add).then_inc(cs_biased, 1)
            dve.wait_ge(cs_biased, i + 1)
            link(v.tensor_reduce(c_max[:], c_s[:], AX.X, ALU.max))
            v.tensor_tensor(c_s[:], c_s[:], c_max[:].unsqueeze(2).broadcast_to([P, H, CW]), ALU.subtract).then_inc(cs_sub, 1)

        def cmp_factor(i):
            dve.wait_ge(cp_ready, i + 1)
            link(v.tensor_reduce(c_den[:], c_s[:], AX.X, ALU.add))
            link(v.reciprocal(c_den[:], c_den[:]))
            link(v.tensor_tensor(c_f[:], c_den[:], gates[:, i, 0:H], ALU.mult))
            if i == 0:
                link(v.tensor_scalar(c_f[:], c_f[:], valid[:, 0:1], None, ALU.mult))

        def cmp_out(i):
            dve.wait_ge(cpv_mm, i + 1)
            v.tensor_tensor(qn[:, i, :].rearrange("p (n d) -> p n d", d=HD), bank(6).rearrange("p (n d) -> p n d", d=HD),
                            c_f[:].unsqueeze(2).broadcast_to([P, H, HD]), ALU.mult).then_inc(o_init, 1)

        def add_bias(u):
            i, h = u // (2 * H), u % H
            n = (i + 1) * P
            dve.wait_ge(scores_done, u + 1)
            if u >= 2:
                dve.wait_ge(pt_done, u - 1)
            v.tensor_tensor_reduce(out=sc_sb[u % 2][:, 0:n], in0=bank(4)[:, 0:n], in1=bias[:, h, S - n:S], scale=-1.0,
                                   scalar=3e38, op0=ALU.add, op1=ALU.min, accum_out=negmax[:, u:u + 1]).then_inc(biased, 1)

        def pt_lo_part(u):
            n = (u // (2 * H) + 1) * P
            dve.wait_ge(pt_hi_done, u + 1)
            v.tensor_tensor(pt_lo[u % 2][:, 0:n], bank(5)[:, 0:n], pt_hi[u % 2][:, 0:n].bitcast(F32),
                            ALU.subtract).then_inc(pt_lo_done, 1)

        def scale_out(grp):
            i, b, kv = grp // 4, grp % 4 // 2, grp % 2
            dve.wait_ge(probs, 4 * grp + 4)
            f = f_u[:, grp % 2, :]
            link(v.reciprocal(f, den[:, 4 * grp:4 * grp + 4]))
            link(v.tensor_tensor(f, f, gates[:, i, (1 + b) * H + kv * G:(1 + b) * H + kv * G + G], ALU.mult))
            dve.wait_ge(pv_done, 4 * grp + 4)
            if grp >= 2:
                dve.wait_ge(o_added, grp - 1)
            v.tensor_tensor(xo[grp % 2][:], bank(7).rearrange("p (g n) -> p g n", g=G),
                            f.unsqueeze(2).broadcast_to([P, G, P]), ALU.mult).then_inc(o_scaled, 1)

        dve.wait_ge(gates_ready, 1)
        q_lo_part(0)
        dve.wait_ge(bias_ready, 2)
        cmp_soft(0)
        cmp_factor(0)
        cmp_out(0)

        def z_lru(ct):
            dve.wait_ge(zl_tanh, ct + 1)
            tz = lru_x[:, 1 + ct % 2, 0:S]
            link(v.scalar_tensor_tensor(out=tz, in0=tz, scalar=1.0, in1=bank(ct), op0=ALU.add, op1=ALU.mult))
            v.scalar_tensor_tensor(out=lru_h[:, ct, :], in0=tz, scalar=gl_half[:, ct:ct + 1], in1=lru_h[:, ct, :],
                                   op0=ALU.mult, op1=ALU.mult).then_inc(yl_full, 1)

        def yl_lo_dve(ct):
            dve.wait_ge(yl_hi_ready, ct + 1)
            v.tensor_tensor(yl_lo[:, ct, :], lru_h[:, ct, :], yl_hi[:, ct, :].bitcast(F32), ALU.subtract).then_inc(yl_ready, 1)

        for u in range(UNITS + 2):
            i, r = u // (2 * H), u % (2 * H)
            if u < UNITS:
                add_bias(u)
            if 1 <= u <= UNITS:
                pt_lo_part(u - 1)
            if u >= 5 and (u - 5) % 4 == 0:
                scale_out((u - 5) // 4)
            if i + 1 < T and u < UNITS:
                if r == 6:
                    q_lo_part(i + 1)
                if r == 8:
                    cmp_soft(i + 1)
                if r == 10:
                    cmp_factor(i + 1)
                if r == 14:
                    cmp_out(i + 1)
            if ZL_AT <= u < ZL_AT + CT:
                z_lru(u - ZL_AT)
            if ZL_AT + 1 <= u < ZL_AT + 1 + CT:
                yl_lo_dve(u - ZL_AT - 1)
        for t in range(T):
            dve.wait_ge(zn_tanh, t + 1)
            v.scalar_tensor_tensor(out=z_silu[:, t, :], in0=z_silu[:, t, :], scalar=1.0, in1=bank(t), op0=ALU.add,
                                   op1=ALU.mult).then_inc(zn_ready, 1)
        dve.wait_ge(n_sq, T)
        link(v.tensor_scalar(ss_n[:], ss_n[:], 1.0 / S, EPS, ALU.mult, ALU.add))
        rsqrt(rs_n[:], ss_n[:], nt1[:, 0:T])
        dve.wait_ge(zn_ready, T)

        def y_rows(t):
            if t >= 1:
                dve.wait_ge(yt_mm, t)
            v.scalar_tensor_tensor(out=y_b[:], in0=qn[:, t, :], scalar=rs_n[:, t:t + 1], in1=z_silu[:, t, :], op0=ALU.mult,
                                   op1=ALU.mult).then_inc(y_ready, 1)

        y_rows(0)
        for t in range(T):
            dve.wait_ge(yn_hi_done, CT * (t + 1))
            for ct in range(CT):
                v.scalar_tensor_tensor(out=yn_lo[:, ct, t * P:(t + 1) * P], in0=bank(7)[:, ct * P:(ct + 1) * P],
                                       scalar=gn_half[:, ct:ct + 1], in1=yn_hi[:, ct, t * P:(t + 1) * P].bitcast(F32),
                                       op0=ALU.mult, op1=ALU.subtract).then_inc(yn_ready, 1)
            if t + 1 < T:
                y_rows(t + 1)
        dve.wait_ge(xres_in, 16)
        dve.wait_ge(gate_bc, 2)
        for n in range(2 * T):
            half, t = n // T, n % T
            dve.wait_ge(out_mm, n + 1)
            v.tensor_tensor(out_sb[:, n, :], bank(4 * half + t), g_bc[:, half * 512:half * 512 + 512], ALU.mult).then_inc(out_gated, 1)
            dve.wait_ge(out_gated, n + 1)
            v.tensor_tensor(out_sb[:, n, :], out_sb[:, n, :], x_res[:, t, half * 512:half * 512 + 512], ALU.add).then_inc(out_added, 1)

    def pe_program(pe):
        mm = nc.tensor.matmul
        tr = nc.tensor.transpose

        pe.wait_ge(rows_in, 16 * 17)
        pe.wait_ge(pool_setup, 1)
        for ct in range(CT):
            tr(bank(5)[:, ct * ROWS:(ct + 1) * ROWS], rows_a[:, ct * P:(ct + 1) * P], ident[0:ROWS, 0:ROWS])
        tr(bank(5)[:, CT * ROWS:CT * ROWS + QROWS], rows_b[:], ident[0:QROWS, 0:QROWS]).then_inc(cols_done, 1)

        def ada(k):
            item_wait(pe, ("ada", k))
            r = raw_of(("ada", k))
            for j in range(16):
                s, kk = j // KC, j % KC
                last = mm(bank(4)[:, j:j + 1], r[:, s * D + kk:(s + 1) * D:KC], c_silu[:, k:k + 1],
                          start=(k == 0 and j == 0), stop=(k == KC - 1), skip_group_check=True)
            last.then_inc(ada_mm, 1)

        pe.wait_ge(c_ready, 1)
        for k in range(3):
            ada(k)
        for n in range(2 * T):
            t, j = n // 2, n % 2
            pe.wait_ge(xn_ready, t + 1)
            if n >= 4:
                pe.wait_ge(xt_ready, n - 3)
            for q in range(4):
                k = 4 * j + q
                last = tr(bank(n % 4)[:, q * P:(q + 1) * P], xn[:, t, k:D:KC], ident[:])
            last.then_inc(xt_psum, 1)
        for k in range(3, KC):
            ada(k)

        def piece_in(p):
            pe.wait_ge(lo_done, p + 1)

        def triple(p, kk, b, k, acts, cols, first, last, weights_still, rows=None):
            wh, wl = wv(w_hi[p % HL], p)[:, kk, :], wv(w_lo[p % HL], p)[:, kk, :]
            a_hi, a_lo = acts
            j = cols
            dst = bank(b)
            if weights_still:
                a, bb = (wh[:, j * P:(j + 1) * P], wl[:, j * P:(j + 1) * P]), (a_hi, a_lo)
                pairs = ((a[1], bb[0]), (a[0], bb[1]), (a[0], bb[0]))
            else:
                pairs = ((a_lo[:, j * P:(j + 1) * P], wh), (a_hi[:, j * P:(j + 1) * P], wl), (a_hi[:, j * P:(j + 1) * P], wh))
            for n, (l, r) in enumerate(pairs):
                ins = mm(dst, l, r, start=(first and n == 0), stop=(last and n == 2))
            return ins

        def group_step(p0, j, banks, weights_still, n_tiles=4, n_k=4):
            k, b = j // n_tiles, j % n_tiles
            p, kk = p0 + k // n_k, k % n_k
            if j % (n_tiles * n_k) == 0:
                piece_in(p)
            ins = triple(p, kk, banks[b], k, (h_hi[:, k, :], h_lo[:, k, :]), b, k == 0, k == KC - 1, weights_still)
            if j % (n_tiles * n_k) == n_tiles * n_k - 1:
                ins.then_inc(piece_done, 1)

        for j in range(32):
            if j % 4 == 0:
                pe.wait_ge(h_ready, j // 4 + 1)
            group_step(PX, j, (0, 1, 2, 3), True)
        pe.wait_ge(w24_ready, 1)
        for t in range(T):
            for k in range(KC):
                pairs = ((h_lo, w24_hi), (h_hi, w24_lo), (h_hi, w24_hi))
                for n, (a, w) in enumerate(pairs):
                    last = mm(bank(7)[:, t * NG:(t + 1) * NG], a[:, k, t * P:(t + 1) * P], w[:, k, :],
                              start=(k == 0 and n == 0), stop=(k == KC - 1 and n == 2))
        last.then_inc(g24_done, 1)
        for j in range(16):
            group_step(PC, j, (4, 5), True, 2, 8)

        def kv_steps(a, b):
            for j in range(a, b):
                if j == 0:
                    pe.wait_ge(lru_x_ready, CT)
                group_step(PKV, j, (0, 1, 2, 3), False)

        def cmp_hidden(w):
            pe.wait_ge(w1_in, 16 * (w + 1))
            pe.wait_ge(cx_ready, 8 * (w + 1))
            for m in range(2):
                for j in range(16):
                    var, j8 = j // 8, j % 8
                    last = mm(bank(6 + w)[:, m * 2 * CW:m * 2 * CW + 2 * NCMP], w1[:, j, m * P:(m + 1) * P],
                              cmp_x[w][:, var, j8, :, var:var + NCMP], start=(j == 0), stop=(j == 15))
            last.then_inc(hid_mm, 1)

        kv_steps(0, 16)
        cmp_hidden(0)
        kv_steps(16, 22)
        pe.wait_ge(gl_ready, 1)
        pe.wait_ge(w2_in, 48)
        for m in range(2):
            last = mm(bank(6)[:, 0:2 * NCMP], w2k[:, m, :], gl_g[:, m, 0:2 * NCMP], start=(m == 0), stop=(m == 1))
        last.then_inc(cw2_mm, 1)
        kv_steps(22, 26)
        pe.wait_ge(kc_sq, 1)
        mm(bank(6)[:, 64:64 + 2 * NCMP], ones[:], gl_t[:, 0:2 * NCMP], start=True, stop=True).then_inc(kc_ss, 1)
        kv_steps(26, 32)
        pe.wait_ge(xc_ready, CT)
        pe.wait_ge(bd_in, 64)
        pe.wait_ge(kc_full, 1)
        pe.wait_ge(kc_hi, 1)
        pe.wait_ge(g24_tanh, 1)
        for ct in range(CT):
            for m in range(2):
                if ct >= 1:
                    pe.wait_ge(rg_tanh, 2 * ct + m - 1)
                mm(bank(6 + m), bd[:, m, ct, :], lru_h[:, ct, :], start=True, stop=True).then_inc(rg_mm, 1)
        pe.wait_ge(cx_ready, 16)
        for b in range(2):
            for t in range(T):
                pe.wait_ge(kn_ready, t + 1)
                last = tr(bank(4 + b)[:, t * P:(t + 1) * P], kn[:, t, b * P:(b + 1) * P], ident[:])
            last.then_inc(kt_mm, 1)
        pe.wait_ge(v_ready, T)
        for j in range(16):
            group_step(PQ, j, (0, 1, 2, 3), False)
        pe.wait_ge(rg_tanh, 2 * CT)
        cmp_hidden(1)
        for j in range(16, 32):
            group_step(PQ, j, (0, 1, 2, 3), False)
        pe.wait_ge(gl_ready, 2)
        for g in range(G):
            for kv in range(KV):
                for m in range(2):
                    last = mm(ps[g * CW:(g + 1) * CW, 7, 256 + kv * HD:256 + (kv + 1) * HD], gl_g[:, m, kv * CW:(kv + 1) * CW],
                              w2v[:, m, :], start=(m == 0), stop=(m == 1))
        last.then_inc(cw2_mm, 1)
        pe.wait_ge(vc_ready, 2 * G)
        pe.wait_ge(lru_sq, 1)
        for t in range(T):
            for ct in range(CT):
                last = mm(bank(7)[:, t:t + 1], lru_c[:, ct, t * P:(t + 1) * P], ones[:, 0:1], start=(ct == 0), stop=(ct == CT - 1))
        last.then_inc(lru_ss, 1)
        pe.wait_ge(gate_used, 4)
        pe.wait_ge(bg_in, 16)
        pe.wait_ge(k_ready, 8)
        for half in range(2):
            mm(bank(4 + half), ones[:], gacc[:, half * 512:half * 512 + 512], start=True, stop=False)
            mm(bank(4 + half), ones[0:1, :], bg_row[0:1, half * 512:half * 512 + 512], start=False, stop=True).then_inc(gate_mm, 1)
        for t in range(T):
            pe.wait_ge(diag_ready, t + 1)
            last = mm(bank(6)[:, t * P:(t + 1) * P], ones[:], diag[:, t, :], start=True, stop=True)
        last.then_inc(rbc_mm, 1)

        def q_turn(i):
            pe.wait_ge(qn_ready, i + 1)
            if i == 0:
                pe.wait_ge(rbc_ready, 1)
            else:
                pe.wait_ge(o_init, i)
            for a in range(H // 2):
                last = tr(bank(6)[:, a * P:(a + 1) * P], qn[:, i, a * P:(a + 1) * P], ident[:])
            last.then_inc(qt_mm, 1)

        def cmp_scores(i):
            pe.wait_ge(q_st_ready, 2 * (i + 1))
            pe.wait_ge(kc_ready, 1)
            for h in range(H):
                for part in range(2):
                    last = mm(bank(6)[:, h * CW:(h + 1) * CW], q_st[i % 2][:, h, :], kc_st[:, part, h // G, :],
                              start=(part == 0), stop=(part == 1))
            last.then_inc(cs_mm, 1)

        def cmp_turn(i):
            pe.wait_ge(cp_ready, i + 1)
            for kv in range(KV):
                last = tr(bank(6)[:, kv * P:(kv + 1) * P], c_s[:, kv * G:(kv + 1) * G, :].rearrange("p g n -> p (g n)"), ident[:])
            last.then_inc(ct_mm, 1)

        def cmp_values(i):
            pe.wait_ge(cpt_ready, i + 1)
            pe.wait_ge(vc_ready, 2 * G)
            for kv in range(KV):
                last = mm(bank(6)[:, kv * 256:(kv + 1) * 256], c_pt[:, kv, :], v_blk[:, kv, :], start=True, stop=True)
            last.then_inc(cpv_mm, 1)

        def scores(u):
            i, b, h = u // (2 * H), u % (2 * H) // H, u % H
            n = (i + 1) * P
            if u == 0:
                pe.wait_ge(k_ready, 8)
                pe.wait_ge(gate_bc, 2)
            else:
                pe.wait_ge(biased, u)
            pe.wait_ge(q_st_ready, 2 * (i + 1))
            for part in range(2):
                last = mm(bank(4)[:, 0:n], q_st[i % 2][:, h, :], k_st[:, b, h // G, part, 0:n], start=(part == 0), stop=(part == 1))
            last.then_inc(scores_done, 1)

        def turn(u):
            pe.wait_ge(probs, u + 1)
            if u >= 1:
                pe.wait_ge(pt_lo_done, u)
            for kt in range(u // (2 * H) + 1):
                last = tr(bank(5)[:, kt * P:(kt + 1) * P], sc_sb[u % 2][:, kt * P:(kt + 1) * P], ident[:])
            last.then_inc(pt_done, 1)

        def values(u):
            i, b, h = u // (2 * H), u % (2 * H) // H, u % H
            pe.wait_ge(pt_lo_done, u + 1)
            if u % 4 == 0 and u >= 4:
                pe.wait_ge(o_scaled, u // 4)
            for kt in range(i + 1):
                for n, part in enumerate((pt_lo, pt_hi)):
                    last = mm(bank(7)[:, h % G * P:(h % G + 1) * P], part[u % 2][:, kt * P:(kt + 1) * P],
                              v_hl[:, b, h // G, kt, :], start=(kt == 0 and n == 0), stop=(kt == i and n == 1))
            last.then_inc(pv_done, 1)

        def filler(j):
            if j < 32:
                if j == 0:
                    pe.wait_ge(qn_ready, T)
                group_step(PZL, j, (0, 1, 2, 3), True)
            elif j < 64:
                if j == 32:
                    pe.wait_ge(yl_full, CT)
                group_step(PZN, j - 32, (0, 1, 2, 3), False)

        q_turn(0)
        cmp_scores(0)
        for j in range(0, FILL0):
            filler(j)
        cmp_turn(0)
        cmp_values(0)
        nf = FILL0
        for u in range(UNITS + 2):
            i, r = u // (2 * H), u % (2 * H)
            if u < UNITS:
                scores(u)
            if nf < 64 and not (u < ZL_AT and nf >= 32) and not (ZL_AT <= u < ZL_AT + CT + 1):
                filler(nf)
                nf += 1
            if 1 <= u <= UNITS:
                turn(u - 1)
            if i + 1 < T and u < UNITS:
                if r == 6:
                    q_turn(i + 1)
                if r == 8:
                    cmp_scores(i + 1)
                if r == 11:
                    cmp_turn(i + 1)
                if r == 13:
                    cmp_values(i + 1)
            if u >= 2:
                values(u - 2)
        while nf < 64:
            filler(nf)
            nf += 1

        def out_step(p, t, b):
            hi_t, lo_t = (yl_hi, yl_lo) if p < PO + 2 else (yn_hi, yn_lo)
            for kk in range(4):
                ins = triple(p, kk, b, kk, (hi_t[:, kk, :], lo_t[:, kk, :]), t, p < PO + 2 and kk == 0,
                             p >= PO + 2 and kk == 3, False)
            return ins

        pe.wait_ge(zn_ready, T)
        piece_in(PO)
        for t in range(T):
            ins = out_step(PO, t, t)
        ins.then_inc(piece_done, 1)
        pe.wait_ge(o_scaled, 4 * T)
        for t in range(T):
            pe.wait_ge(y_ready, t + 1)
            if t >= 1:
                pe.wait_ge(yn_ready, CT * t)
            for ct in range(CT):
                last = tr(bank(7)[:, ct * P:(ct + 1) * P], y_b[:, ct * P:(ct + 1) * P], ident[:])
            last.then_inc(yt_mm, 1)
            if t < T - 1:
                if t == 0:
                    piece_in(PO + 1)
                ins = out_step(PO + 1, t, 4 + t)
        pe.wait_ge(yn_ready, CT * T)
        ins = out_step(PO + 1, T - 1, 7)
        ins.then_inc(piece_done, 1)
        for half in range(2):
            piece_in(PO + 2 + half)
            for t in range(T):
                out_step(PO + 2 + half, t, 4 * half + t).then_inc(out_mm, 1)

    ZL_AT, FILL0 = 32, 4
    pt_sq = sb("pt_sq", [P, S], r_sb)

    with nc.Block() as block:
        block.sync(sync_program)
        block.gpsimd(pool_program)
        block.scalar(act_program)
        block.vector(dve_program)
        block.tensor(pe_program)


_INS = ['x', 'c', 'w_ada', 'b_ada', 'norm_g', 'w_in', 'conv_w', 'conv_b', 'w_rg_a', 'b_rg_a', 'w_rg_x', 'b_rg_x',
        'lru_lambda', 'cmp_pos_k', 'cmp_w1_k', 'cmp_w2_k', 'cmp_pos_v', 'cmp_w1_v', 'cmp_w2_v', 'g_q', 'g_k_cmp',
        'g_k_slc', 'g_k_win', 'g_out_lru', 'g_out_nsa', 'w_out']
_OUTS = [((1, 512, 1024), 'float32')]


def kernel(**inputs):
    import numpy as _np
    import concourse.bacc as _bacc
    from concourse import mybir as _mybir
    from concourse.bass_utils import run_bass_kernel_spmd as _run

    nc = _bacc.Bacc("TRN2", target_bir_lowering=False, num_devices=1)
    arrays, args = {}, []
    for name in _INS:
        a = _np.ascontiguousarray(inputs[name])
        arrays[f"in_{name}_dram"] = a
        args.append(nc.dram_tensor(f"in_{name}_dram", a.shape, _mybir.dt.from_np(a.dtype), kind="ExternalInput").ap())
    for i, (shape, dtype) in enumerate(_OUTS):
        dt = _mybir.dt.from_np(_np.dtype(dtype))
        args.append(nc.dram_tensor(f"out_{i}_dram", shape, dt, kind="ExternalOutput").ap())
    build(nc, *args)
    r = _run(nc, [arrays], core_ids=[0])
    got = tuple(r.results[0][f"out_{i}_dram"] for i in range(len(_OUTS)))
    return got[0]
```

```python
import concourse.bass as bass
from concourse import mybir

ALU = mybir.AluOpType
ACT = mybir.ActivationFunctionType
AX = mybir.AxisListType
F32 = mybir.dt.float32
F32R = mybir.dt.float32r
I32 = mybir.dt.int32

P = 128
S = 512
D = 1024
T = S // P
KC = D // P
LRU = 512
CT = LRU // P
H = 8
KV = 2
G = H // KV
HD = 64
TAPS = 4
LRU_C = 8.0
CW = 32
NCMP = 31
MASKED = -1e30
EPS = 1e-6
SCALE = HD ** -0.5
SLOPES = [2.0 ** (-8.0 * (h + 1) / H) for h in range(H)]
UNITS = T * 2 * H
GELU_A, GELU_B = 0.7978845608028654, 0.044715
MAGIC = float(0x5F3759DF)

C_XLRU, C_ZLRU, C_Q, C_KCMP, C_KSLC, C_VSLC, C_KWIN, C_VWIN, C_GATE, C_ZNSA = 0, 512, 1024, 1536, 1792, 1920, 2048, 2176, 2304, 2328
NG = 24

R_CW, R_CB, R_BA, R_BX, R_LAM, R_GL, R_GN, ROWS = 0, 4, 5, 6, 7, 8, 9, 10
Q_GQ, Q_GS, Q_GW, Q_GC, Q_POSK, Q_POSV, QROWS = 0, 1, 2, 3, 4, 20, 36

PIECES = ([("in", C_XLRU, 512, k) for k in (0, 4)] + [("in", C_KCMP, 256, 0)]
          + [("in", c, 512, k) for c in (C_KSLC, C_Q, C_ZNSA, C_ZLRU) for k in (0, 4)]
          + [("out", 512 * half, 512, ct) for ct in (0, 4) for half in (0, 1)])
NP = len(PIECES)
PX, PC, PKV, PQ, PZN, PZL, PO = 0, 2, 3, 5, 7, 9, 11
RAW, HL = 3, 2
ITEMS = ([("ada", k) for k in range(6)] + [("w", 0)] + [("ada", k) for k in range(6, KC)] + [("w", p) for p in range(1, 9)]
         + [("gate", 0), ("gate", 1), ("w", 9), ("gate", 2), ("gate", 3)] + [("w", p) for p in range(10, NP)])
ITEM_OF = {it: n for n, it in enumerate(ITEMS)}


def build(nc, x, c, w_ada, b_ada, norm_g, w_in, conv_w, conv_b, w_rg_a, b_rg_a, w_rg_x, b_rg_x, lru_lambda,
          cmp_pos_k, cmp_w1_k, cmp_w2_k, cmp_pos_v, cmp_w1_v, cmp_w2_v, g_q, g_k_cmp, g_k_slc, g_k_win,
          g_out_lru, g_out_nsa, w_out, out):
    x, out = x[0], out[0]
    w_ada, w_in, w_out = w_ada[0], w_in[0], w_out[0]
    w1_dram = (cmp_w1_k[0], cmp_w1_v[0])
    w2_dram = (cmp_w2_k[0], cmp_w2_v[0])

    top = [(nc.sbuf_base + 63) // 64 * 64]

    def region(size):
        at = top[0]
        top[0] = at + (size + 31) // 32 * 32
        return at

    def sb(name, shape, at, dt=F32):
        return nc.alloc_sbuf_tensor_at(name, shape, dt, offset=at)

    r_raw, r_hl, r_ht = region(RAW * 8192), region(HL * 16384), region(32768)
    r_x1, r_x2, r_w1 = region(8256 + 8192), region(16384), region(16384)
    r_kt, r_v, r_qn, r_qs = region(16384), region(8192), region(8192), region(8192)
    r_sb, r_pt, r_xo, r_bc = region(4096), region(8192), region(4096), region(4096)
    r_cs, r_vb, r_gb = region(2048), region(2048), region(4096)

    raw = [sb(f"raw{n}", [P, 2048], r_raw + 8192 * n) for n in range(RAW)]
    w_hi = [sb(f"w_hi{n}", [P, 2048], r_hl + 16384 * n, F32R) for n in range(HL)]
    w_lo = [sb(f"w_lo{n}", [P, 2048], r_hl + 16384 * n + 8192, F32R) for n in range(HL)]
    h_hi = sb("h_hi", [P, KC, S], r_ht, F32R)
    h_lo = sb("h_lo", [P, KC, S], r_ht + 16384, F32R)
    x_res = sb("x_res", [P, T, D], r_ht)
    yn_hi = sb("yn_hi", [P, CT, S], r_ht + 16384, F32R)
    yn_lo = sb("yn_lo", [P, CT, S], r_ht + 24576, F32R)
    xn = sb("xn", [P, T, D], r_x1)
    lru_x = sb("lru_x", [P, CT, S + 3], r_x1)
    lru_h = sb("lru_h", [P, CT, S], r_x1 + 8256)
    z_silu = sb("z_silu", [P, T, S], r_x2 + 8192)
    xT = sb("xT", [P, KC, S], r_x2)
    lru_c = sb("lru_c", [P, CT, S], r_x2)
    lru_d = sb("lru_d", [P, CT, S], r_x2 + 8192)
    yl_hi = sb("yl_hi", [P, CT, S], r_x2, F32R)
    yl_lo = sb("yl_lo", [P, CT, S], r_x1 + 8256, F32R)
    w1 = sb("w1", [P, 16, 256], r_w1)
    bias = sb("bias", [P, H, S], r_w1)
    out_sb = sb("out_sb", [P, 2 * T, 512], r_w1)
    k_st = sb("k_st", [P, 2, KV, 2, S], r_kt, F32R)
    junk = sb("junk", [P, D], r_kt)
    v_hl = sb("v_hl", [P, 2, KV, T, P], r_v, F32R)
    qn = sb("qn", [P, T, S], r_qn)
    kn = sb("kn", [P, T, 256], r_pt + 4096)
    q_st = [sb(f"q_st{n}", [P, H, P], r_qs + 4096 * n, F32R) for n in range(2)]
    bd = sb("bd", [P, 2, CT, P], r_qs)
    w24 = sb("w24", [P, KC, NG], r_qs + 4096)
    w24_hi = sb("w24_hi", [P, KC, NG], r_qs + 4864, F32R)
    w24_lo = sb("w24_lo", [P, KC, NG], r_qs + 5632, F32R)
    sc_sb = [sb(f"sc_sb{n}", [P, S], at) for n, at in enumerate((r_sb, r_sb + 2048, r_bc + 2048))]
    gacc = sb("gacc", [P, D], r_gb)
    macc = sb("macc", [P, 2 * D], r_kt + 8192)
    g24_t = sb("g24_t", [NG, S], r_xo)
    pt_hi = [sb(f"pt_hi{n}", [P, S], r_pt + 4096 * n, F32R) for n in range(2)]
    pt_lo = [sb(f"pt_lo{n}", [P, S], r_pt + 4096 * n + 2048, F32R) for n in range(2)]
    rows_a = sb("rows_a", [ROWS, LRU], r_gb)
    rows_b = sb("rows_b", [QROWS, P], r_gb + 2048)
    cmp_x = [sb(f"cmp_x{w}", [P, 2, 8, KV, CW], r_pt if w == 0 else r_bc) for w in range(2)]
    bias_c = sb("bias_c", [P, H, CW], r_bc)
    mask_c = sb("mask_c", [P, T, CW], r_bc + 1024)
    xo = [sb(f"xo{n}", [P, G, P], r_xo + 2048 * n) for n in range(2)]
    sq = [sb(f"sq{n}", [P, S], r_xo + 2048 * n) for n in range(2)]
    c_s = sb("c_s", [P, H, CW], r_cs)
    c_pt = sb("c_pt", [P, KV, P], r_cs + 1024)
    gl_q = sb("gl_q", [P, 2, 2 * CW], r_cs)
    gl_g = sb("gl_g", [P, 2, 2 * CW], r_cs + 512)
    gl_t = sb("gl_t", [P, 2 * CW], r_cs + 1024)
    gl_r = sb("gl_r", [P, 2 * CW], r_cs + 1280)
    v_blk = sb("v_blk", [P, KV, G * HD], r_vb)
    g_bc = sb("g_bc", [P, D], r_gb)
    y_b = sb("y_b", [P, S], r_xo)

    def small(name, shape, dt=F32):
        n = 1
        for d in shape[1:]:
            n *= d
        return sb(name, shape, region(4 * n), dt)

    early = [r_v]

    def start_small(name, shape):
        at, n = early[0], 1
        for d in shape[1:]:
            n *= d
        early[0] = at + (4 * n + 31) // 32 * 32
        return sb(name, shape, at)

    ident, ones = small("ident", [P, P]), small("ones", [P, P])
    w2k, w2v = sb("w2k", [P, 2, P], r_kt + 4096), sb("w2v", [P, 2, HD], r_cs + 1536)
    diag = sb("diag", [P, T, P], r_cs)
    kc_st = small("kc_st", [P, 2, KV, CW], F32R)
    cols_a, cols_b = small("cols_a", [P, CT, ROWS]), small("cols_b", [P, QROWS])
    den, negmax = small("den", [P, UNITS]), small("negmax", [P, UNITS])
    gates = small("gates", [P, T, NG])
    c_col, c_t, c_silu = start_small("c_col", [P, KC]), start_small("c_t", [P, KC]), small("c_silu", [P, KC])
    b_mod, ng_col, mod, s1 = [start_small(n, sh) for n, sh in (("b_mod", [P, 2, KC]), ("ng_col", [P, KC]), ("mod", [P, 2, KC]), ("s1", [P, KC]))]
    ss_x, rs_x = start_small("ss_x", [P, T]), start_small("rs_x", [P, T])
    gk = small("gk", [P, 3])
    hb, sp, n4sp, p4sp, gl_half = small("hb", [P, 2, CT]), small("sp", [P, CT]), small("n4sp", [P, CT]), small("p4sp", [P, CT]), small("gl_half", [P, CT])
    lam_abs, lam_e, lam_s, lam_2 = [start_small(n, [P, CT]) for n in ("lam_abs", "lam_e", "lam_s", "lam_2")]
    gn_half = small("gn_half", [P, CT])
    ss_q, rs_q = sb("ss_q", [P, T, H], r_vb), sb("rs_q", [P, T, H], r_vb + 128)
    ss_k, rs_k = sb("ss_k", [P, T, 4], r_vb + 256), sb("rs_k", [P, T, 4], r_vb + 320)
    nt1 = small("nt1", [P, 64])
    c_max, c_den, c_f = small("c_max", [P, H]), small("c_den", [P, H]), small("c_f", [P, H])
    f_u = small("f_u", [P, 4, G])
    valid = small("valid", [P, 1])
    ss_l, rs_l, ss_n, rs_n = [small(n, [P, T]) for n in ("ss_l", "rs_l", "ss_n", "rs_n")]

    ps = nc.alloc_psum_tensor("ps", [P, 8, 512], F32)

    names = {}

    def sem(name):
        names[name] = nc.alloc_semaphore(name)
        return names[name]

    rows_in, c_in, small_in, w24_in, bd_in, w2_in, bg_in, w1_in, xres_in, stored = [sem(n) for n in (
        "rows_in", "c_in", "small_in", "w24_in", "bd_in", "w2_in", "bg_in", "w1_in", "xres_in", "stored")]
    x_in = [sem(f"x_in{t}") for t in range(T)]
    raw_in = [sem(f"raw_in{n}") for n in range(RAW)]
    (pool_setup, dve_setup, c_tanh, c_ready, cols_done, cols_ready, ssx_ready, rsx_ready, xn_ready, xt_psum, xt_ready,
     ada_used, ada_mm, gacc_ready, h_full, h_hi_ready, h_ready, hi_done, lo_done, piece_done, z_done, gate_used) = [sem(n) for n in (
        "pool_setup", "dve_setup", "c_tanh", "c_ready", "cols_done", "cols_ready", "ssx_ready", "rsx_ready", "xn_ready", "xt_psum",
        "xt_ready", "ada_used", "ada_mm", "gacc_ready", "h_full", "h_hi_ready", "h_ready", "hi_done", "lo_done", "piece_done",
        "z_done", "gate_used")]
    (w24_hi_ready, w24_ready, g24_done, g24_tanh, g24_turned, gates_ready, lam_exp, lam_ready, lru_x_ready, xc_ready, rg_mm,
     rg_tanh, ix_ready, a_ready, one_less_a2, sqrt_ready, lru_h_ready, lru_sq, lru_ss, diag_ready, rbc_mm, rbc_ready,
     hr_ready, zl_tanh, yl_full, yl_hi_ready, yl_ready) = [sem(n) for n in (
        "w24_hi_ready", "w24_ready", "g24_done", "g24_tanh", "g24_turned", "gates_ready", "lam_exp", "lam_ready", "lru_x_ready",
        "xc_ready", "rg_mm", "rg_tanh", "ix_ready", "a_ready", "one_less_a2", "sqrt_ready", "lru_h_ready", "lru_sq",
        "lru_ss", "diag_ready", "rbc_mm", "rbc_ready", "hr_ready", "zl_tanh", "yl_full", "yl_hi_ready", "yl_ready")]
    (cx_ready, hid_mm, gl_sq, gl_poly, gl_tanh, gl_ready, cw2_mm, kc_sq, kc_ss, kc_full, kc_hi, kc_ready, vc_ready,
     kv_sq, k_sum, q_sum, kn_ready, v_hi, v_ready, kt_mm, k_hi, k_ready, q_sq, qn_ready, gate_mm, gate_bc) = [sem(n) for n in (
        "cx_ready", "hid_mm", "gl_sq", "gl_poly", "gl_tanh", "gl_ready", "cw2_mm", "kc_sq", "kc_ss", "kc_full", "kc_hi",
        "kc_ready", "vc_ready", "kv_sq", "k_sum", "q_sum", "kn_ready", "v_hi", "v_ready", "kt_mm", "k_hi", "k_ready", "q_sq",
        "qn_ready", "gate_mm", "gate_bc")]
    (bias_d, bias_s, bias_ready, qt_mm, q_hi, q_st_ready, cs_mm, cs_sub, cs_biased, cp_ready, ct_mm, cpt_ready, cpv_mm, o_init,
     scores_done, biased, probs, pt_done, pt_hi_done, pt_lo_done, pv_done, o_scaled, o_added,
     zn_tanh, zn_ready, n_sq, y_ready, yt_mm, yn_hi_done, yn_ready, out_mm, out_gated, out_added,
     pchain, dchain, achain) = [sem(n) for n in (
        "bias_d", "bias_s", "bias_ready", "qt_mm", "q_hi", "q_st_ready", "cs_mm", "cs_sub", "cs_biased", "cp_ready", "ct_mm",
        "cpt_ready", "cpv_mm", "o_init", "scores_done", "biased", "probs", "pt_done", "pt_hi_done", "pt_lo_done",
        "pv_done", "o_scaled", "o_added", "zn_tanh", "zn_ready", "n_sq", "y_ready", "yt_mm", "yn_hi_done",
        "yn_ready", "out_mm", "out_gated", "out_added", "pchain", "dchain", "achain")]

    def bank(b):
        return ps[:, b, :]

    def z_wait(eng, g):
        if g % T == T - 1:
            eng.wait_ge(piece_done, PZN + 2 * (g // T + 1))
        else:
            eng.wait_ge(z_done, (T - 1) * (g // T) + g % T + 1)

    def score_bank(u):
        return bank((4, 2)[u % 2])

    def turned_bank(u):
        return bank((5, 3)[u % 2])

    def item_wait(eng, it):
        n = ITEM_OF[it]
        eng.wait_ge(raw_in[n % RAW], 16 * (n // RAW + 1))

    def raw_of(it):
        return raw[ITEM_OF[it] % RAW]

    def piece_cols(p):
        return PIECES[p][2]

    def wv(t, p):
        return t[:].rearrange("p (k n) -> p k n", n=piece_cols(p))

    def small_loads(sp):
        sp.dma_start(rows_a[R_CW:R_CW + TAPS, :], conv_w[0]).then_inc(rows_in, 16)
        for r, v in ((R_CB, conv_b), (R_BA, b_rg_a), (R_BX, b_rg_x), (R_LAM, lru_lambda), (R_GL, g_out_lru), (R_GN, g_out_nsa)):
            sp.dma_start(rows_a[r:r + 1, :], v).then_inc(rows_in, 16)
        for r, v in ((Q_GQ, g_q), (Q_GS, g_k_slc), (Q_GW, g_k_win), (Q_GC, g_k_cmp)):
            sp.dma_start(rows_b[r:r + 1, :].rearrange("o (e d) -> o e d", e=2),
                         v.unsqueeze(1).broadcast_to([1, 2, HD])).then_inc(rows_in, 16)
        for r, v in ((Q_POSK, cmp_pos_k), (Q_POSV, cmp_pos_v)):
            sp.dma_start(rows_b[r:r + 16, :], v[0].rearrange("(j e) d -> j (e d)", e=2)).then_inc(rows_in, 16)
        sp.dma_start(w24[:], w_in.rearrange("(p k) n -> p k n", k=KC)[:, :, C_GATE:C_GATE + NG]).then_inc(w24_in, 16)
        for rep in range(2):
            sp.dma_start(w2k[:, :, rep * HD:rep * HD + HD], w2_dram[0].rearrange("(k p) n -> p k n", p=P)).then_inc(w2_in, 16)
        sp.dma_start(w2v[:], w2_dram[1].rearrange("(k p) n -> p k n", p=P)).then_inc(w2_in, 16)
        sp.wait_ge(pool_setup, 2)
        for m, w in enumerate((w_rg_a, w_rg_x)):
            for e in range(2):
                sp.dma_start(bd[e * HD:e * HD + HD, m, :, e * HD:e * HD + HD],
                              w[0].rearrange("(t e) i j -> e i t j", e=2)[e]).then_inc(bd_in, 16)

    def sync_program(sp):
        for n, (kind, p) in enumerate(ITEMS):
            if n >= RAW:
                k0, p0 = ITEMS[n - RAW]
                sp.wait_ge({"ada": ada_used, "gate": gate_used, "w": lo_done}[k0], p0 + 1)
            slot = raw[n % RAW]
            if kind == "ada":
                src, dst = w_ada.rearrange("(p k) n -> p k n", k=KC)[:, p, 0:2048], slot[:]
            elif kind == "gate":
                src = w_ada.rearrange("(p k) n -> p k n", k=KC)[:, 2 * p:2 * p + 2, 2048:3072]
                dst = slot[:].rearrange("p (k n) -> p k n", k=2)
            else:
                side, c0, n_cols, k0 = PIECES[p]
                if side == "in":
                    src = w_in.rearrange("(p k) n -> p k n", k=KC)[:, k0:k0 + 2048 // n_cols, c0:c0 + n_cols]
                else:
                    src = w_out.rearrange("(k p) n -> p k n", p=P)[:, k0:k0 + 4, c0:c0 + n_cols]
                dst = wv(slot, p)
            sp.dma_start(dst, src).then_inc(raw_in[n % RAW], 16)
            if n == 0:
                for t in range(T):
                    sp.dma_start(xn[:, t, :], x[t * P:(t + 1) * P, :]).then_inc(x_in[t], 16)
            if n == RAW - 1:
                small_loads(sp)
            if (kind, p) == ("w", 2):
                sp.wait_ge(gacc_ready, 1)
                sp.dma_start(gacc[0:1, :], b_ada[0:1, 2048:3072]).then_inc(bg_in, 16)
                sp.dma_start(w1[:], w1_dram[0].rearrange("(k p) n -> p k n", p=P)).then_inc(w1_in, 16)
            if (kind, p) == ("w", 4):
                sp.wait_ge(hid_mm, 1)
                sp.dma_start(w1[:], w1_dram[1].rearrange("(k p) n -> p k n", p=P)).then_inc(w1_in, 16)
        sp.wait_ge(piece_done, PZL + 2)
        sp.dma_start(x_res[:], x.rearrange("(t p) n -> p t n", p=P)).then_inc(xres_in, 16)
        for n in range(2 * T):
            half, t = n // T, n % T
            sp.wait_ge(out_added, n + 1)
            sp.dma_start(out[t * P:(t + 1) * P, half * 512:half * 512 + 512], out_sb[:, n, :]).then_inc(stored, 16)
        sp.wait_ge(stored, 16 * 2 * T)

    def pool_program(g):
        gp = nc.gpsimd
        gp.memset(ident[:], 0.0).then_inc(pchain, 1)
        g.wait_ge(pchain, 1)
        gp.affine_select(out=ident[:], in_=ident[:], compare_op=ALU.not_equal, fill=1.0, base=0,
                         pattern=[[-1, P]], channel_multiplier=1).then_inc(pool_setup, 1)
        gp.memset(bd[:], 0.0).then_inc(pool_setup, 1)
        gp.memset(valid[:], 1.0).then_inc(pchain, 1)
        g.wait_ge(pchain, 2)
        gp.affine_select(out=valid[:], in_=valid[:], compare_op=ALU.is_ge, fill=0.0, base=-31,
                         pattern=[[0, 1]], channel_multiplier=1).then_inc(pool_setup, 1)

        def lo(p):
            g.wait_ge(hi_done, p + 1)
            item_wait(g, ("w", p))
            gp.tensor_tensor(w_lo[p % HL][:], raw_of(("w", p))[:], w_hi[p % HL][:].bitcast(F32),
                             ALU.subtract).then_inc(lo_done, 1)

        g.wait_ge(lam_ready, 1)
        gp.memset(gacc[:], 0.0).then_inc(gacc_ready, 1)
        g.wait_ge(w24_hi_ready, 1)
        gp.tensor_tensor(w24_lo[:], w24[:], w24_hi[:].bitcast(F32), ALU.subtract).then_inc(w24_ready, 1)
        for p in range(PQ + 3):
            lo(p)
        g.wait_ge(hid_mm, 2)
        gp.iota(bias[:, 0, :], pattern=[[1, S]], base=-(S - P), channel_multiplier=-1,
                allow_small_or_imprecise_dtypes=True).then_inc(bias_d, 1)
        gp.iota(bias_c[:, 0, :], pattern=[[16, CW]], base=31, channel_multiplier=-1,
                allow_small_or_imprecise_dtypes=True).then_inc(bias_d, 1)
        gp.memset(mask_c[:], 0.0).then_inc(bias_d, 1)
        lo(8)
        g.wait_ge(bias_s, 2)
        g.wait_ge(bias_d, 3)
        gp.affine_select(out=bias[:, :, S - P:S], in_=bias[:, :, S - P:S], compare_op=ALU.is_ge, fill=MASKED, base=0,
                         pattern=[[0, H], [-1, P]], channel_multiplier=1).then_inc(bias_ready, 1)
        gp.affine_select(out=mask_c[:], in_=mask_c[:], compare_op=ALU.is_ge, fill=MASKED, base=-31,
                         pattern=[[P, T], [-16, CW]], channel_multiplier=1).then_inc(bias_ready, 1)

        def o_add(grp):
            i, b, kv = grp // 4, grp % 4 // 2, grp % 2
            g.wait_ge(o_scaled, grp + 1)
            o = qn[:, i, kv * 256:kv * 256 + 256].rearrange("p (g d) -> p g d", g=G)
            if grp % 4 == 0:
                g.wait_ge(o_init, i + 1)
            n = pool_n[0]
            gp.tensor_tensor(o, o, xo[grp % 2][:, :, 0:HD], ALU.add).then_inc(pchain, 1)
            pool_n[0] += 1
            g.wait_ge(pchain, pool_n[0])
            gp.tensor_tensor(o, o, xo[grp % 2][:, :, HD:P], ALU.add).then_inc(o_added, 1)
            g.wait_ge(o_added, grp + 1)

        pool_n = [2]
        for grp in range(4 * T):
            if grp in LO_AT:
                lo(LO_AT[grp])
            o_add(grp)
        for p in range(13, NP):
            lo(p)

    def act_program(act):
        sc = nc.scalar
        act.dma_start(c_col[:], c[0].rearrange("(p k) -> p k", k=KC)).then_inc(c_in, 16)
        act.dma_start(b_mod[:], b_ada[0, 0:2048].rearrange("(s p k) -> p s k", s=2, k=KC)).then_inc(small_in, 16)
        act.dma_start(ng_col[:], norm_g[0].rearrange("(p k) -> p k", k=KC)).then_inc(small_in, 16)
        def hi(p):
            item_wait(act, ("w", p))
            if p >= HL:
                act.wait_ge(piece_done, p - HL + 1)
            sc.activation(w_hi[p % HL][:], raw_of(("w", p))[:], ACT.Copy).then_inc(hi_done, 1)

        act.wait_ge(c_in, 16)
        sc.activation(c_t[:], c_col[:], ACT.Tanh, scale=0.5).then_inc(c_tanh, 1)
        for t in range(T):
            act.wait_ge(x_in[t], 16)
            if t >= 1:
                act.wait_ge(ssx_ready, t)
            sc.activation(junk[:], xn[:, t, :], ACT.Square, accum_out=ss_x[:, t:t + 1]).then_inc(ssx_ready, 1)
        act.wait_ge(rsx_ready, 1)
        for t in range(T):
            sc.activation(xn[:, t, :], xn[:, t, :], ACT.Copy, scale=rs_x[:, t:t + 1]).then_inc(xn_ready, 1)
        act.wait_ge(w24_in, 16)
        sc.activation(w24_hi[:], w24[:], ACT.Copy).then_inc(w24_hi_ready, 1)
        act.wait_ge(lam_ready, 1)
        sc.activation(lam_e[:], lam_abs[:], ACT.Exp, scale=-1.0).then_inc(lam_exp, 1)
        for n in range(2 * T):
            t, j = n // 2, n % 2
            act.wait_ge(xt_psum, n + 1)
            sc.activation(xT[:, 4 * j:4 * j + 4, t * P:(t + 1) * P],
                          bank(n % 4).rearrange("p (k n) -> p k n", k=4), ACT.Copy).then_inc(xt_ready, 1)
        hi(0)
        for k in range(KC):
            act.wait_ge(h_full, k + 1)
            sc.activation(h_hi[:, k, :], xT[:, k, :], ACT.Copy).then_inc(h_hi_ready, 1)
        hi(1)
        hi(2)
        act.wait_ge(piece_done, PX + 2)
        for ct in range(CT):
            sc.activation(lru_x[:, ct, 3:S + 3], bank(ct), ACT.Copy).then_inc(lru_x_ready, 1)
        hi(3)
        act.wait_ge(g24_done, 1)
        sc.activation(g24_t[:], ps[0:NG, 7, :], ACT.Tanh, scale=0.5).then_inc(g24_tanh, 1)
        hi(4)

        def gelu_act(w):
            hid = bank((6, 0)[w])[:, 0:4 * CW].rearrange("p (m n) -> p m n", m=2)
            act.wait_ge(hid_mm, w + 1)
            sc.activation(gl_q[:, :, 0:2 * NCMP], hid[:, :, 0:2 * NCMP], ACT.Square).then_inc(gl_sq, 1)
            act.wait_ge(gl_poly, w + 1)
            sc.activation(gl_q[:, :, 0:2 * NCMP], gl_q[:, :, 0:2 * NCMP], ACT.Tanh, scale=GELU_A).then_inc(gl_tanh, 1)

        gelu_act(0)
        hi(5)
        act.wait_ge(cw2_mm, 1)
        sc.activation(gl_t[:, 0:2 * NCMP], bank(6)[:, 0:2 * NCMP], ACT.Square, scale=0.5).then_inc(kc_sq, 1)
        act.wait_ge(kc_full, 1)
        sc.activation(kc_st[:, 0, :, 0:NCMP], gl_t[:, 0:2 * NCMP].rearrange("p (k n) -> p k n", k=KV), ACT.Copy).then_inc(kc_hi, 1)
        act.wait_ge(piece_done, PKV + 2)
        act.wait_ge(g24_turned, 1)
        for t in range(T):
            row = bank(t).rearrange("p (b s n) -> p b s n", b=2, s=2)
            if t >= 2:
                act.wait_ge(k_sum, t - 1)
            sc.activation(sq[t % 2][:, 0:256].rearrange("p (b n) -> p b n", b=2), row[:, :, 0, :], ACT.Square).then_inc(kv_sq, 1)
            for b in range(2):
                sc.activation(v_hl[:, b, :, t, 0:HD], row[:, b, 1, :].rearrange("p (k d) -> p k d", k=KV), ACT.Copy).then_inc(v_hi, 1)
        hi(6)
        for ct in range(CT):
            for m in range(2):
                act.wait_ge(rg_mm, 2 * ct + m + 1)
                dst = (lru_c, lru_d)[m]
                sc.activation(dst[:, ct, :], bank(m), ACT.Tanh, scale=0.5, bias=hb[:, m, ct:ct + 1]).then_inc(rg_tanh, 1)
        for b in range(2):
            act.wait_ge(kt_mm, b + 1)
            for kv in range(KV):
                src = ps[kv * HD:kv * HD + HD, 2 + b, :]
                for half in (kv, 1 - kv):
                    sc.activation(k_st[half * HD:half * HD + HD, b, kv, 0, :], src, ACT.Identity,
                                  scale=gk[kv * HD:kv * HD + HD, b:b + 1]).then_inc(k_hi, 1)
        hi(7)
        gelu_act(1)
        act.wait_ge(ix_ready, 1)
        act.wait_ge(rg_tanh, 2 * CT)
        for ct in range(CT):
            sc.activation(lru_d[:, ct, :], lru_c[:, ct, :], ACT.Exp, scale=n4sp[:, ct:ct + 1], bias=n4sp[:, ct:ct + 1]).then_inc(a_ready, 1)
            sc.activation(lru_x[:, ct, 0:S], lru_c[:, ct, :], ACT.Tanh, scale=p4sp[:, ct:ct + 1], bias=p4sp[:, ct:ct + 1]).then_inc(a_ready, 1)
            act.wait_ge(a_ready, 3 * ct + 2)
            sc.activation(lru_c[:, ct, :], lru_d[:, ct, :], ACT.Square).then_inc(a_ready, 1)
        act.wait_ge(one_less_a2, 1)
        sc.activation(lru_c[:], lru_c[:], ACT.Sqrt, scale=0.25).then_inc(sqrt_ready, 1)
        act.wait_ge(piece_done, PQ + 2)
        for t in range(T):
            if t >= 2:
                act.wait_ge(q_sum, t - 1)
            sc.activation(sq[t % 2][:], bank(4 + t), ACT.Square).then_inc(q_sq, 1)
        hi(8)
        act.wait_ge(bias_d, 2)
        for h in range(H - 1, -1, -1):
            a = sc.activation(bias[:, h, :], bias[:, 0, :], ACT.Copy, scale=SLOPES[h])
            b = sc.activation(bias_c[:, h, :], bias_c[:, 0, :], ACT.Copy, scale=SLOPES[h])
        a.then_inc(bias_s, 1)
        b.then_inc(bias_s, 1)

        def q_hi_part(i):
            act.wait_ge(qt_mm, i + 1)
            if i >= 2:
                act.wait_ge(scores_done, 2 * H * (i - 1))
                act.wait_ge(cs_mm, i - 1)
            src = bank(6).rearrange("p (a n) -> p a n", a=H // 2)
            for e in range(2):
                sc.activation(q_st[i % 2][e * HD:e * HD + HD, e:H:2, :], src[e * HD:e * HD + HD], ACT.Copy).then_inc(q_hi, 1)

        def cmp_exp(i):
            act.wait_ge(cs_sub, i + 1)
            sc.activation(c_s[:], c_s[:], ACT.Exp).then_inc(cp_ready, 1)

        def cmp_pt(i):
            act.wait_ge(ct_mm, i + 1)
            sc.activation(c_pt[:], bank(6)[:, 0:256].rearrange("p (k n) -> p k n", k=KV), ACT.Copy).then_inc(cpt_ready, 1)

        def prob(u):
            act.wait_ge(biased, u + 1)
            n = (u // (2 * H) + 1) * P
            sc.activation(sc_sb[u % 3][:, 0:n], sc_sb[u % 3][:, 0:n], ACT.Exp, scale=-1.0, bias=negmax[:, u:u + 1],
                          accum_out=den[:, u:u + 1]).then_inc(probs, 1)

        def pt_hi_part(u):
            act.wait_ge(pt_done, u + 1)
            if u >= 2:
                act.wait_ge(pv_done, u - 1)
            n = (u // (2 * H) + 1) * P
            sc.activation(pt_hi[u % 2][:, 0:n], turned_bank(u)[:, 0:n], ACT.Copy).then_inc(pt_hi_done, 1)

        q_hi_part(0)
        cmp_exp(0)
        cmp_pt(0)
        def z_lru(ct):
            z_wait(act, T + ct)
            act.wait_ge(hr_ready, 1)
            if ct >= 2:
                act.wait_ge(yl_full, ct - 1)
            sc.activation(lru_x[:, 1 + ct % 2, 0:S], bank(ct % 2), ACT.Tanh, scale=0.5).then_inc(zl_tanh, 1)

        def yl_hi_part(ct):
            act.wait_ge(yl_full, ct + 1)
            sc.activation(yl_hi[:, ct, :], lru_h[:, ct, :], ACT.Copy).then_inc(yl_hi_ready, 1)

        def z_nsa(t):
            z_wait(act, t)
            act.wait_ge(lru_h_ready, CT)
            sc.activation(z_silu[:, t, :], bank(t % 2), ACT.Tanh, scale=0.5).then_inc(zn_tanh, 1)

        for u in range(UNITS + 2):
            i, r = u // (2 * H), u % (2 * H)
            if u in HI_AT:
                hi(HI_AT[u])
            if u >= 2:
                pt_hi_part(u - 2)
            if u < UNITS:
                prob(u)
            if u == 0:
                act.wait_ge(lru_h_ready, CT)
                sc.activation(lru_c[:], lru_h[:], ACT.Square).then_inc(lru_sq, 1)
            if u == 5:
                act.wait_ge(rbc_mm, 1)
                sc.activation(lru_x[:, 0, 0:S], bank(6), ACT.Copy).then_inc(rbc_ready, 1)
            if i + 1 < T and u < UNITS:
                if r == 7:
                    q_hi_part(i + 1)
                if r == 10:
                    cmp_exp(i + 1)
                if r == 13:
                    cmp_pt(i + 1)
            if u in ZN_AT:
                z_nsa(ZN_AT.index(u))
            if u in ZL_AT:
                z_lru(ZL_AT.index(u))
            if u - 1 in ZL_AT:
                yl_hi_part(ZL_AT.index(u - 1))
        for t in range(T):
            act.wait_ge(o_added, 4 * (t + 1))
            if t >= 1:
                act.wait_ge(n_sq, t)
            sc.activation(pt_sq[:], qn[:, t, :], ACT.Square, accum_out=ss_n[:, t:t + 1]).then_inc(n_sq, 1)
        act.wait_ge(gate_mm, 2)
        for half in range(2):
            sc.activation(g_bc[:, half * 512:half * 512 + 512], bank(4 + half), ACT.Copy).then_inc(gate_bc, 1)
        hi(13)
        for t in range(T):
            act.wait_ge(yt_mm, t + 1)
            for ct in range(CT):
                sc.activation(yn_hi[:, ct, t * P:(t + 1) * P], bank(7)[:, ct * P:(ct + 1) * P], ACT.Identity,
                              scale=gn_half[:, ct:ct + 1]).then_inc(yn_hi_done, 1)
        hi(14)

    def dve_program(dve):
        v = nc.vector
        n_link = [0]

        def link(ins):
            n_link[0] += 1
            ins.then_inc(dchain, 1)
            dve.wait_ge(dchain, n_link[0])

        def rsqrt(dst, src, tmp):
            link(v.tensor_scalar(tmp.bitcast(I32), src.bitcast(I32), 1, None, ALU.logical_shift_right))
            link(v.tensor_scalar(dst.bitcast(I32), tmp.bitcast(I32), -1.0, MAGIC, ALU.mult, ALU.add))
            for _ in range(3):
                link(v.tensor_tensor(tmp, dst, dst, ALU.mult))
                link(v.scalar_tensor_tensor(out=tmp, in0=tmp, scalar=-0.5, in1=src, op0=ALU.mult, op1=ALU.mult))
                link(v.scalar_tensor_tensor(out=dst, in0=tmp, scalar=1.5, in1=dst, op0=ALU.add, op1=ALU.mult))

        link(v.memset(ones[:], 1.0))
        link(v.memset(kc_st[:].bitcast(F32), 0.0))
        link(v.memset(gl_g[:], 0.0))
        dve.wait_ge(c_tanh, 1)
        link(v.scalar_tensor_tensor(out=c_silu[:], in0=c_t[:], scalar=1.0, in1=c_col[:], op0=ALU.add, op1=ALU.mult))
        v.tensor_scalar(c_silu[:], c_silu[:], 0.5, None, ALU.mult).then_inc(c_ready, 1)
        def ada_acc(k):
            item_wait(dve, ("ada", k))
            r = raw_of(("ada", k))
            if k == 0:
                dve.wait_ge(c_ready, 1)
                v.tensor_scalar(macc[:], r[:], c_silu[:, k:k + 1], None, ALU.mult).then_inc(ada_used, 1)
            else:
                dve.wait_ge(ada_used, k)
                v.scalar_tensor_tensor(out=macc[:], in0=r[:], scalar=c_silu[:, k:k + 1], in1=macc[:], op0=ALU.mult,
                                       op1=ALU.add).then_inc(ada_used, 1)

        ada_acc(0)
        dve.wait_ge(ssx_ready, T)
        link(v.tensor_scalar(ss_x[:], ss_x[:], 1.0 / D, EPS, ALU.mult, ALU.add))
        rsqrt(rs_x[:], ss_x[:], nt1[:, 0:T])
        v.tensor_copy(rs_x[:], rs_x[:]).then_inc(rsx_ready, 1)
        ada_acc(1)
        ada_acc(2)
        dve.wait_ge(cols_done, 1)
        v.tensor_copy(cols_a[:].rearrange("p c r -> p (c r)"), bank(5)[:, 0:CT * ROWS]).then_inc(dchain, 1)
        n_link[0] += 1
        link(v.tensor_copy(cols_b[:], bank(5)[:, CT * ROWS:CT * ROWS + QROWS]))
        lam = cols_a[:, :, R_LAM]
        v.scalar_tensor_tensor(out=lam_abs[:], in0=lam, scalar=-1.0, in1=lam, op0=ALU.mult, op1=ALU.max).then_inc(lam_ready, 1)
        for k in range(3, KC):
            ada_acc(k)
        dve.wait_ge(ada_mm, 1)
        dve.wait_ge(small_in, 32)
        link(v.tensor_tensor(mod[:], bank(4)[:, 0:2 * KC].rearrange("p (s k) -> p s k", s=2), b_mod[:], ALU.add))
        link(v.scalar_tensor_tensor(out=s1[:], in0=mod[:, 1, :], scalar=1.0, in1=ng_col[:], op0=ALU.add, op1=ALU.mult))
        dve.wait_ge(xt_ready, 2 * T)

        def h_lo_part(k):
            dve.wait_ge(h_hi_ready, k + 1)
            v.tensor_tensor(h_lo[:, k, :], xT[:, k, :], h_hi[:, k, :].bitcast(F32), ALU.subtract).then_inc(h_ready, 1)

        for k in range(KC):
            v.tensor_scalar(xT[:, k, :], xT[:, k, :], s1[:, k:k + 1], mod[:, 0, k:k + 1], ALU.mult, ALU.add).then_inc(h_full, 1)
            if k >= 1:
                dve.wait_ge(h_full, k)
                h_lo_part(k - 1)
        dve.wait_ge(h_full, KC)
        h_lo_part(KC - 1)
        dve.wait_ge(h_ready, KC)
        dve.wait_ge(lam_exp, 1)
        link(v.tensor_scalar(lam_s[:], lam_e[:], 2.0, None, ALU.add))
        link(v.reciprocal(lam_s[:], lam_s[:]))
        link(v.tensor_tensor(lam_s[:], lam_s[:], lam_e[:], ALU.mult))
        link(v.tensor_tensor(lam_2[:], lam_s[:], lam_s[:], ALU.mult))
        link(v.tensor_scalar(sp[:], lam_2[:], 1.0 / 15, None, ALU.mult))
        for odd in (13, 11, 9, 7, 5, 3):
            link(v.scalar_tensor_tensor(out=sp[:], in0=sp[:], scalar=1.0 / odd, in1=lam_2[:], op0=ALU.add, op1=ALU.mult))
        link(v.scalar_tensor_tensor(out=sp[:], in0=sp[:], scalar=1.0, in1=lam_s[:], op0=ALU.add, op1=ALU.mult))
        link(v.tensor_scalar(lam_2[:], lam, -1.0, 0.0, ALU.mult, ALU.max))
        link(v.scalar_tensor_tensor(out=sp[:], in0=sp[:], scalar=2.0, in1=lam_2[:], op0=ALU.mult, op1=ALU.add))
        link(v.tensor_scalar(p4sp[:], sp[:], LRU_C / 2, None, ALU.mult))
        link(v.tensor_scalar(n4sp[:], sp[:], -LRU_C / 2, None, ALU.mult))
        for m, r in enumerate((R_BA, R_BX)):
            link(v.tensor_scalar(hb[:, m, :], cols_a[:, :, r], 0.5, None, ALU.mult))
        link(v.tensor_scalar(gl_half[:], cols_a[:, :, R_GL], 0.5, None, ALU.mult))
        link(v.tensor_scalar(gn_half[:], cols_a[:, :, R_GN], 0.5, None, ALU.mult))
        for b, r in enumerate((Q_GS, Q_GW, Q_GC)):
            ins = v.scalar_tensor_tensor(out=gk[:, b:b + 1], in0=cols_b[:, Q_GQ:Q_GQ + 1], scalar=SCALE,
                                         in1=cols_b[:, r:r + 1], op0=ALU.mult, op1=ALU.mult)
            if b == 2:
                ins.then_inc(cols_ready, 1)
            else:
                link(ins)
        v.memset(lru_x[:, :, 0:3], 0.0).then_inc(dchain, 1)
        n_link[0] += 1
        for ct in range(CT):
            dve.wait_ge(lru_x_ready, ct + 1)
            dve.wait_ge(dchain, n_link[0])
            link(v.tensor_scalar(lru_h[:, ct, :], lru_x[:, ct, 0:S], cols_a[:, ct, R_CW:R_CW + 1],
                                 cols_a[:, ct, R_CB:R_CB + 1], ALU.mult, ALU.add))
            for i in range(1, TAPS):
                ins = v.scalar_tensor_tensor(out=lru_h[:, ct, :], in0=lru_x[:, ct, i:i + S],
                                             scalar=cols_a[:, ct, R_CW + i:R_CW + i + 1], in1=lru_h[:, ct, :],
                                             op0=ALU.mult, op1=ALU.add)
                if i == TAPS - 1:
                    ins.then_inc(xc_ready, 1)
                else:
                    link(ins)

        def cmp_stack(w):
            dve.wait_ge(piece_done, PC + 1)
            for kv in range(KV):
                for par in range(2):
                    for var in range(2):
                        src = ps[kv * HD:kv * HD + HD, 4 + w, :].rearrange("p (c j e) -> p e j c", j=8, e=2)[:, par]
                        q0 = (Q_POSK, Q_POSV)[w] + 8 * var
                        pos = cols_b[par * HD:par * HD + HD, q0:q0 + 8].unsqueeze(2).broadcast_to([HD, 8, CW])
                        ins = v.tensor_tensor(cmp_x[w][par * HD:par * HD + HD, var, :, kv, :], src, pos, ALU.add)
                        ins.then_inc(cx_ready, 1)

        cmp_stack(0)
        cmp_stack(1)
        dve.wait_ge(g24_turned, 1)
        v.tensor_scalar(gates[:], bank(7)[:, 0:T * NG].rearrange("p (t n) -> p t n", t=T), 0.5, 0.5, ALU.mult,
                        ALU.add).then_inc(gates_ready, 1)

        def gate_acc(n):
            item_wait(dve, ("gate", n))
            r = raw_of(("gate", n))[:].rearrange("p (k n) -> p k n", k=2)
            for j in range(2):
                k = 2 * n + j
                if k == 0:
                    dve.wait_ge(bg_in, 16)
                ins = v.scalar_tensor_tensor(out=gacc[:], in0=r[:, j, :], scalar=c_silu[:, k:k + 1], in1=gacc[:],
                                             op0=ALU.mult, op1=ALU.add)
                if j == 0:
                    link(ins)
                else:
                    ins.then_inc(gate_used, 1)
            dve.wait_ge(gate_used, n + 1)

        def gelu_dve(w):
            hid = bank((6, 0)[w])[:, 0:4 * CW].rearrange("p (m n) -> p m n", m=2)[:, :, 0:2 * NCMP]
            q = gl_q[:, :, 0:2 * NCMP]
            dve.wait_ge(gl_sq, w + 1)
            link(v.tensor_scalar(q, q, GELU_B, 1.0, ALU.mult, ALU.add))
            v.tensor_tensor(q, hid, q, ALU.mult).then_inc(gl_poly, 1)
            dve.wait_ge(gl_tanh, w + 1)
            if w == 0:
                o, i0, i1 = gl_g[:, :, 0:2 * NCMP], q, hid
                v.scalar_tensor_tensor(out=o, in0=i0, scalar=1.0, in1=i1, op0=ALU.add, op1=ALU.mult).then_inc(gl_ready, 1)
            else:
                link(v.memset(gl_g[:], 0.0))
                for m in range(2):
                    o = gl_g[:, m, :].rearrange("p (k n) -> p k n", k=KV)[:, :, 0:NCMP]
                    i0 = gl_q[:, m, 0:2 * NCMP].rearrange("p (k n) -> p k n", k=KV)
                    i1 = hid[:, m, :].rearrange("p (k n) -> p k n", k=KV)
                    ins = v.scalar_tensor_tensor(out=o, in0=i0, scalar=1.0, in1=i1, op0=ALU.add, op1=ALU.mult)
                    if m == 0:
                        link(ins)
                    else:
                        ins.then_inc(gl_ready, 1)

        gelu_dve(0)
        dve.wait_ge(kc_ss, 1)
        ms, kr = gl_r[:, 0:2 * NCMP], gl_q[:, 0, 0:2 * NCMP]
        link(v.tensor_scalar(ms, bank(6)[:, 64:64 + 2 * NCMP], 1.0 / P, EPS, ALU.mult, ALU.add))
        rsqrt(kr, ms, nt1[:, 0:2 * NCMP])
        link(v.tensor_scalar(kr, kr, 0.5, None, ALU.mult))
        kc = gl_t[:, 0:2 * NCMP]
        v.scalar_tensor_tensor(out=kc, in0=bank(6)[:, 0:2 * NCMP], scalar=gk[:, 2:3], in1=kr, op0=ALU.mult,
                               op1=ALU.mult).then_inc(kc_full, 1)
        dve.wait_ge(kc_hi, 1)
        v.tensor_tensor(kc_st[:, 1, :, 0:NCMP], kc.rearrange("p (k n) -> p k n", k=KV),
                        kc_st[:, 0, :, 0:NCMP].bitcast(F32), ALU.subtract).then_inc(kc_ready, 1)
        for t in range(T):
            dve.wait_ge(kv_sq, t + 1)
            v.tensor_reduce(ss_k[:, t, :], sq[t % 2][:, 0:256].rearrange("p (n d) -> p n d", d=HD), AX.X, ALU.add).then_inc(k_sum, 1)
        dve.wait_ge(k_sum, T)
        link(v.tensor_scalar(ss_k[:], ss_k[:], 1.0 / HD, EPS, ALU.mult, ALU.add))
        rsqrt(rs_k[:].rearrange("p t n -> p (t n)"), ss_k[:].rearrange("p t n -> p (t n)"), nt1[:, 0:4 * T])
        for t in range(T):
            row = bank(t).rearrange("p (b s n) -> p b s n", b=2, s=2)
            dve.wait_ge(v_hi, 2 * (t + 1))
            for b in range(2):
                v.tensor_tensor(kn[:, t, b * P:(b + 1) * P].rearrange("p (k d) -> p k d", k=KV),
                                row[:, b, 0, :].rearrange("p (k d) -> p k d", k=KV),
                                rs_k[:, t, 2 * b:2 * b + 2].unsqueeze(2).broadcast_to([P, KV, HD]), ALU.mult).then_inc(kn_ready, 1)
            for b in range(2):
                v.tensor_tensor(v_hl[:, b, :, t, HD:P], row[:, b, 1, :].rearrange("p (k d) -> p k d", k=KV),
                                v_hl[:, b, :, t, 0:HD].bitcast(F32), ALU.subtract).then_inc(v_ready, 1)
        dve.wait_ge(rg_tanh, 2 * CT)
        v.scalar_tensor_tensor(out=lru_h[:], in0=lru_d[:], scalar=1.0, in1=lru_h[:], op0=ALU.add, op1=ALU.mult).then_inc(ix_ready, 1)
        for b in range(2):
            for kv in range(KV):
                for n, half in enumerate((kv, 1 - kv)):
                    dve.wait_ge(k_hi, 4 * b + 2 * kv + 2)
                    v.scalar_tensor_tensor(out=k_st[half * HD:half * HD + HD, b, kv, 1, :],
                                           in0=ps[kv * HD:kv * HD + HD, 2 + b, :], scalar=gk[kv * HD:kv * HD + HD, b:b + 1],
                                           in1=k_st[kv * HD:kv * HD + HD, b, kv, 0, :].bitcast(F32),
                                           op0=ALU.mult, op1=ALU.subtract).then_inc(k_ready, 1)
        gelu_dve(1)
        dve.wait_ge(a_ready, 3 * CT)
        v.scalar_tensor_tensor(out=lru_c[:], in0=lru_c[:], scalar=1.0, in1=lru_x[:, :, 0:S], op0=ALU.add, op1=ALU.mult).then_inc(one_less_a2, 1)
        for t in range(T):
            dve.wait_ge(q_sq, t + 1)
            v.tensor_reduce(ss_q[:, t, :], sq[t % 2][:].rearrange("p (n d) -> p n d", d=HD), AX.X, ALU.add).then_inc(q_sum, 1)
        dve.wait_ge(q_sum, T)
        link(v.tensor_scalar(ss_q[:], ss_q[:], 1.0 / HD, EPS, ALU.mult, ALU.add))
        rsqrt(rs_q[:].rearrange("p t n -> p (t n)"), ss_q[:].rearrange("p t n -> p (t n)"), nt1[:, 0:H * T])
        for t in range(T):
            v.tensor_tensor(qn[:, t, :].rearrange("p (n d) -> p n d", d=HD), bank(4 + t).rearrange("p (n d) -> p n d", d=HD),
                            rs_q[:, t, :].unsqueeze(2).broadcast_to([P, H, HD]), ALU.mult).then_inc(qn_ready, 1)

        def lru_scan():
            dve.wait_ge(sqrt_ready, 1)
            link(v.tensor_tensor(lru_c[:], lru_c[:], lru_h[:], ALU.mult))
            for ct in range(CT):
                v.tensor_tensor_scan(lru_h[:, ct, :], lru_d[:, ct, :], lru_c[:, ct, :], 0.0, ALU.mult, ALU.add).then_inc(lru_h_ready, 1)

        def value_blocks():
            dve.wait_ge(qn_ready, T)
            link(v.memset(v_blk[:], 0.0))
            dve.wait_ge(cw2_mm, 2)
            for kv in range(KV):
                for g in range(G):
                    v.tensor_scalar(v_blk[g * CW:(g + 1) * CW, kv, g * HD:(g + 1) * HD],
                                    ps[g * CW:(g + 1) * CW, 3, kv * HD:(kv + 1) * HD], 0.5, None, ALU.mult).then_inc(vc_ready, 1)

        def lru_norm():
            dve.wait_ge(lru_ss, 1)
            link(v.tensor_scalar(ss_l[:], bank(6)[:, 0:T], 1.0 / LRU, EPS, ALU.mult, ALU.add))
            rsqrt(rs_l[:], ss_l[:], nt1[:, 0:T])
            for t in range(T):
                v.tensor_scalar(diag[:, t, :], ident[:], rs_l[:, t:t + 1], None, ALU.mult).then_inc(diag_ready, 1)

        def q_lo_part(i):
            src = bank(6).rearrange("p (a n) -> p a n", a=H // 2)
            for e in range(2):
                dve.wait_ge(q_hi, 2 * i + e + 1)
                o = 1 - e
                v.tensor_tensor(q_st[i % 2][o * HD:o * HD + HD, e:H:2, :], src[e * HD:e * HD + HD],
                                q_st[i % 2][e * HD:e * HD + HD, e:H:2, :].bitcast(F32), ALU.subtract).then_inc(q_st_ready, 1)

        def cmp_soft(i):
            dve.wait_ge(cs_mm, i + 1)
            if i >= 1:
                dve.wait_ge(ct_mm, i)
            link(v.tensor_tensor(c_s[:], bank(6)[:, 0:256].rearrange("p (h n) -> p h n", h=H), bias_c[:], ALU.add))
            v.tensor_tensor(c_s[:], c_s[:], mask_c[:, i:i + 1, :].broadcast_to([P, H, CW]), ALU.add).then_inc(cs_biased, 1)
            dve.wait_ge(cs_biased, i + 1)
            link(v.tensor_reduce(c_max[:], c_s[:], AX.X, ALU.max))
            v.tensor_tensor(c_s[:], c_s[:], c_max[:].unsqueeze(2).broadcast_to([P, H, CW]), ALU.subtract).then_inc(cs_sub, 1)

        def cmp_factor(i):
            dve.wait_ge(cp_ready, i + 1)
            link(v.tensor_reduce(c_den[:], c_s[:], AX.X, ALU.add))
            link(v.reciprocal(c_den[:], c_den[:]))
            link(v.tensor_tensor(c_f[:], c_den[:], gates[:, i, 0:H], ALU.mult))
            if i == 0:
                link(v.tensor_scalar(c_f[:], c_f[:], valid[:, 0:1], None, ALU.mult))

        def cmp_out(i):
            dve.wait_ge(cpv_mm, i + 1)
            v.tensor_tensor(qn[:, i, :].rearrange("p (n d) -> p n d", d=HD), bank(6).rearrange("p (n d) -> p n d", d=HD),
                            c_f[:].unsqueeze(2).broadcast_to([P, H, HD]), ALU.mult).then_inc(o_init, 1)

        def add_bias(u):
            i, h = u // (2 * H), u % H
            n = (i + 1) * P
            dve.wait_ge(scores_done, u + 1)
            if u >= 3:
                dve.wait_ge(pt_done, u - 2)
            v.tensor_tensor_reduce(out=sc_sb[u % 3][:, 0:n], in0=score_bank(u)[:, 0:n], in1=bias[:, h, S - n:S], scale=-1.0,
                                   scalar=3e38, op0=ALU.add, op1=ALU.min, accum_out=negmax[:, u:u + 1]).then_inc(biased, 1)

        def pt_lo_part(u):
            n = (u // (2 * H) + 1) * P
            dve.wait_ge(pt_hi_done, u + 1)
            if u >= 2:
                dve.wait_ge(pv_done, u - 1)
            v.tensor_tensor(pt_lo[u % 2][:, 0:n], turned_bank(u)[:, 0:n], pt_hi[u % 2][:, 0:n].bitcast(F32),
                            ALU.subtract).then_inc(pt_lo_done, 1)

        def out_factor(grp):
            i, b, kv = grp // 4, grp % 4 // 2, grp % 2
            dve.wait_ge(probs, 4 * grp + 4)
            f = f_u[:, grp % 4, :]
            link(v.reciprocal(f, den[:, 4 * grp:4 * grp + 4]))
            link(v.tensor_tensor(f, f, gates[:, i, (1 + b) * H + kv * G:(1 + b) * H + kv * G + G], ALU.mult))

        def scale_out(grp):
            dve.wait_ge(pv_done, 4 * grp + 4)
            if grp >= 2:
                dve.wait_ge(o_added, grp - 1)
            v.tensor_tensor(xo[grp % 2][:], bank(7).rearrange("p (g n) -> p g n", g=G),
                            f_u[:, grp % 4, :].unsqueeze(2).broadcast_to([P, G, P]), ALU.mult).then_inc(o_scaled, 1)

        dve.wait_ge(gates_ready, 1)
        q_lo_part(0)
        value_blocks()
        dve.wait_ge(bias_ready, 2)
        cmp_soft(0)
        cmp_factor(0)
        cmp_out(0)
        lru_scan()

        def z_lru(ct):
            dve.wait_ge(zl_tanh, ct + 1)
            tz = lru_x[:, 1 + ct % 2, 0:S]
            link(v.scalar_tensor_tensor(out=tz, in0=tz, scalar=1.0, in1=bank(ct % 2), op0=ALU.add, op1=ALU.mult))
            v.scalar_tensor_tensor(out=lru_h[:, ct, :], in0=tz, scalar=gl_half[:, ct:ct + 1], in1=lru_h[:, ct, :],
                                   op0=ALU.mult, op1=ALU.mult).then_inc(yl_full, 1)

        def yl_lo_dve(ct):
            dve.wait_ge(yl_hi_ready, ct + 1)
            v.tensor_tensor(yl_lo[:, ct, :], lru_h[:, ct, :], yl_hi[:, ct, :].bitcast(F32), ALU.subtract).then_inc(yl_ready, 1)

        def z_nsa(t):
            dve.wait_ge(zn_tanh, t + 1)
            v.scalar_tensor_tensor(out=z_silu[:, t, :], in0=z_silu[:, t, :], scalar=1.0, in1=bank(t % 2), op0=ALU.add,
                                   op1=ALU.mult).then_inc(zn_ready, 1)

        for u in range(UNITS + 4):
            i, r = u // (2 * H), u % (2 * H)
            if u < UNITS:
                add_bias(u)
            if 3 <= u < UNITS + 3:
                pt_lo_part(u - 3)
            if u >= 6 and (u - 6) % 4 == 0:
                out_factor((u - 6) // 4)
            if u >= 7 and (u - 7) % 4 == 0:
                scale_out((u - 7) // 4)
            if u in GATE_AT:
                gate_acc(GATE_AT.index(u))
            if u == 3:
                lru_norm()
            if u == 7:
                dve.wait_ge(rbc_ready, 1)
                v.tensor_tensor(lru_h[:], lru_h[:], lru_x[:, 0:1, 0:S].broadcast_to([P, CT, S]), ALU.mult).then_inc(hr_ready, 1)
            if i + 1 < T and u < UNITS:
                if r == 7:
                    q_lo_part(i + 1)
                if r == 9:
                    cmp_soft(i + 1)
                if r == 11:
                    cmp_factor(i + 1)
                if r == 15:
                    cmp_out(i + 1)
            if u in ZN_AT:
                z_nsa(ZN_AT.index(u))
            if u in ZL_AT:
                z_lru(ZL_AT.index(u))
            if u - 1 in ZL_AT:
                yl_lo_dve(ZL_AT.index(u - 1))
        dve.wait_ge(n_sq, T)
        link(v.tensor_scalar(ss_n[:], ss_n[:], 1.0 / S, EPS, ALU.mult, ALU.add))
        rsqrt(rs_n[:], ss_n[:], nt1[:, 0:T])
        dve.wait_ge(zn_ready, T)

        def y_rows(t):
            if t >= 1:
                dve.wait_ge(yt_mm, t)
            v.scalar_tensor_tensor(out=y_b[:], in0=qn[:, t, :], scalar=rs_n[:, t:t + 1], in1=z_silu[:, t, :], op0=ALU.mult,
                                   op1=ALU.mult).then_inc(y_ready, 1)

        y_rows(0)
        for t in range(T):
            dve.wait_ge(yn_hi_done, CT * (t + 1))
            for ct in range(CT):
                v.scalar_tensor_tensor(out=yn_lo[:, ct, t * P:(t + 1) * P], in0=bank(7)[:, ct * P:(ct + 1) * P],
                                       scalar=gn_half[:, ct:ct + 1], in1=yn_hi[:, ct, t * P:(t + 1) * P].bitcast(F32),
                                       op0=ALU.mult, op1=ALU.subtract).then_inc(yn_ready, 1)
            if t + 1 < T:
                y_rows(t + 1)
        dve.wait_ge(xres_in, 16)
        dve.wait_ge(gate_bc, 2)
        for n in range(2 * T):
            half, t = n // T, n % T
            dve.wait_ge(out_mm, n + 1)
            v.tensor_tensor(out_sb[:, n, :], bank(4 * half + t), g_bc[:, half * 512:half * 512 + 512], ALU.mult).then_inc(out_gated, 1)
            dve.wait_ge(out_gated, n + 1)
            v.tensor_tensor(out_sb[:, n, :], out_sb[:, n, :], x_res[:, t, half * 512:half * 512 + 512], ALU.add).then_inc(out_added, 1)

    def pe_program(pe):
        mm = nc.tensor.matmul
        tr = nc.tensor.transpose

        pe.wait_ge(rows_in, 16 * 13)
        pe.wait_ge(pool_setup, 1)
        for ct in range(CT):
            tr(bank(5)[:, ct * ROWS:(ct + 1) * ROWS], rows_a[:, ct * P:(ct + 1) * P], ident[0:ROWS, 0:ROWS])
        tr(bank(5)[:, CT * ROWS:CT * ROWS + QROWS], rows_b[:], ident[0:QROWS, 0:QROWS]).then_inc(cols_done, 1)

        pe.wait_ge(ada_used, 4)
        for n in range(2 * T):
            t, j = n // 2, n % 2
            pe.wait_ge(xn_ready, t + 1)
            if n >= 4:
                pe.wait_ge(xt_ready, n - 3)
            for q in range(4):
                k = 4 * j + q
                last = tr(bank(n % 4)[:, q * P:(q + 1) * P], xn[:, t, k:D:KC], ident[:])
            last.then_inc(xt_psum, 1)
        pe.wait_ge(ada_used, KC)
        for j in range(2 * KC):
            s, kk = j // KC, j % KC
            last = mm(bank(4)[:, j:j + 1], macc[:, s * D + kk:(s + 1) * D:KC], ones[:, 0:1], start=True, stop=True)
        last.then_inc(ada_mm, 1)

        def piece_in(p):
            pe.wait_ge(lo_done, p + 1)

        def triple(p, kk, b, k, acts, cols, first, last, weights_still, rows=None):
            wh, wl = wv(w_hi[p % HL], p)[:, kk, :], wv(w_lo[p % HL], p)[:, kk, :]
            a_hi, a_lo = acts
            j = cols
            dst = bank(b)
            if weights_still:
                a, bb = (wh[:, j * P:(j + 1) * P], wl[:, j * P:(j + 1) * P]), (a_hi, a_lo)
                pairs = ((a[1], bb[0]), (a[0], bb[1]), (a[0], bb[0]))
            else:
                pairs = ((a_lo[:, j * P:(j + 1) * P], wh), (a_hi[:, j * P:(j + 1) * P], wl), (a_hi[:, j * P:(j + 1) * P], wh))
            for n, (l, r) in enumerate(pairs):
                ins = mm(dst, l, r, start=(first and n == 0), stop=(last and n == 2))
            return ins

        def group_step(p0, j, banks, weights_still, n_tiles=4, n_k=4):
            k, b = j // n_tiles, j % n_tiles
            p, kk = p0 + k // n_k, k % n_k
            if j % (n_tiles * n_k) == 0:
                piece_in(p)
            ins = triple(p, kk, banks[b], k, (h_hi[:, k, :], h_lo[:, k, :]), b, k == 0, k == KC - 1, weights_still)
            if j % (n_tiles * n_k) == n_tiles * n_k - 1:
                ins.then_inc(piece_done, 1)

        for j in range(32):
            if j % 4 == 0:
                pe.wait_ge(h_ready, j // 4 + 1)
            group_step(PX, j, (0, 1, 2, 3), True)
        pe.wait_ge(w24_ready, 1)
        for k in range(KC):
            for n, (a, w) in enumerate(((h_lo, w24_hi), (h_hi, w24_lo), (h_hi, w24_hi))):
                last = mm(ps[0:NG, 7, :], w[:, k, :], a[:, k, :], start=(k == 0 and n == 0), stop=(k == KC - 1 and n == 2))
        last.then_inc(g24_done, 1)
        for j in range(16):
            group_step(PC, j, (4, 5), True, 2, 8)

        pe.wait_ge(g24_tanh, 1)
        for t in range(T):
            last = tr(bank(7)[:, t * NG:(t + 1) * NG], g24_t[:, t * P:(t + 1) * P], ident[0:NG, 0:NG])
        last.then_inc(g24_turned, 1)

        def kv_steps(a, b):
            for j in range(a, b):
                if j == 0:
                    pe.wait_ge(lru_x_ready, CT)
                group_step(PKV, j, (0, 1, 2, 3), False)

        def cmp_hidden(w, b):
            pe.wait_ge(w1_in, 16 * (w + 1))
            pe.wait_ge(cx_ready, 8 * (w + 1))
            for m in range(2):
                for j in range(16):
                    var, j8 = j // 8, j % 8
                    last = mm(bank(b)[:, m * 2 * CW:m * 2 * CW + 2 * NCMP], w1[:, j, m * P:(m + 1) * P],
                              cmp_x[w][:, var, j8, :, var:var + NCMP], start=(j == 0), stop=(j == 15))
            last.then_inc(hid_mm, 1)

        kv_steps(0, 16)
        cmp_hidden(0, 6)
        kv_steps(16, 22)
        pe.wait_ge(gl_ready, 1)
        pe.wait_ge(w2_in, 48)
        for m in range(2):
            last = mm(bank(6)[:, 0:2 * NCMP], w2k[:, m, :], gl_g[:, m, 0:2 * NCMP], start=(m == 0), stop=(m == 1))
        last.then_inc(cw2_mm, 1)
        kv_steps(22, 25)
        pe.wait_ge(kc_sq, 1)
        mm(bank(6)[:, 64:64 + 2 * NCMP], ones[:], gl_t[:, 0:2 * NCMP], start=True, stop=True).then_inc(kc_ss, 1)
        kv_steps(25, 32)
        pe.wait_ge(cx_ready, 16)
        pe.wait_ge(gates_ready, 1)
        pe.wait_ge(kc_full, 1)
        for j in range(16):
            group_step(PQ, j, (4, 5, 6, 7), False)
        pe.wait_ge(xc_ready, CT)
        pe.wait_ge(bd_in, 64)
        pe.wait_ge(v_ready, 2 * T)
        for ct in range(CT):
            for m in range(2):
                if ct >= 1:
                    pe.wait_ge(rg_tanh, 2 * ct + m - 1)
                mm(bank(m), bd[:, m, ct, :], lru_h[:, ct, :], start=True, stop=True).then_inc(rg_mm, 1)
            if ct == 0:
                for b in range(2):
                    for t in range(T):
                        pe.wait_ge(kn_ready, 2 * (t + 1))
                        last = tr(bank(2 + b)[:, t * P:(t + 1) * P], kn[:, t, b * P:(b + 1) * P], ident[:])
                    last.then_inc(kt_mm, 1)
        pe.wait_ge(rg_tanh, 2 * CT)
        cmp_hidden(1, 0)
        for j in range(16, 32):
            group_step(PQ, j, (4, 5, 6, 7), False)

        def value_weights():
            pe.wait_ge(gl_ready, 2)
            pe.wait_ge(k_ready, 8)
            for g in range(G):
                for kv in range(KV):
                    for m in range(2):
                        last = mm(ps[g * CW:(g + 1) * CW, 3, kv * HD:(kv + 1) * HD], gl_g[:, m, kv * CW:(kv + 1) * CW],
                                  w2v[:, m, :], start=(m == 0), stop=(m == 1))
            last.then_inc(cw2_mm, 1)

        def lru_squares():
            pe.wait_ge(lru_sq, 1)
            pe.wait_ge(o_init, 1)
            for t in range(T):
                for ct in range(CT):
                    last = mm(bank(6)[:, t:t + 1], lru_c[:, ct, t * P:(t + 1) * P], ones[:, 0:1], start=(ct == 0), stop=(ct == CT - 1))
            last.then_inc(lru_ss, 1)

        def lru_rstd():
            for t in range(T):
                pe.wait_ge(diag_ready, t + 1)
                last = mm(bank(6)[:, t * P:(t + 1) * P], ones[:], diag[:, t, :], start=True, stop=True)
            last.then_inc(rbc_mm, 1)

        def q_turn(i):
            pe.wait_ge(qn_ready, 3)
            if i >= 1:
                pe.wait_ge(o_init, i)
            if i == 1:
                pe.wait_ge(rbc_ready, 1)
            for a in range(H // 2):
                last = tr(bank(6)[:, a * P:(a + 1) * P], qn[:, i, a * P:(a + 1) * P], ident[:])
            last.then_inc(qt_mm, 1)

        def cmp_scores(i):
            pe.wait_ge(q_st_ready, 2 * (i + 1))
            pe.wait_ge(kc_ready, 1)
            for h in range(H):
                for part in range(2):
                    last = mm(bank(6)[:, h * CW:(h + 1) * CW], q_st[i % 2][:, h, :], kc_st[:, part, h // G, :],
                              start=(part == 0), stop=(part == 1))
            last.then_inc(cs_mm, 1)

        def cmp_turn(i):
            pe.wait_ge(cp_ready, i + 1)
            for kv in range(KV):
                last = tr(bank(6)[:, kv * P:(kv + 1) * P], c_s[:, kv * G:(kv + 1) * G, :].rearrange("p g n -> p (g n)"), ident[:])
            last.then_inc(ct_mm, 1)

        def cmp_values(i):
            pe.wait_ge(cpt_ready, i + 1)
            pe.wait_ge(vc_ready, 2 * G)
            for kv in range(KV):
                last = mm(bank(6)[:, kv * 256:(kv + 1) * 256], c_pt[:, kv, :], v_blk[:, kv, :], start=True, stop=True)
            last.then_inc(cpv_mm, 1)

        def scores(u):
            i, b, h = u // (2 * H), u % (2 * H) // H, u % H
            n = (i + 1) * P
            if u == 0:
                pe.wait_ge(k_ready, 8)
                pe.wait_ge(qn_ready, T)
            if u >= 2:
                pe.wait_ge(biased, u - 1)
            pe.wait_ge(q_st_ready, 2 * (i + 1))
            for part in range(2):
                last = mm(score_bank(u)[:, 0:n], q_st[i % 2][:, h, :], k_st[:, b, h // G, part, 0:n], start=(part == 0), stop=(part == 1))
            last.then_inc(scores_done, 1)

        def turn(u):
            pe.wait_ge(probs, u + 1)
            if u == 1:
                pe.wait_ge(vc_ready, 2 * G)
            if u >= 2:
                pe.wait_ge(pt_lo_done, u - 1)
            for kt in range(u // (2 * H) + 1):
                last = tr(turned_bank(u)[:, kt * P:(kt + 1) * P], sc_sb[u % 3][:, kt * P:(kt + 1) * P], ident[:])
            last.then_inc(pt_done, 1)

        def values(u):
            i, b, h = u // (2 * H), u % (2 * H) // H, u % H
            pe.wait_ge(pt_lo_done, u + 1)
            if u % 4 == 0 and u >= 4:
                pe.wait_ge(o_scaled, u // 4)
            for kt in range(i + 1):
                for n, part in enumerate((pt_lo, pt_hi)):
                    last = mm(bank(7)[:, h % G * P:(h % G + 1) * P], part[u % 2][:, kt * P:(kt + 1) * P],
                              v_hl[:, b, h // G, kt, :], start=(kt == 0 and n == 0), stop=(kt == i and n == 1))
            last.then_inc(pv_done, 1)

        def filler(j):
            if j < 64:
                g, k = j // KC, j % KC
                t, p = g % T, (PZN if g < T else PZL) + k // 4
                if k == 0:
                    if g < 2:
                        pe.wait_ge(gl_ready, 2)
                    elif g < T + 2:
                        pe.wait_ge(zn_ready, g - 1)
                    else:
                        pe.wait_ge(yl_full, g - T - 1)
                if t == 0:
                    piece_in(p)
                ins = triple(p, k % 4, t % 2, k, (h_hi[:, k, :], h_lo[:, k, :]), t, k == 0, k == KC - 1, g >= T)
                if t == T - 1 and k == 3:
                    ins.then_inc(piece_done, 1)
                if k == KC - 1:
                    ins.then_inc(piece_done if t == T - 1 else z_done, 1)

        def attention_step(u):
            i, r = u // (2 * H), u % (2 * H)
            if u < UNITS:
                scores(u)
            if u >= 4:
                values(u - 4)
            if u in FILL_OF:
                filler(FILL_OF[u])
            if 2 <= u < UNITS + 2:
                turn(u - 2)
            if u == 2:
                lru_squares()
            if u == 5:
                lru_rstd()
            if i + 1 < T and u < UNITS:
                if r == 7:
                    q_turn(i + 1)
                if r == 9:
                    cmp_scores(i + 1)
                if r == 12:
                    cmp_turn(i + 1)
                if r == 14:
                    cmp_values(i + 1)

        for j in range(8):
            filler(j)
        q_turn(0)
        value_weights()
        for j in range(8, 12):
            filler(j)
        cmp_scores(0)
        for j in range(12, FILL0):
            filler(j)
        cmp_turn(0)
        cmp_values(0)
        for u in range(UNITS + 4):
            attention_step(u)

        def out_step(p, t, b):
            hi_t, lo_t = (yl_hi, yl_lo) if p < PO + 2 else (yn_hi, yn_lo)
            for kk in range(4):
                ins = triple(p, kk, b, kk, (hi_t[:, kk, :], lo_t[:, kk, :]), t, p < PO + 2 and kk == 0,
                             p >= PO + 2 and kk == 3, False)
            return ins

        pe.wait_ge(gate_used, 4)
        pe.wait_ge(biased, UNITS)
        pe.wait_ge(pt_lo_done, UNITS)
        for half in range(2):
            mm(bank(4 + half), ones[:], gacc[:, half * 512:half * 512 + 512], start=True, stop=True).then_inc(gate_mm, 1)
        pe.wait_ge(yl_ready, CT)
        piece_in(PO)
        for t in range(T):
            ins = out_step(PO, t, t)
        ins.then_inc(piece_done, 1)
        pe.wait_ge(o_scaled, 4 * T)
        pe.wait_ge(gate_bc, 2)
        for t in range(T):
            pe.wait_ge(y_ready, t + 1)
            if t >= 1:
                pe.wait_ge(yn_ready, CT * t)
            for ct in range(CT):
                last = tr(bank(7)[:, ct * P:(ct + 1) * P], y_b[:, ct * P:(ct + 1) * P], ident[:])
            last.then_inc(yt_mm, 1)
            if t < T - 1:
                if t == 0:
                    piece_in(PO + 1)
                ins = out_step(PO + 1, t, 4 + t)
        pe.wait_ge(yn_ready, CT * T)
        ins = out_step(PO + 1, T - 1, 7)
        ins.then_inc(piece_done, 1)
        for half in range(2):
            piece_in(PO + 2 + half)
            for t in range(T):
                out_step(PO + 2 + half, t, 4 * half + t).then_inc(out_mm, 1)

    FILL0 = 16
    FILL_OF = {u: FILL0 - 3 + u for u in range(3, 51)}
    ZN_AT, ZL_AT = [1, 2, 12, 20], [28, 36, 44, 52]
    HI_AT = {15: 9, 19: 10, 47: 11, 51: 12}
    LO_AT = {3: 9, 4: 10, 11: 11, 12: 12}
    GATE_AT = [6, 10, 14, 18]
    pt_sq = sb("pt_sq", [P, S], r_sb)

    with nc.Block() as block:
        block.sync(sync_program)
        block.gpsimd(pool_program)
        block.scalar(act_program)
        block.vector(dve_program)
        block.tensor(pe_program)


_INS = ['x', 'c', 'w_ada', 'b_ada', 'norm_g', 'w_in', 'conv_w', 'conv_b', 'w_rg_a', 'b_rg_a', 'w_rg_x', 'b_rg_x',
        'lru_lambda', 'cmp_pos_k', 'cmp_w1_k', 'cmp_w2_k', 'cmp_pos_v', 'cmp_w1_v', 'cmp_w2_v', 'g_q', 'g_k_cmp',
        'g_k_slc', 'g_k_win', 'g_out_lru', 'g_out_nsa', 'w_out']
_OUTS = [((1, 512, 1024), 'float32')]


def kernel(**inputs):
    import numpy as _np
    import concourse.bacc as _bacc
    from concourse import mybir as _mybir
    from concourse.bass_utils import run_bass_kernel_spmd as _run

    nc = _bacc.Bacc("TRN2", target_bir_lowering=False, num_devices=1)
    arrays, args = {}, []
    for name in _INS:
        a = _np.ascontiguousarray(inputs[name])
        arrays[f"in_{name}_dram"] = a
        args.append(nc.dram_tensor(f"in_{name}_dram", a.shape, _mybir.dt.from_np(a.dtype), kind="ExternalInput").ap())
    for i, (shape, dtype) in enumerate(_OUTS):
        dt = _mybir.dt.from_np(_np.dtype(dtype))
        args.append(nc.dram_tensor(f"out_{i}_dram", shape, dt, kind="ExternalOutput").ap())
    build(nc, *args)
    r = _run(nc, [arrays], core_ids=[0])
    got = tuple(r.results[0][f"out_{i}_dram"] for i in range(len(_OUTS)))
    return got[0]
```

```python
import concourse.bass as bass
from concourse import mybir

ALU = mybir.AluOpType
ACT = mybir.ActivationFunctionType
AX = mybir.AxisListType
F32 = mybir.dt.float32
F32R = mybir.dt.float32r
I32 = mybir.dt.int32

P = 128
S = 512
D = 1024
T = S // P
KC = D // P
LRU = 512
CT = LRU // P
H = 8
KV = 2
G = H // KV
HD = 64
TAPS = 4
LRU_C = 8.0
CW = 32
NCMP = 31
MASKED = -1e30
EPS = 1e-6
SCALE = HD ** -0.5
SLOPES = [2.0 ** (-8.0 * (h + 1) / H) for h in range(H)]
UNITS = T * 2 * H
GELU_A, GELU_B = 0.7978845608028654, 0.044715
MAGIC = float(0x5F3759DF)

C_XLRU, C_ZLRU, C_Q, C_KCMP, C_KSLC, C_VSLC, C_KWIN, C_VWIN, C_GATE, C_ZNSA = 0, 512, 1024, 1536, 1792, 1920, 2048, 2176, 2304, 2328
NG = 24

R_CW, R_CB, R_BA, R_BX, R_LAM, R_GL, R_GN, ROWS = 0, 4, 5, 6, 7, 8, 9, 10
Q_GQ, Q_GS, Q_GW, Q_GC, Q_POSK, Q_POSV, QROWS = 0, 1, 2, 3, 4, 20, 36

PIECES = ([("in", C_XLRU, 512, k) for k in (0, 4)] + [("in", C_KCMP, 256, 0)]
          + [("in", c, 512, k) for c in (C_KSLC, C_Q, C_ZNSA, C_ZLRU) for k in (0, 4)]
          + [("out", 512 * half, 512, ct) for ct in (0, 4) for half in (0, 1)])
NP = len(PIECES)
PX, PC, PKV, PQ, PZN, PZL, PO = 0, 2, 3, 5, 7, 9, 11
RAW, HL = 3, 2
ITEMS = ([("ada", k) for k in range(KC)]
         + [("w", p) for p in range(4)] + [("gate", 0), ("w", 4), ("gate", 1), ("w", 5), ("gate", 2), ("w", 6), ("gate", 3)]
         + [("w", p) for p in range(7, NP)])
ITEM_OF = {it: n for n, it in enumerate(ITEMS)}


def build(nc, x, c, w_ada, b_ada, norm_g, w_in, conv_w, conv_b, w_rg_a, b_rg_a, w_rg_x, b_rg_x, lru_lambda,
          cmp_pos_k, cmp_w1_k, cmp_w2_k, cmp_pos_v, cmp_w1_v, cmp_w2_v, g_q, g_k_cmp, g_k_slc, g_k_win,
          g_out_lru, g_out_nsa, w_out, out):
    x, out = x[0], out[0]
    w_ada, w_in, w_out = w_ada[0], w_in[0], w_out[0]
    w1_dram = (cmp_w1_k[0], cmp_w1_v[0])
    w2_dram = (cmp_w2_k[0], cmp_w2_v[0])

    top = [(nc.sbuf_base + 63) // 64 * 64]

    def region(size):
        at = top[0]
        top[0] = at + (size + 31) // 32 * 32
        return at

    def sb(name, shape, at, dt=F32):
        return nc.alloc_sbuf_tensor_at(name, shape, dt, offset=at)

    r_raw, r_hl, r_ht = region(RAW * 8192), region(HL * 16384), region(32768)
    r_x1, r_x2, r_w1 = region(8256 + 8192), region(16384), region(16384)
    r_kt, r_v, r_qn, r_qs = region(16384), region(8192), region(8192), region(8192)
    r_sb, r_pt, r_xo, r_bc = region(4096), region(8192), region(4096), region(4096)
    r_cs, r_vb, r_gb = region(2048), region(2048), region(4096)

    raw = [sb(f"raw{n}", [P, 2048], r_raw + 8192 * n) for n in range(RAW)]
    w_hi = [sb(f"w_hi{n}", [P, 2048], r_hl + 16384 * n, F32R) for n in range(HL)]
    w_lo = [sb(f"w_lo{n}", [P, 2048], r_hl + 16384 * n + 8192, F32R) for n in range(HL)]
    h_hi = sb("h_hi", [P, KC, S], r_ht, F32R)
    h_lo = sb("h_lo", [P, KC, S], r_ht + 16384, F32R)
    part = sb("part", [P, 2 * T, 512], r_ht)
    yn_hi = sb("yn_hi", [P, CT, S], r_ht + 16384, F32R)
    yn_lo = sb("yn_lo", [P, CT, S], r_ht + 24576, F32R)
    xn = sb("xn", [P, T, D], r_x1)
    h_f = sb("h_f", [P, KC, S], r_x1)
    lru_x = sb("lru_x", [P, CT, S + 3], r_x1)
    lru_h = sb("lru_h", [P, CT, S], r_x1 + 8256)
    z_silu = sb("z_silu", [P, T, S], r_x2 + 8192)
    xT = sb("xT", [P, KC, S], r_x2)
    lru_c = sb("lru_c", [P, CT, S], r_x2)
    lru_d = sb("lru_d", [P, CT, S], r_x2 + 8192)
    yl_hi = sb("yl_hi", [P, CT, S], r_x2, F32R)
    yl_lo = sb("yl_lo", [P, CT, S], r_x1 + 8256, F32R)
    w1 = sb("w1", [P, 16, 256], r_w1)
    bias = sb("bias", [P, H, S], r_w1)
    x_res = sb("x_res", [P, T, D], r_w1)
    k_st = sb("k_st", [P, 2, KV, 2, S], r_kt, F32R)
    junk = sb("junk", [P, D], r_kt)
    v_hl = sb("v_hl", [P, 2, KV, T, P], r_v, F32R)
    qn = sb("qn", [P, T, S], r_qn)
    kn = sb("kn", [P, T, 256], r_pt + 4096)
    q_st = [sb(f"q_st{n}", [P, H, P], r_qs + 4096 * n, F32R) for n in range(2)]
    bd = sb("bd", [P, 2, CT, P], r_qs)
    w24 = sb("w24", [P, KC, NG], r_qs + 4096)
    w24_hl = sb("w24_hl", [P, KC, 2 * NG], r_qs + 4864, F32R)
    sc_sb = [sb(f"sc_sb{n}", [P, S], at) for n, at in enumerate((r_sb, r_sb + 2048, r_bc + 2048))]
    gacc = sb("gacc", [P, D], r_gb)
    macc = sb("macc", [P, 2 * D], r_kt + 8192)
    g24_t = sb("g24_t", [2 * NG, S], r_xo)
    pt_hi = [sb(f"pt_hi{n}", [P, S], r_pt + 4096 * n, F32R) for n in range(2)]
    pt_lo = [sb(f"pt_lo{n}", [P, S], r_pt + 4096 * n + 2048, F32R) for n in range(2)]
    rows_a = sb("rows_a", [ROWS, LRU], r_gb)
    rows_b = sb("rows_b", [QROWS, P], r_gb + 2048)
    cmp_x = [sb(f"cmp_x{w}", [P, 2, 8, KV, CW], r_pt if w == 0 else r_bc) for w in range(2)]
    bias_c = sb("bias_c", [P, H, CW], r_bc)
    bias_m = sb("bias_m", [P, H, CW], r_bc + 1024)
    xo = [sb(f"xo{n}", [P, G, P], r_xo + 2048 * n) for n in range(2)]
    sq = [sb(f"sq{n}", [P, S], r_xo + 2048 * n) for n in range(2)]
    c_s = sb("c_s", [P, H, CW], r_cs)
    c_pt = sb("c_pt", [P, KV, P], r_cs + 1024)
    gl_q = sb("gl_q", [P, 2, 2 * CW], r_cs)
    gl_g = sb("gl_g", [P, 2, 2 * CW], r_cs + 512)
    gl_t = sb("gl_t", [P, 2 * CW], r_cs + 1024)
    gl_r = sb("gl_r", [P, 2 * CW], r_cs + 1280)
    v_blk = sb("v_blk", [P, KV, G * HD], r_vb)
    g_bc = sb("g_bc", [P, D], r_gb)

    def small(name, shape, dt=F32):
        n = 1
        for d in shape[1:]:
            n *= d
        return sb(name, shape, region(4 * n), dt)

    early = [r_v]

    def start_small(name, shape):
        at, n = early[0], 1
        for d in shape[1:]:
            n *= d
        early[0] = at + (4 * n + 31) // 32 * 32
        return sb(name, shape, at)

    ident, ones = small("ident", [P, P]), small("ones", [P, P])
    pair = small("pair", [2 * NG, NG])
    w2k, w2v = sb("w2k", [P, 2, P], r_kt + 4096), sb("w2v", [P, 2, HD], r_cs + 1536)
    kc_st = small("kc_st", [P, KV, 2, CW], F32R)
    cols_a, cols_b = small("cols_a", [P, CT, ROWS]), small("cols_b", [P, QROWS])
    den, negmax = small("den", [P, UNITS]), small("negmax", [P, UNITS])
    gates = small("gates", [P, T, NG])
    c_col, c_t, c_silu = start_small("c_col", [P, KC]), start_small("c_t", [P, KC]), small("c_silu", [P, KC])
    b_mod, ng_col, mod, s1 = [start_small(n, sh) for n, sh in (("b_mod", [P, 2, KC]), ("ng_col", [P, KC]), ("mod", [P, 2, KC]), ("s1", [P, KC]))]
    msum = start_small("msum", [P, 2 * KC])
    ss_x, rs_x = start_small("ss_x", [P, T]), start_small("rs_x", [P, T])
    gk = small("gk", [P, 3])
    hb, sp, n4sp, p4sp, gl_half = small("hb", [P, 2, CT]), small("sp", [P, CT]), small("n4sp", [P, CT]), small("p4sp", [P, CT]), small("gl_half", [P, CT])
    lam_abs, lam_e, lam_s, lam_2 = [start_small(n, [P, CT]) for n in ("lam_abs", "lam_e", "lam_s", "lam_2")]
    gn_half = small("gn_half", [P, CT])
    ss_q, rs_q = sb("ss_q", [P, T, H], r_vb), sb("rs_q", [P, T, H], r_vb + 128)
    ss_k, rs_k = sb("ss_k", [P, T, 4], r_vb + 256), sb("rs_k", [P, T, 4], r_vb + 320)
    nt1 = small("nt1", [P, 64])
    c_max, c_den, c_f = small("c_max", [P, H]), small("c_den", [P, H]), small("c_f", [P, H])
    f_u = small("f_u", [P, 4, G])
    valid = small("valid", [P, 1])
    ss_l, rs_l, ss_n, rs_n = [small(n, [P, T]) for n in ("ss_l", "rs_l", "ss_n", "rs_n")]

    ps = nc.alloc_psum_tensor("ps", [P, 8, 512], F32)

    names = {}

    def sem(name):
        names[name] = nc.alloc_semaphore(name)
        return names[name]

    rows_in, c_in, small_in, w24_in, bd_in, w2_in, bg_in, w1_in, xres_in, stored = [sem(n) for n in (
        "rows_in", "c_in", "small_in", "w24_in", "bd_in", "w2_in", "bg_in", "w1_in", "xres_in", "stored")]
    x_in = [sem(f"x_in{t}") for t in range(T)]
    shift_in = [sem(f"shift_in{n}") for n in range(RAW)]
    raw_in = [sem(f"raw_in{n}") for n in range(RAW)]
    (pool_setup, c_tanh, c_ready, cols_done, cols_ready, ssx_ready, rsx_ready, xn_ready, xt_psum, xt_ready,
     ada_used, ada_mm, ada_sum, shift_acc, hi_first, gacc_ready, s1_ready, h_full, h_hi_ready, h_ready, hi_done, lo_first, lo_done, piece_done, tile_done, z_done, gate_used) = [sem(n) for n in (
        "pool_setup", "c_tanh", "c_ready", "cols_done", "cols_ready", "ssx_ready", "rsx_ready", "xn_ready", "xt_psum",
        "xt_ready", "ada_used", "ada_mm", "ada_sum", "shift_acc", "hi_first", "gacc_ready", "s1_ready", "h_full", "h_hi_ready", "h_ready", "hi_done", "lo_first", "lo_done", "piece_done",
        "tile_done", "z_done", "gate_used")]
    (w24_hi_ready, w24_ready, g24_done, g24_out, pair_ready, g24_tanh, g24_turned, gates_ready, lam_exp, lam_ready, lru_x_ready, xc_ready, rg_mm,
     rg_tanh, ix_ready, a_ready, one_less_a2, sqrt_ready, lru_in, lru_h_ready, lru_sq, lru_sum, lru_ss, ssl_ready,
     zl_tanh, yl_full, yl_hi_ready, yl_ready) = [sem(n) for n in (
        "w24_hi_ready", "w24_ready", "g24_done", "g24_out", "pair_ready", "g24_tanh", "g24_turned", "gates_ready", "lam_exp", "lam_ready", "lru_x_ready",
        "xc_ready", "rg_mm", "rg_tanh", "ix_ready", "a_ready", "one_less_a2", "sqrt_ready", "lru_in", "lru_h_ready", "lru_sq",
        "lru_sum", "lru_ss", "ssl_ready", "zl_tanh", "yl_full", "yl_hi_ready", "yl_ready")]
    (cx_ready, hid_mm, gl_sq, gl_poly, gl_tanh, gl_ready, cw2_mm, kc_sq, kc_ss, kc_full, kc_hi, kc_ready, vc_ready,
     kv_sq, k_sum, q_sum, kn_ready, v_hi, v_ready, kt_mm, k_hi, k_lo, k_ready, q_sq, qn_ready, gate_mm, gate_bc) = [sem(n) for n in (
        "cx_ready", "hid_mm", "gl_sq", "gl_poly", "gl_tanh", "gl_ready", "cw2_mm", "kc_sq", "kc_ss", "kc_full", "kc_hi",
        "kc_ready", "vc_ready", "kv_sq", "k_sum", "q_sum", "kn_ready", "v_hi", "v_ready", "kt_mm", "k_hi", "k_lo", "k_ready", "q_sq",
        "qn_ready", "gate_mm", "gate_bc")]
    (bias_d, bias_h, bias_s, bias_ready, bias_m_ready, vblk_clear, qt_mm, q_hi, q_st_ready, cs_mm, cs_sub, cs_biased, cp_ready, ct_mm, cpt_ready, cpv_mm, o_init,
     scores_done, biased, probs, pt_done, pt_hi_done, pt_lo_done, pv_done, o_scaled, o_added,
     zn_tanh, zn_ready, n_sq, y_ready, yt_mm, yn_hi_done, yn_ready, out_mm, out_gated, out_added, part_mm, part_ready, res_added,
     pchain, dchain) = [sem(n) for n in (
        "bias_d", "bias_h", "bias_s", "bias_ready", "bias_m_ready", "vblk_clear", "qt_mm", "q_hi", "q_st_ready", "cs_mm", "cs_sub", "cs_biased", "cp_ready", "ct_mm",
        "cpt_ready", "cpv_mm", "o_init", "scores_done", "biased", "probs", "pt_done", "pt_hi_done", "pt_lo_done",
        "pv_done", "o_scaled", "o_added", "zn_tanh", "zn_ready", "n_sq", "y_ready", "yt_mm", "yn_hi_done",
        "yn_ready", "out_mm", "out_gated", "out_added", "part_mm", "part_ready", "res_added", "pchain", "dchain")]

    def bank(b):
        return ps[:, b, :]

    def tile_wait(eng, p0, t):
        if t == T - 1:
            eng.wait_ge(piece_done, p0 + 2)
        else:
            eng.wait_ge(tile_done, 3 * (PX, PKV, PQ).index(p0) + t + 1)

    def z_wait(eng, g):
        if g % T == T - 1:
            eng.wait_ge(piece_done, PZN + 2 * (g // T + 1))
        else:
            eng.wait_ge(z_done, (T - 1) * (g // T) + g % T + 1)

    def score_bank(u):
        return bank((4, 2)[u % 2])

    def turned_bank(u):
        return bank((5, 3)[u % 2])

    def item_wait(eng, it):
        n = ITEM_OF[it]
        eng.wait_ge(raw_in[n % RAW], 16 * (n // RAW + 1))

    def raw_of(it):
        return raw[ITEM_OF[it] % RAW]

    def wv(t, p):
        return t[:].rearrange("p (k n) -> p k n", n=PIECES[p][2])

    def row_loads(sp):
        sp.dma_start(rows_a[R_CW:R_CW + TAPS, :], conv_w[0]).then_inc(rows_in, 16)
        for r, v in ((R_CB, conv_b), (R_BA, b_rg_a), (R_BX, b_rg_x), (R_LAM, lru_lambda), (R_GL, g_out_lru), (R_GN, g_out_nsa)):
            sp.dma_start(rows_a[r:r + 1, :], v).then_inc(rows_in, 16)
        for r, v in ((Q_GQ, g_q), (Q_GS, g_k_slc), (Q_GW, g_k_win), (Q_GC, g_k_cmp)):
            sp.dma_start(rows_b[r:r + 1, :].rearrange("o (e d) -> o e d", e=2),
                         v.unsqueeze(1).broadcast_to([1, 2, HD])).then_inc(rows_in, 16)
        for r, v in ((Q_POSK, cmp_pos_k), (Q_POSV, cmp_pos_v)):
            sp.dma_start(rows_b[r:r + 16, :], v[0].rearrange("(j e) d -> j (e d)", e=2)).then_inc(rows_in, 16)

    def small_loads(sp):
        sp.dma_start(w24[:], w_in.rearrange("(p k) n -> p k n", k=KC)[:, :, C_GATE:C_GATE + NG]).then_inc(w24_in, 16)
        for rep in range(2):
            sp.dma_start(w2k[:, :, rep * HD:rep * HD + HD], w2_dram[0].rearrange("(k p) n -> p k n", p=P)).then_inc(w2_in, 16)
        sp.dma_start(w2v[:], w2_dram[1].rearrange("(k p) n -> p k n", p=P)).then_inc(w2_in, 16)
        sp.wait_ge(pool_setup, 2)
        for m, w in enumerate((w_rg_a, w_rg_x)):
            for e in range(2):
                sp.dma_start(bd[e * HD:e * HD + HD, m, :, e * HD:e * HD + HD],
                              w[0].rearrange("(t e) i j -> e i t j", e=2)[e]).then_inc(bd_in, 16)

    def sync_program(sp):
        for n, (kind, p) in enumerate(ITEMS):
            if n >= RAW:
                k0, p0 = ITEMS[n - RAW]
                sp.wait_ge({"ada": ada_used, "gate": gate_used, "w": lo_done}[k0], p0 + 1)
            slot = raw[n % RAW]
            if kind == "ada":
                src = w_ada.rearrange("(p k) n -> p k n", k=KC)[:, p, 0:2048]
                sp.dma_start(slot[:, 0:D], src[:, 0:D]).then_inc(shift_in[n % RAW], 16)
                src, dst = src[:, D:2 * D], slot[:, D:2 * D]
            elif kind == "gate":
                src = w_ada.rearrange("(p k) n -> p k n", k=KC)[:, 2 * p:2 * p + 2, 2048:3072]
                dst = slot[:].rearrange("p (k n) -> p k n", k=2)
            else:
                side, c0, n_cols, k0 = PIECES[p]
                if side == "in":
                    src = w_in.rearrange("(p k) n -> p k n", k=KC)[:, k0:k0 + 2048 // n_cols, c0:c0 + n_cols]
                else:
                    src = w_out.rearrange("(k p) n -> p k n", p=P)[:, k0:k0 + 4, c0:c0 + n_cols]
                dst = wv(slot, p)
            sp.dma_start(dst, src).then_inc(raw_in[n % RAW], 16)
            if n == 0:
                for t in range(T):
                    sp.dma_start(xn[:, t, :], x[t * P:(t + 1) * P, :]).then_inc(x_in[t], 16)
            if n == RAW - 1:
                row_loads(sp)
            if (kind, p) == ("w", 1):
                small_loads(sp)
            if (kind, p) == ("w", 8):
                for b in range(2):
                    for kv in range(KV):
                        a, o = kv * HD, (1 - kv) * HD
                        sp.wait_ge(k_lo, 2 * b + kv + 1)
                        sp.dma_start(k_st[o:o + HD, b, kv].bitcast(F32), k_st[a:a + HD, b, kv].bitcast(F32)).then_inc(k_ready, 16)
            if (kind, p) == ("w", 2):
                sp.wait_ge(gacc_ready, 1)
                sp.dma_start(gacc[0:1, :], b_ada[0:1, 2048:3072]).then_inc(bg_in, 16)
                sp.dma_start(w1[:], w1_dram[0].rearrange("(k p) n -> p k n", p=P)).then_inc(w1_in, 16)
            if (kind, p) == ("gate", 2):
                sp.wait_ge(hid_mm, 1)
                sp.dma_start(w1[:], w1_dram[1].rearrange("(k p) n -> p k n", p=P)).then_inc(w1_in, 16)
        sp.wait_ge(biased, UNITS)
        sp.dma_start(x_res[:], x.rearrange("(t p) n -> p t n", p=P)).then_inc(xres_in, 16)
        for n, (half, t) in enumerate(OUT_ORDER):
            sp.wait_ge(out_added, n + 1)
            sp.dma_start(out[t * P:(t + 1) * P, half * 512:half * 512 + 512], part[:, half * T + t, :]).then_inc(stored, 16)
        sp.wait_ge(stored, 16 * 2 * T)

    def pool_program(g):
        gp = nc.gpsimd
        gp.memset(ident[:], 0.0).then_inc(pchain, 1)
        g.wait_ge(pchain, 1)
        gp.affine_select(out=ident[:], in_=ident[:], compare_op=ALU.not_equal, fill=1.0, base=0,
                         pattern=[[-1, P]], channel_multiplier=1).then_inc(pool_setup, 1)
        gp.memset(bd[:], 0.0).then_inc(pool_setup, 1)
        g.wait_ge(pool_setup, 1)
        gp.tensor_tensor(pair[:], ident[0:2 * NG, 0:NG], ident[0:2 * NG, NG:2 * NG], ALU.add).then_inc(pair_ready, 1)
        gp.memset(valid[:], 1.0).then_inc(pchain, 1)
        g.wait_ge(pchain, 2)
        gp.affine_select(out=valid[:], in_=valid[:], compare_op=ALU.is_ge, fill=0.0, base=-31,
                         pattern=[[0, 1]], channel_multiplier=1).then_inc(pool_setup, 1)

        def lo(p):
            g.wait_ge(hi_done, p + 1)
            item_wait(g, ("w", p))
            gp.tensor_tensor(w_lo[p % HL][:], raw_of(("w", p))[:], w_hi[p % HL][:].bitcast(F32),
                             ALU.subtract).then_inc(lo_done, 1)

        g.wait_ge(lam_ready, 1)
        gp.memset(gacc[:], 0.0).then_inc(gacc_ready, 1)
        g.wait_ge(hi_first, 1)
        item_wait(g, ("w", 0))
        gp.tensor_tensor(w_lo[0][:, 0:1024], raw_of(("w", 0))[:, 0:1024], w_hi[0][:, 0:1024].bitcast(F32),
                         ALU.subtract).then_inc(lo_first, 1)
        g.wait_ge(hi_done, 1)
        gp.tensor_tensor(w_lo[0][:, 1024:2048], raw_of(("w", 0))[:, 1024:2048], w_hi[0][:, 1024:2048].bitcast(F32),
                         ALU.subtract).then_inc(lo_done, 1)
        lo(1)
        g.wait_ge(w24_hi_ready, 1)
        gp.tensor_tensor(w24_hl[:, :, NG:2 * NG], w24[:], w24_hl[:, :, 0:NG].bitcast(F32), ALU.subtract).then_inc(w24_ready, 1)
        for p in range(2, PQ + 3):
            lo(p)
        g.wait_ge(hid_mm, 2)
        gp.iota(bias[:, 0, :], pattern=[[1, S]], base=-(S - P), channel_multiplier=-1,
                allow_small_or_imprecise_dtypes=True).then_inc(bias_d, 1)
        gp.iota(bias_c[:, 0, :], pattern=[[16, CW]], base=31, channel_multiplier=-1,
                allow_small_or_imprecise_dtypes=True).then_inc(bias_d, 1)
        lo(8)
        g.wait_ge(bias_s, 2)
        gp.affine_select(out=bias[:, :, S - P:S], in_=bias[:, :, S - P:S], compare_op=ALU.is_ge, fill=MASKED, base=0,
                         pattern=[[0, H], [-1, P]], channel_multiplier=1).then_inc(bias_ready, 1)

        def mask_cmp(i):
            if i >= 1:
                g.wait_ge(cs_biased, i)
            gp.affine_select(out=bias_m[:], in_=bias_c[:], compare_op=ALU.is_ge, fill=MASKED, base=i * P - 31,
                             pattern=[[0, H], [-16, CW]], channel_multiplier=1).then_inc(bias_m_ready, 1)

        mask_cmp(0)

        def o_add(grp):
            i, b, kv = grp // 4, grp % 4 // 2, grp % 2
            g.wait_ge(o_scaled, grp + 1)
            o = qn[:, i, kv * 256:kv * 256 + 256].rearrange("p (g d) -> p g d", g=G)
            if grp % 4 == 0:
                g.wait_ge(o_init, i + 1)
            n = pool_n[0]
            gp.tensor_tensor(o, o, xo[grp % 2][:, :, 0:HD], ALU.add).then_inc(pchain, 1)
            pool_n[0] += 1
            g.wait_ge(pchain, pool_n[0])
            gp.tensor_tensor(o, o, xo[grp % 2][:, :, HD:P], ALU.add).then_inc(o_added, 1)
            g.wait_ge(o_added, grp + 1)

        g.wait_ge(qn_ready, T)
        gp.memset(v_blk[:], 0.0).then_inc(vblk_clear, 1)
        g.wait_ge(lru_h_ready, CT)
        gp.tensor_tensor(lru_c[:], lru_h[:], lru_h[:], ALU.mult).then_inc(lru_sq, 1)
        g.wait_ge(lru_sq, 1)
        gp.tensor_tensor(lru_c[:, 0:2, :], lru_c[:, 0:2, :], lru_c[:, 2:4, :], ALU.add).then_inc(lru_sum, 1)
        g.wait_ge(lru_sum, 1)
        gp.tensor_tensor(lru_c[:, 0, :], lru_c[:, 0, :], lru_c[:, 1, :], ALU.add).then_inc(lru_sum, 1)
        pool_n = [2]
        for grp in range(4 * T):
            if grp in LO_AT:
                lo(LO_AT[grp])
            if grp % 4 == 0 and grp // 4 + 1 < T:
                mask_cmp(grp // 4 + 1)
            o_add(grp)
        g.wait_ge(xres_in, 16)
        g.wait_ge(part_ready, 2 * T)
        for half, t in OUT_ORDER:
            n = half * T + t
            gp.tensor_tensor(part[:, n, :], part[:, n, :], x_res[:, t, half * 512:half * 512 + 512], ALU.add).then_inc(res_added, 1)

    def act_program(act):
        sc = nc.scalar
        act.dma_start(c_col[:], c[0].rearrange("(p k) -> p k", k=KC)).then_inc(c_in, 16)
        act.dma_start(b_mod[:], b_ada[0, 0:2048].rearrange("(s p k) -> p s k", s=2, k=KC)).then_inc(small_in, 16)
        act.dma_start(ng_col[:], norm_g[0].rearrange("(p k) -> p k", k=KC)).then_inc(small_in, 16)

        def hi(p):
            item_wait(act, ("w", p))
            if p - HL >= PO:
                act.wait_ge(part_mm, T * (p - HL - PO + 1))
            elif p >= HL:
                act.wait_ge(piece_done, p - HL + 1)
            sc.activation(w_hi[p % HL][:], raw_of(("w", p))[:], ACT.Copy).then_inc(hi_done, 1)

        act.wait_ge(c_in, 16)
        sc.activation(c_t[:], c_col[:], ACT.Tanh, scale=0.5).then_inc(c_tanh, 1)
        for t in range(T):
            act.wait_ge(x_in[t], 16)
            if t >= 1:
                act.wait_ge(ssx_ready, t)
            sc.activation(junk[:], xn[:, t, :], ACT.Square, accum_out=ss_x[:, t:t + 1]).then_inc(ssx_ready, 1)
        act.wait_ge(rsx_ready, 1)
        for t in range(T):
            sc.activation(xn[:, t, :], xn[:, t, :], ACT.Copy, scale=rs_x[:, t:t + 1]).then_inc(xn_ready, 1)
        act.wait_ge(lam_ready, 1)
        sc.activation(lam_e[:], lam_abs[:], ACT.Exp, scale=-1.0).then_inc(lam_exp, 1)
        for n in range(2 * T):
            t, j = n // 2, n % 2
            act.wait_ge(xt_psum, n + 1)
            sc.activation(xT[:, 4 * j:4 * j + 4, t * P:(t + 1) * P],
                          bank(n % 4).rearrange("p (k n) -> p k n", k=4), ACT.Copy).then_inc(xt_ready, 1)
        act.wait_ge(xt_ready, 2 * T)
        item_wait(act, ("w", 0))
        sc.activation(w_hi[0][:, 0:1024], raw_of(("w", 0))[:, 0:1024], ACT.Copy).then_inc(hi_first, 1)
        sc.activation(w_hi[0][:, 1024:2048], raw_of(("w", 0))[:, 1024:2048], ACT.Copy).then_inc(hi_done, 1)
        act.wait_ge(s1_ready, 1)
        for k in range(KC):
            if k == KC // 2:
                hi(1)
            sc.activation(h_hi[:, k, :], xT[:, k, :], ACT.Identity, scale=s1[:, k:k + 1], bias=mod[:, 0, k:k + 1]).then_inc(h_hi_ready, 1)
        act.wait_ge(w24_in, 16)
        sc.activation(w24_hl[:, :, 0:NG], w24[:], ACT.Copy).then_inc(w24_hi_ready, 1)
        hi(2)
        for ct in range(CT):
            tile_wait(act, PX, ct)
            sc.activation(lru_x[:, ct, 3:S + 3], bank(ct), ACT.Copy).then_inc(lru_x_ready, 1)
        hi(3)
        act.wait_ge(g24_done, 1)
        sc.activation(g24_t[:], ps[0:2 * NG, 7, :], ACT.Copy).then_inc(g24_out, 1)
        hi(4)

        def gelu_act(w):
            hid = bank((6, 2)[w])[:, 0:4 * CW].rearrange("p (m n) -> p m n", m=2)
            act.wait_ge(hid_mm, w + 1)
            sc.activation(gl_q[:, :, 0:2 * NCMP], hid[:, :, 0:2 * NCMP], ACT.Square).then_inc(gl_sq, 1)
            act.wait_ge(gl_poly, w + 1)
            sc.activation(gl_q[:, :, 0:2 * NCMP], gl_q[:, :, 0:2 * NCMP], ACT.Tanh, scale=GELU_A).then_inc(gl_tanh, 1)

        gelu_act(0)
        hi(5)
        act.wait_ge(cw2_mm, 1)
        sc.activation(gl_t[:, 0:2 * NCMP], bank(6)[:, 0:2 * NCMP], ACT.Square, scale=0.5).then_inc(kc_sq, 1)
        act.wait_ge(kc_full, 1)
        sc.activation(kc_st[:, :, 0, 0:NCMP], gl_t[:, 0:2 * NCMP].rearrange("p (k n) -> p k n", k=KV), ACT.Copy).then_inc(kc_hi, 1)
        act.wait_ge(g24_turned, 1)
        sc.activation(gates[:], bank(7)[:, 0:T * NG].rearrange("p (t n) -> p t n", t=T), ACT.Tanh, scale=0.5).then_inc(g24_tanh, 1)
        for t in range(T):
            tile_wait(act, PKV, t)
            row = bank(t).rearrange("p (b s n) -> p b s n", b=2, s=2)
            if t >= 2:
                act.wait_ge(k_sum, t - 1)
            sc.activation(sq[t % 2][:, 0:256].rearrange("p (b n) -> p b n", b=2), row[:, :, 0, :], ACT.Square).then_inc(kv_sq, 1)
            for b in range(2):
                sc.activation(v_hl[:, b, :, t, 0:HD], row[:, b, 1, :].rearrange("p (k d) -> p k d", k=KV), ACT.Copy).then_inc(v_hi, 1)
        hi(6)
        for ct in range(CT):
            for m in range(2):
                act.wait_ge(rg_mm, 2 * ct + m + 1)
                dst = (lru_c, lru_d)[m]
                sc.activation(dst[:, ct, :], bank(ct % 2 * 2 + m), ACT.Tanh, scale=0.5, bias=hb[:, m, ct:ct + 1]).then_inc(rg_tanh, 1)
        for b in range(2):
            act.wait_ge(kt_mm, b + 1)
            for kv in range(KV):
                a = kv * HD
                sc.activation(k_st[a:a + HD, b, kv, 0, :], ps[a:a + HD, b, :], ACT.Identity,
                              scale=gk[a:a + HD, b:b + 1]).then_inc(k_hi, 1)
        hi(7)
        act.wait_ge(ix_ready, 1)
        act.wait_ge(rg_tanh, 2 * CT)
        for ct in range(CT):
            sc.activation(lru_d[:, ct, :], lru_c[:, ct, :], ACT.Exp, scale=n4sp[:, ct:ct + 1], bias=n4sp[:, ct:ct + 1]).then_inc(a_ready, 1)
            sc.activation(lru_x[:, ct, 0:S], lru_c[:, ct, :], ACT.Tanh, scale=p4sp[:, ct:ct + 1], bias=p4sp[:, ct:ct + 1]).then_inc(a_ready, 1)
            act.wait_ge(a_ready, 3 * ct + 2)
            sc.activation(lru_c[:, ct, :], lru_d[:, ct, :], ACT.Square).then_inc(a_ready, 1)
        gelu_act(1)
        for t in range(T):
            tile_wait(act, PQ, t)
            if t >= 2:
                act.wait_ge(q_sum, t - 1)
            sc.activation(sq[t % 2][:], bank(4 + t), ACT.Square).then_inc(q_sq, 1)
        for half in range(2):
            act.wait_ge(gate_mm, half + 1)
            sc.activation(g_bc[:, half * 512:half * 512 + 512], bank(2 - half), ACT.Copy).then_inc(gate_bc, 1)
        hi(8)
        act.wait_ge(one_less_a2, 1)
        sc.activation(lru_c[:], lru_c[:], ACT.Sqrt, scale=0.25).then_inc(sqrt_ready, 1)

        def q_hi_part(i):
            act.wait_ge(qt_mm, i + 1)
            if i >= 2:
                act.wait_ge(scores_done, 2 * H * (i - 1))
                act.wait_ge(cs_mm, i - 1)
            src = bank(6).rearrange("p (a n) -> p a n", a=H // 2)
            for e in range(2):
                sc.activation(q_st[i % 2][e * HD:e * HD + HD, e:H:2, :], src[e * HD:e * HD + HD], ACT.Copy).then_inc(q_hi, 1)

        def cmp_exp(i):
            act.wait_ge(cs_sub, i + 1)
            sc.activation(c_s[:], c_s[:], ACT.Exp).then_inc(cp_ready, 1)

        def cmp_pt(i):
            act.wait_ge(ct_mm, i + 1)
            sc.activation(c_pt[:], bank(6)[:, 0:256].rearrange("p (k n) -> p k n", k=KV), ACT.Copy).then_inc(cpt_ready, 1)

        def prob(u):
            act.wait_ge(biased, u + 1)
            n = (u // (2 * H) + 1) * P
            sc.activation(sc_sb[u % 3][:, 0:n], sc_sb[u % 3][:, 0:n], ACT.Exp, scale=-1.0, bias=negmax[:, u:u + 1],
                          accum_out=den[:, u:u + 1]).then_inc(probs, 1)

        def pt_hi_part(u):
            act.wait_ge(pt_done, u + 1)
            if u >= 2:
                act.wait_ge(pv_done, u - 1)
            n = (u // (2 * H) + 1) * P
            sc.activation(pt_hi[u % 2][:, 0:n], turned_bank(u)[:, 0:n], ACT.Copy).then_inc(pt_hi_done, 1)

        q_hi_part(0)
        def z_lru(ct):
            z_wait(act, T + ct)
            act.wait_ge(one_less_a2, 1)
            if ct >= 2:
                act.wait_ge(yl_full, ct - 1)
            sc.activation(lru_x[:, 1 + ct % 2, 0:S], bank(ct % 2), ACT.Tanh, scale=0.5).then_inc(zl_tanh, 1)

        def yl_hi_part(ct):
            act.wait_ge(yl_full, ct + 1)
            act.wait_ge(lru_ss, 1)
            sc.activation(yl_hi[:, ct, :], lru_h[:, ct, :], ACT.Copy).then_inc(yl_hi_ready, 1)

        def z_nsa(t):
            z_wait(act, t)
            act.wait_ge(lru_h_ready, CT)
            sc.activation(z_silu[:, t, :], bank(t % 2), ACT.Tanh, scale=0.5).then_inc(zn_tanh, 1)

        def o_squares(t):
            act.wait_ge(o_added, 4 * (t + 1))
            if t >= 1:
                act.wait_ge(n_sq, t)
            sc.activation(o_sq[:], qn[:, t, :], ACT.Square, accum_out=ss_n[:, t:t + 1]).then_inc(n_sq, 1)

        def yn_hi_part(t):
            act.wait_ge(yt_mm, t + 1)
            for ct in range(CT):
                sc.activation(yn_hi[:, ct, t * P:(t + 1) * P], bank(6)[:, ct * P:(ct + 1) * P], ACT.Identity,
                              scale=gn_half[:, ct:ct + 1]).then_inc(yn_hi_done, 1)

        z_nsa(0)
        cmp_exp(0)
        for u in range(UNITS + 2):
            i, r = u // (2 * H), u % (2 * H)
            if u >= 2:
                pt_hi_part(u - 2)
            if u < UNITS:
                prob(u)
            if u in HI_AT:
                hi(HI_AT[u])
            if u == 1:
                cmp_pt(0)
            if i + 1 < T and u < UNITS:
                if r == AT_Q_HI:
                    q_hi_part(i + 1)
                if r == AT_C_EXP:
                    cmp_exp(i + 1)
                if r == AT_C_PT:
                    cmp_pt(i + 1)
            if u in ZN_AT:
                z_nsa(ZN_AT.index(u))
            if u in ZL_AT:
                z_lru(ZL_AT.index(u))
            if u - 2 in ZL_AT:
                yl_hi_part(ZL_AT.index(u - 2))
            if u in SQ_AT:
                o_squares(SQ_AT.index(u))
            if u - 2 in Y_AT:
                yn_hi_part(Y_AT.index(u - 2))
        yn_hi_part(T - 1)
        o_squares(T - 1)

    def dve_program(dve):
        v = nc.vector
        n_link = [0]

        def link(ins):
            n_link[0] += 1
            ins.then_inc(dchain, 1)
            dve.wait_ge(dchain, n_link[0])

        def rsqrt(dst, src, tmp):
            link(v.tensor_scalar(tmp.bitcast(I32), src.bitcast(I32), 1, None, ALU.logical_shift_right))
            link(v.tensor_scalar(dst.bitcast(I32), tmp.bitcast(I32), -1.0, MAGIC, ALU.mult, ALU.add))
            for _ in range(3):
                link(v.tensor_tensor(tmp, dst, dst, ALU.mult))
                link(v.scalar_tensor_tensor(out=tmp, in0=tmp, scalar=-0.5, in1=src, op0=ALU.mult, op1=ALU.mult))
                link(v.scalar_tensor_tensor(out=dst, in0=tmp, scalar=1.5, in1=dst, op0=ALU.add, op1=ALU.mult))

        link(v.memset(ones[:], 1.0))
        link(v.memset(kc_st[:].bitcast(F32), 0.0))
        link(v.memset(gl_g[:], 0.0))
        dve.wait_ge(c_tanh, 1)
        link(v.scalar_tensor_tensor(out=c_silu[:], in0=c_t[:], scalar=1.0, in1=c_col[:], op0=ALU.add, op1=ALU.mult))
        v.tensor_scalar(c_silu[:], c_silu[:], 0.5, None, ALU.mult).then_inc(c_ready, 1)

        def ada_acc(k):
            r = raw_of(("ada", k))
            for half in range(2):
                if half == 0:
                    dve.wait_ge(shift_in[k % RAW], 16 * (k // RAW + 1))
                    if k >= 1:
                        dve.wait_ge(ada_used, k)
                else:
                    item_wait(dve, ("ada", k))
                m, w = [a[:, half * D:(half + 1) * D] for a in (macc, r)]
                if k == 0 and half == 0:
                    dve.wait_ge(c_ready, 1)
                if k == 0:
                    ins = v.tensor_scalar(m, w, c_silu[:, k:k + 1], None, ALU.mult)
                else:
                    ins = v.scalar_tensor_tensor(out=m, in0=w, scalar=c_silu[:, k:k + 1], in1=m, op0=ALU.mult, op1=ALU.add)
                if half == 1:
                    ins.then_inc(ada_used, 1)
                elif k == KC - 1:
                    ins.then_inc(shift_acc, 1)

        ada_acc(0)
        dve.wait_ge(ssx_ready, T)
        link(v.tensor_scalar(ss_x[:], ss_x[:], 1.0 / D, EPS, ALU.mult, ALU.add))
        rsqrt(rs_x[:], ss_x[:], nt1[:, 0:T])
        v.tensor_copy(rs_x[:], rs_x[:]).then_inc(rsx_ready, 1)
        ada_acc(1)
        ada_acc(2)
        dve.wait_ge(cols_done, 1)
        v.tensor_copy(cols_a[:].rearrange("p c r -> p (c r)"), bank(5)[:, 0:CT * ROWS]).then_inc(dchain, 1)
        n_link[0] += 1
        link(v.tensor_copy(cols_b[:], bank(5)[:, CT * ROWS:CT * ROWS + QROWS]))
        lam = cols_a[:, :, R_LAM]
        v.scalar_tensor_tensor(out=lam_abs[:], in0=lam, scalar=-1.0, in1=lam, op0=ALU.mult, op1=ALU.max).then_inc(lam_ready, 1)
        for k in range(3, KC):
            ada_acc(k)
        for b in range(4):
            dve.wait_ge(ada_mm, b + 1)
            v.tensor_reduce(msum[:, 4 * b:4 * b + 4], bank(4 + b).rearrange("p (j n) -> p j n", j=4), AX.X, ALU.add).then_inc(ada_sum, 1)
        dve.wait_ge(ada_sum, 4)
        dve.wait_ge(small_in, 32)
        link(v.tensor_tensor(mod[:], msum[:].rearrange("p (s k) -> p s k", s=2), b_mod[:], ALU.add))
        v.scalar_tensor_tensor(out=s1[:], in0=mod[:, 1, :], scalar=1.0, in1=ng_col[:], op0=ALU.add, op1=ALU.mult).then_inc(s1_ready, 1)
        dve.wait_ge(s1_ready, 1)
        dve.wait_ge(xt_ready, 2 * T)

        def h_lo_part(k):
            dve.wait_ge(h_hi_ready, k + 1)
            v.tensor_tensor(h_lo[:, k, :], h_f[:, k, :], h_hi[:, k, :].bitcast(F32), ALU.subtract).then_inc(h_ready, 1)

        for k in range(KC):
            v.tensor_scalar(h_f[:, k, :], xT[:, k, :], s1[:, k:k + 1], mod[:, 0, k:k + 1], ALU.mult, ALU.add).then_inc(h_full, 1)
            dve.wait_ge(h_full, k + 1)
            h_lo_part(k)
        dve.wait_ge(h_ready, KC)
        dve.wait_ge(lam_exp, 1)
        link(v.tensor_scalar(lam_s[:], lam_e[:], 2.0, None, ALU.add))
        link(v.reciprocal(lam_s[:], lam_s[:]))
        link(v.tensor_tensor(lam_s[:], lam_s[:], lam_e[:], ALU.mult))
        link(v.tensor_tensor(lam_2[:], lam_s[:], lam_s[:], ALU.mult))
        link(v.tensor_scalar(sp[:], lam_2[:], 1.0 / 15, None, ALU.mult))
        for odd in (13, 11, 9, 7, 5, 3):
            link(v.scalar_tensor_tensor(out=sp[:], in0=sp[:], scalar=1.0 / odd, in1=lam_2[:], op0=ALU.add, op1=ALU.mult))
        link(v.scalar_tensor_tensor(out=sp[:], in0=sp[:], scalar=1.0, in1=lam_s[:], op0=ALU.add, op1=ALU.mult))
        link(v.tensor_scalar(lam_2[:], lam, -1.0, 0.0, ALU.mult, ALU.max))
        link(v.scalar_tensor_tensor(out=sp[:], in0=sp[:], scalar=2.0, in1=lam_2[:], op0=ALU.mult, op1=ALU.add))
        link(v.tensor_scalar(p4sp[:], sp[:], LRU_C / 2, None, ALU.mult))
        link(v.tensor_scalar(n4sp[:], sp[:], -LRU_C / 2, None, ALU.mult))
        for m, r in enumerate((R_BA, R_BX)):
            link(v.tensor_scalar(hb[:, m, :], cols_a[:, :, r], 0.5, None, ALU.mult))
        link(v.tensor_scalar(gl_half[:], cols_a[:, :, R_GL], 0.5, None, ALU.mult))
        link(v.tensor_scalar(gn_half[:], cols_a[:, :, R_GN], 0.5, None, ALU.mult))
        for b, r in enumerate((Q_GS, Q_GW, Q_GC)):
            ins = v.scalar_tensor_tensor(out=gk[:, b:b + 1], in0=cols_b[:, Q_GQ:Q_GQ + 1], scalar=SCALE,
                                         in1=cols_b[:, r:r + 1], op0=ALU.mult, op1=ALU.mult)
            if b == 2:
                ins.then_inc(cols_ready, 1)
            else:
                link(ins)
        v.memset(lru_x[:, :, 0:3], 0.0).then_inc(dchain, 1)
        n_link[0] += 1

        def gate_acc(n):
            item_wait(dve, ("gate", n))
            r = raw_of(("gate", n))[:].rearrange("p (k n) -> p k n", k=2)
            for j in range(2):
                k = 2 * n + j
                if k == 0:
                    dve.wait_ge(bg_in, 16)
                ins = v.scalar_tensor_tensor(out=gacc[:], in0=r[:, j, :], scalar=c_silu[:, k:k + 1], in1=gacc[:],
                                             op0=ALU.mult, op1=ALU.add)
                if j == 0:
                    link(ins)
                else:
                    ins.then_inc(gate_used, 1)
            dve.wait_ge(gate_used, n + 1)

        gate_acc(0)
        for ct in range(CT):
            dve.wait_ge(lru_x_ready, ct + 1)
            if ct == 0:
                dve.wait_ge(dchain, n_link[0])
            link(v.tensor_scalar(lru_h[:, ct, :], lru_x[:, ct, 0:S], cols_a[:, ct, R_CW:R_CW + 1],
                                 cols_a[:, ct, R_CB:R_CB + 1], ALU.mult, ALU.add))
            for i in range(1, TAPS):
                ins = v.scalar_tensor_tensor(out=lru_h[:, ct, :], in0=lru_x[:, ct, i:i + S],
                                             scalar=cols_a[:, ct, R_CW + i:R_CW + i + 1], in1=lru_h[:, ct, :],
                                             op0=ALU.mult, op1=ALU.add)
                if i == TAPS - 1:
                    ins.then_inc(xc_ready, 1)
                else:
                    link(ins)

        def cmp_stack(w):
            dve.wait_ge(piece_done, PC + 1)
            for kv in range(KV):
                for par in range(2):
                    for var in range(2):
                        src = ps[kv * HD:kv * HD + HD, 4 + w, :].rearrange("p (c j e) -> p e j c", j=8, e=2)[:, par]
                        q0 = (Q_POSK, Q_POSV)[w] + 8 * var
                        pos = cols_b[par * HD:par * HD + HD, q0:q0 + 8].unsqueeze(2).broadcast_to([HD, 8, CW])
                        ins = v.tensor_tensor(cmp_x[w][par * HD:par * HD + HD, var, :, kv, :], src, pos, ALU.add)
                        ins.then_inc(cx_ready, 1)

        cmp_stack(0)
        cmp_stack(1)
        gate_acc(1)

        def gelu_dve(w):
            hid = bank((6, 2)[w])[:, 0:4 * CW].rearrange("p (m n) -> p m n", m=2)[:, :, 0:2 * NCMP]
            q = gl_q[:, :, 0:2 * NCMP]
            dve.wait_ge(gl_sq, w + 1)
            link(v.tensor_scalar(q, q, GELU_B, 1.0, ALU.mult, ALU.add))
            v.tensor_tensor(q, hid, q, ALU.mult).then_inc(gl_poly, 1)
            dve.wait_ge(gl_tanh, w + 1)
            if w == 0:
                o, i0, i1 = gl_g[:, :, 0:2 * NCMP], q, hid
                v.scalar_tensor_tensor(out=o, in0=i0, scalar=1.0, in1=i1, op0=ALU.add, op1=ALU.mult).then_inc(gl_ready, 1)
            else:
                link(v.memset(gl_g[:], 0.0))
                for m in range(2):
                    o = gl_g[:, m, :].rearrange("p (k n) -> p k n", k=KV)[:, :, 0:NCMP]
                    i0 = gl_q[:, m, 0:2 * NCMP].rearrange("p (k n) -> p k n", k=KV)
                    i1 = hid[:, m, :].rearrange("p (k n) -> p k n", k=KV)
                    ins = v.scalar_tensor_tensor(out=o, in0=i0, scalar=1.0, in1=i1, op0=ALU.add, op1=ALU.mult)
                    if m == 0:
                        link(ins)
                    else:
                        ins.then_inc(gl_ready, 1)

        gelu_dve(0)
        gate_acc(2)
        dve.wait_ge(kc_ss, 1)
        ms, kr = gl_r[:, 0:2 * NCMP], gl_q[:, 0, 0:2 * NCMP]
        link(v.tensor_scalar(ms, bank(6)[:, 64:64 + 2 * NCMP], 1.0 / P, EPS, ALU.mult, ALU.add))
        rsqrt(kr, ms, nt1[:, 0:2 * NCMP])
        link(v.tensor_scalar(kr, kr, 0.5, None, ALU.mult))
        kc = gl_t[:, 0:2 * NCMP]
        v.scalar_tensor_tensor(out=kc, in0=bank(6)[:, 0:2 * NCMP], scalar=gk[:, 2:3], in1=kr, op0=ALU.mult,
                               op1=ALU.mult).then_inc(kc_full, 1)
        dve.wait_ge(kc_hi, 1)
        v.tensor_tensor(kc_st[:, :, 1, 0:NCMP], kc.rearrange("p (k n) -> p k n", k=KV),
                        kc_st[:, :, 0, 0:NCMP].bitcast(F32), ALU.subtract).then_inc(kc_ready, 1)
        for t0, t1 in ((0, T - 1), (T - 1, T)):
            for t in range(t0, t1):
                dve.wait_ge(kv_sq, t + 1)
                v.tensor_reduce(ss_k[:, t, :], sq[t % 2][:, 0:256].rearrange("p (n d) -> p n d", d=HD), AX.X, ALU.add).then_inc(k_sum, 1)
            dve.wait_ge(k_sum, t1)
            ms, rs = [a[:, t0:t1, :].rearrange("p t n -> p (t n)") for a in (ss_k, rs_k)]
            link(v.tensor_scalar(ms, ms, 1.0 / HD, EPS, ALU.mult, ALU.add))
            rsqrt(rs, ms, nt1[:, 0:4 * (t1 - t0)])
            for t in range(t0, t1):
                row = bank(t).rearrange("p (b s n) -> p b s n", b=2, s=2)
                dve.wait_ge(v_hi, 2 * (t + 1))
                for b in range(2):
                    v.tensor_tensor(kn[:, t, b * P:(b + 1) * P].rearrange("p (k d) -> p k d", k=KV),
                                    row[:, b, 0, :].rearrange("p (k d) -> p k d", k=KV),
                                    rs_k[:, t, 2 * b:2 * b + 2].unsqueeze(2).broadcast_to([P, KV, HD]), ALU.mult).then_inc(kn_ready, 1)
                for b in range(2):
                    v.tensor_tensor(v_hl[:, b, :, t, HD:P], row[:, b, 1, :].rearrange("p (k d) -> p k d", k=KV),
                                    v_hl[:, b, :, t, 0:HD].bitcast(F32), ALU.subtract).then_inc(v_ready, 1)
        dve.wait_ge(g24_tanh, 1)
        v.tensor_scalar(gates[:], gates[:], 0.5, 0.5, ALU.mult, ALU.add).then_inc(gates_ready, 1)
        gate_acc(3)
        dve.wait_ge(rg_tanh, 2 * CT)
        v.scalar_tensor_tensor(out=lru_h[:], in0=lru_d[:], scalar=1.0, in1=lru_h[:], op0=ALU.add, op1=ALU.mult).then_inc(ix_ready, 1)
        for b in range(2):
            for kv in range(KV):
                a = kv * HD
                dve.wait_ge(k_hi, 2 * b + kv + 1)
                v.scalar_tensor_tensor(out=k_st[a:a + HD, b, kv, 1, :], in0=ps[a:a + HD, b, :], scalar=gk[a:a + HD, b:b + 1],
                                       in1=k_st[a:a + HD, b, kv, 0, :].bitcast(F32), op0=ALU.mult, op1=ALU.subtract).then_inc(k_lo, 1)
        dve.wait_ge(bias_d, 2)
        for h in range(H - 1, 0, -1):
            v.tensor_scalar(bias[:, h, :], bias[:, 0, :], SLOPES[h], None, ALU.mult).then_inc(bias_h, 1)
            v.tensor_scalar(bias_c[:, h, :], bias_c[:, 0, :], SLOPES[h], None, ALU.mult).then_inc(bias_h, 1)
        v.tensor_scalar(bias[:, 0, :], bias[:, 0, :], SLOPES[0], None, ALU.mult).then_inc(bias_s, 1)
        v.tensor_scalar(bias_c[:, 0, :], bias_c[:, 0, :], SLOPES[0], None, ALU.mult).then_inc(bias_s, 1)
        gelu_dve(1)
        dve.wait_ge(a_ready, 3 * CT)
        v.scalar_tensor_tensor(out=lru_c[:], in0=lru_c[:], scalar=1.0, in1=lru_x[:, :, 0:S], op0=ALU.add, op1=ALU.mult).then_inc(one_less_a2, 1)
        for t in range(T):
            dve.wait_ge(q_sq, t + 1)
            v.tensor_reduce(ss_q[:, t, :], sq[t % 2][:].rearrange("p (n d) -> p n d", d=HD), AX.X, ALU.add).then_inc(q_sum, 1)
        dve.wait_ge(q_sum, T)
        link(v.tensor_scalar(ss_q[:], ss_q[:], 1.0 / HD, EPS, ALU.mult, ALU.add))
        rsqrt(rs_q[:].rearrange("p t n -> p (t n)"), ss_q[:].rearrange("p t n -> p (t n)"), nt1[:, 0:H * T])
        for t in range(T):
            v.tensor_tensor(qn[:, t, :].rearrange("p (n d) -> p n d", d=HD), bank(4 + t).rearrange("p (n d) -> p n d", d=HD),
                            rs_q[:, t, :].unsqueeze(2).broadcast_to([P, H, HD]), ALU.mult).then_inc(qn_ready, 1)
        dve.wait_ge(sqrt_ready, 1)
        v.tensor_tensor(lru_c[:], lru_c[:], lru_h[:], ALU.mult).then_inc(lru_in, 1)

        def recurrence():
            dve.wait_ge(lru_in, 1)
            for ct in range(CT):
                v.tensor_tensor_scan(lru_h[:, ct, :], lru_d[:, ct, :], lru_c[:, ct, :], 0.0, ALU.mult, ALU.add).then_inc(lru_h_ready, 1)

        def value_blocks():
            dve.wait_ge(vblk_clear, 1)
            dve.wait_ge(cw2_mm, 2)
            for kv in range(KV):
                for g in range(G):
                    v.tensor_scalar(v_blk[g * CW:(g + 1) * CW, kv, g * HD:(g + 1) * HD],
                                    ps[g * CW:(g + 1) * CW, 3, kv * HD:(kv + 1) * HD], 0.5, None, ALU.mult).then_inc(vc_ready, 1)

        def q_lo_part(i):
            src = bank(6).rearrange("p (a n) -> p a n", a=H // 2)
            for e in range(2):
                dve.wait_ge(q_hi, 2 * i + e + 1)
                o = 1 - e
                v.tensor_tensor(q_st[i % 2][o * HD:o * HD + HD, e:H:2, :], src[e * HD:e * HD + HD],
                                q_st[i % 2][e * HD:e * HD + HD, e:H:2, :].bitcast(F32), ALU.subtract).then_inc(q_st_ready, 1)

        def cmp_soft(i):
            dve.wait_ge(cs_mm, i + 1)
            if i >= 1:
                dve.wait_ge(ct_mm, i)
            dve.wait_ge(bias_m_ready, i + 1)
            src = bank(6).rearrange("p (h s n) -> p h s n", h=H, s=2)
            link(v.tensor_tensor(c_s[:], src[:, :, 1, :], bias_m[:], ALU.add))
            v.tensor_tensor(c_s[:], src[:, :, 0, :], c_s[:], ALU.add).then_inc(cs_biased, 1)

        def cmp_max(i):
            dve.wait_ge(cs_biased, i + 1)
            link(v.tensor_reduce(c_max[:], c_s[:], AX.X, ALU.max))
            v.tensor_tensor(c_s[:], c_s[:], c_max[:].unsqueeze(2).broadcast_to([P, H, CW]), ALU.subtract).then_inc(cs_sub, 1)

        def cmp_factor(i):
            dve.wait_ge(cp_ready, i + 1)
            link(v.tensor_reduce(c_den[:], c_s[:], AX.X, ALU.add))
            link(v.reciprocal(c_den[:], c_den[:]))
            link(v.tensor_tensor(c_f[:], c_den[:], gates[:, i, 0:H], ALU.mult))
            if i == 0:
                link(v.tensor_scalar(c_f[:], c_f[:], valid[:, 0:1], None, ALU.mult))

        def cmp_out(i):
            dve.wait_ge(cpv_mm, i + 1)
            v.tensor_tensor(qn[:, i, :].rearrange("p (n d) -> p n d", d=HD), bank(6).rearrange("p (n d) -> p n d", d=HD),
                            c_f[:].unsqueeze(2).broadcast_to([P, H, HD]), ALU.mult).then_inc(o_init, 1)

        def add_bias(u):
            i, h = u // (2 * H), u % H
            n = (i + 1) * P
            dve.wait_ge(scores_done, u + 1)
            if u >= 3:
                dve.wait_ge(pt_done, u - 2)
            v.tensor_tensor_reduce(out=sc_sb[u % 3][:, 0:n], in0=score_bank(u)[:, 0:n], in1=bias[:, h, S - n:S], scale=-1.0,
                                   scalar=3e38, op0=ALU.add, op1=ALU.min, accum_out=negmax[:, u:u + 1]).then_inc(biased, 1)

        def pt_lo_part(u):
            n = (u // (2 * H) + 1) * P
            dve.wait_ge(pt_hi_done, u + 1)
            if u >= 2:
                dve.wait_ge(pv_done, u - 1)
            v.tensor_tensor(pt_lo[u % 2][:, 0:n], turned_bank(u)[:, 0:n], pt_hi[u % 2][:, 0:n].bitcast(F32),
                            ALU.subtract).then_inc(pt_lo_done, 1)

        def out_factor(grp):
            i, b, kv = grp // 4, grp % 4 // 2, grp % 2
            dve.wait_ge(probs, 4 * grp + 4)
            f = f_u[:, grp % 4, :]
            link(v.reciprocal(f, den[:, 4 * grp:4 * grp + 4]))
            link(v.tensor_tensor(f, f, gates[:, i, (1 + b) * H + kv * G:(1 + b) * H + kv * G + G], ALU.mult))

        def scale_out(grp):
            dve.wait_ge(pv_done, 4 * grp + 4)
            if grp >= 2:
                dve.wait_ge(o_added, grp - 1)
            v.tensor_tensor(xo[grp % 2][:], bank(7).rearrange("p (g n) -> p g n", g=G),
                            f_u[:, grp % 4, :].unsqueeze(2).broadcast_to([P, G, P]), ALU.mult).then_inc(o_scaled, 1)

        dve.wait_ge(gates_ready, 1)
        q_lo_part(0)
        recurrence()
        dve.wait_ge(bias_ready, 1)
        cmp_soft(0)
        cmp_max(0)
        value_blocks()

        def z_lru(ct):
            dve.wait_ge(zl_tanh, ct + 1)
            dve.wait_ge(lru_sq, 1)
            tz = lru_x[:, 1 + ct % 2, 0:S]
            link(v.scalar_tensor_tensor(out=tz, in0=tz, scalar=1.0, in1=bank(ct % 2), op0=ALU.add, op1=ALU.mult))
            v.scalar_tensor_tensor(out=lru_h[:, ct, :], in0=tz, scalar=gl_half[:, ct:ct + 1], in1=lru_h[:, ct, :],
                                   op0=ALU.mult, op1=ALU.mult).then_inc(yl_full, 1)

        def yl_lo_dve(ct):
            dve.wait_ge(yl_hi_ready, ct + 1)
            v.tensor_tensor(yl_lo[:, ct, :], lru_h[:, ct, :], yl_hi[:, ct, :].bitcast(F32), ALU.subtract).then_inc(yl_ready, 1)

        def z_nsa(t):
            dve.wait_ge(zn_tanh, t + 1)
            v.scalar_tensor_tensor(out=z_silu[:, t, :], in0=z_silu[:, t, :], scalar=1.0, in1=bank(t % 2), op0=ALU.add,
                                   op1=ALU.mult).then_inc(zn_ready, 1)

        def part_out(n):
            half, t = n // T, n % T
            dve.wait_ge(part_mm, n + 1)
            dve.wait_ge(gate_bc, 2)
            v.scalar_tensor_tensor(out=part[:, n, :], in0=bank(n % 2), scalar=rs_l[:, t:t + 1],
                                   in1=g_bc[:, half * 512:half * 512 + 512], op0=ALU.mult, op1=ALU.mult).then_inc(part_ready, 1)

        def y_rows(t):
            dve.wait_ge(o_added, 4 * (t + 1))
            dve.wait_ge(zn_ready, t + 1)
            v.tensor_tensor(z_silu[:, t, :], qn[:, t, :], z_silu[:, t, :], ALU.mult).then_inc(y_ready, 1)

        def rms_n(t0, t1):
            dve.wait_ge(n_sq, t1)
            link(v.tensor_scalar(ss_n[:, t0:t1], ss_n[:, t0:t1], 1.0 / S, EPS, ALU.mult, ALU.add))
            rsqrt(rs_n[:, t0:t1], ss_n[:, t0:t1], nt1[:, 0:t1 - t0])

        def final(n):
            half, t = OUT_ORDER[n]
            dve.wait_ge(out_mm, n + 1)
            if n == 0:
                dve.wait_ge(probs, UNITS)
                dve.wait_ge(pt_done, UNITS)
            if n >= 2:
                dve.wait_ge(out_added, n - 1)
            v.scalar_tensor_tensor(out=tail[n % 2][:], in0=bank(OUT_BANKS[n]), scalar=rs_n[:, t:t + 1],
                                   in1=g_bc[:, half * 512:half * 512 + 512], op0=ALU.mult, op1=ALU.mult).then_inc(out_gated, 1)
            dve.wait_ge(out_gated, n + 1)
            dve.wait_ge(res_added, n + 1)
            o = part[:, half * T + t, :]
            v.tensor_tensor(o, o, tail[n % 2][:], ALU.add).then_inc(out_added, 1)

        def yn_lo_part(t):
            dve.wait_ge(yn_hi_done, CT * (t + 1))
            for ct in range(CT):
                v.scalar_tensor_tensor(out=yn_lo[:, ct, t * P:(t + 1) * P], in0=bank(6)[:, ct * P:(ct + 1) * P],
                                       scalar=gn_half[:, ct:ct + 1], in1=yn_hi[:, ct, t * P:(t + 1) * P].bitcast(F32),
                                       op0=ALU.mult, op1=ALU.subtract).then_inc(yn_ready, 1)

        for u in range(UNITS + 4):
            i, r = u // (2 * H), u % (2 * H)
            if u < UNITS:
                add_bias(u)
            if 3 <= u < UNITS + 3:
                pt_lo_part(u - 3)
            if u >= 6 and (u - 6) % 4 == 0:
                out_factor((u - 6) // 4)
            if u >= 7 and (u - 7) % 4 == 0:
                scale_out((u - 7) // 4)
            if u == LSS_AT + 1:
                dve.wait_ge(lru_ss, 1)
                v.tensor_scalar(ss_l[:], bank(6)[:, 0:T], 1.0 / LRU, EPS, ALU.mult, ALU.add).then_inc(ssl_ready, 1)
            if u == RSL_AT:
                dve.wait_ge(ssl_ready, 1)
                rsqrt(rs_l[:], ss_l[:], nt1[:, 0:T])
            if u == 0:
                z_nsa(0)
                cmp_factor(0)
            if u == 3:
                cmp_out(0)
            if i + 1 < T and u < UNITS:
                if r == AT_Q_LO:
                    q_lo_part(i + 1)
                if r == AT_C_SOFT:
                    cmp_soft(i + 1)
                if r == AT_C_MAX:
                    cmp_max(i + 1)
                if r == AT_C_FACTOR:
                    cmp_factor(i + 1)
                if r == AT_C_OUT:
                    cmp_out(i + 1)
            if u >= 1 and u - 1 in ZN_AT:
                z_nsa(ZN_AT.index(u - 1))
            if u - 1 in ZL_AT:
                z_lru(ZL_AT.index(u - 1))
            if u - 3 in ZL_AT:
                yl_lo_dve(ZL_AT.index(u - 3))
            if u in PART_AT:
                part_out(PART_AT.index(u))
            if u in Y_AT:
                y_rows(Y_AT.index(u))
            if u - 3 in Y_AT:
                yn_lo_part(Y_AT.index(u - 3))
            if u == UNITS + 3:
                rms_n(0, T - 1)
        y_rows(T - 1)
        final(0)
        final(1)
        yn_lo_part(T - 1)
        rms_n(T - 1, T)
        for n in range(2, 2 * T):
            final(n)

    def pe_program(pe):
        mm = nc.tensor.matmul
        tr = nc.tensor.transpose

        pe.wait_ge(rows_in, 16 * 13)
        pe.wait_ge(pool_setup, 1)
        for ct in range(CT):
            tr(bank(5)[:, ct * ROWS:(ct + 1) * ROWS], rows_a[:, ct * P:(ct + 1) * P], ident[0:ROWS, 0:ROWS])
        tr(bank(5)[:, CT * ROWS:CT * ROWS + QROWS], rows_b[:], ident[0:QROWS, 0:QROWS]).then_inc(cols_done, 1)

        for n in range(2 * T):
            t, j = n // 2, n % 2
            pe.wait_ge(xn_ready, t + 1)
            if n >= 4:
                pe.wait_ge(xt_ready, n - 3)
            for q in range(4):
                k = 4 * j + q
                last = tr(bank(n % 4)[:, q * P:(q + 1) * P], xn[:, t, k:D:KC], ident[:])
            last.then_inc(xt_psum, 1)

        def keep_warm(n):
            for _ in range(n):
                mm(bank(0)[:, 0:P], ident[:], ident[:], start=True, stop=True)

        pe.wait_ge(xt_ready, 2 * T)
        pe.wait_ge(ada_used, 5)
        keep_warm(8)
        pe.wait_ge(shift_acc, 1)
        for j in range(2 * KC):
            if j == KC:
                pe.wait_ge(ada_used, KC)
            sh, kk = j // KC, j % KC
            ins = tr(bank(4 + j // 4)[:, j % 4 * P:(j % 4 + 1) * P], macc[:, sh * D + kk:(sh + 1) * D:KC], ident[:])
            if j % 4 == 3:
                ins.then_inc(ada_mm, 1)

        def piece_in(p):
            pe.wait_ge(lo_done, p + 1)

        def triple(p, kk, b, k, acts, cols, first, last, weights_still, rows=None):
            wh, wl = wv(w_hi[p % HL], p)[:, kk, :], wv(w_lo[p % HL], p)[:, kk, :]
            a_hi, a_lo = acts
            j = cols
            dst = bank(b)
            if weights_still:
                a, bb = (wh[:, j * P:(j + 1) * P], wl[:, j * P:(j + 1) * P]), (a_hi, a_lo)
                pairs = ((a[1], bb[0]), (a[0], bb[1]), (a[0], bb[0]))
            else:
                pairs = ((a_lo[:, j * P:(j + 1) * P], wh), (a_hi[:, j * P:(j + 1) * P], wl), (a_hi[:, j * P:(j + 1) * P], wh))
            for n, (l, r) in enumerate(pairs):
                ins = mm(dst, l, r, start=(first and n == 0), stop=(last and n == 2))
            return ins

        def group_step(p0, j, banks, weights_still, n_tiles=4, n_k=4):
            k, b = j // n_tiles, j % n_tiles
            if j >= 16:
                k, b = 4 + j % 4, j // 4 - 4
            p, kk = p0 + k // n_k, k % n_k
            if j % (n_tiles * n_k) == 0 and p > 0 or j == 8 and p == 0:
                piece_in(p)
            ins = triple(p, kk, banks[b], k, (h_hi[:, k, :], h_lo[:, k, :]), b, k == 0, k == KC - 1, weights_still)
            if j % (n_tiles * n_k) == n_tiles * n_k - 1:
                ins.then_inc(piece_done, 1)
            elif j >= 16 and k == KC - 1:
                ins.then_inc(tile_done, 1)

        keep_warm(8)
        wh, wl = wv(w_hi[0], 0)[:, 0, :], wv(w_lo[0], 0)[:, 0, :]
        pe.wait_ge(hi_first, 1)
        pe.wait_ge(h_hi_ready, 1)
        for b in range(4):
            mm(bank(b), wh[:, b * P:(b + 1) * P], h_hi[:, 0, :], start=True, stop=False)
        pe.wait_ge(h_ready, 1)
        for b in range(4):
            mm(bank(b), wh[:, b * P:(b + 1) * P], h_lo[:, 0, :], start=False, stop=False)
        pe.wait_ge(lo_first, 1)
        for b in range(4):
            mm(bank(b), wl[:, b * P:(b + 1) * P], h_hi[:, 0, :], start=False, stop=False)
        for j in range(4, 32):
            if j % 4 == 0 and j <= 16:
                pe.wait_ge(h_ready, j // 4 + 1 if j < 16 else KC)
            group_step(PX, j, (0, 1, 2, 3), True)
        pe.wait_ge(w24_ready, 1)
        for k in range(KC):
            for n, a in enumerate((h_lo, h_hi)):
                last = mm(ps[0:2 * NG, 7, :], w24_hl[:, k, :], a[:, k, :], start=(k == 0 and n == 0), stop=(k == KC - 1 and n == 1))
        last.then_inc(g24_done, 1)
        for j in range(16):
            group_step(PC, j, (4, 5), True, 2, 8)

        pe.wait_ge(g24_out, 1)
        pe.wait_ge(pair_ready, 1)
        for t in range(T):
            last = mm(bank(7)[:, t * NG:(t + 1) * NG], g24_t[:, t * P:(t + 1) * P], pair[:], start=True, stop=True)
        last.then_inc(g24_turned, 1)

        def kv_steps(a, b):
            for j in range(a, b):
                if j == 0:
                    pe.wait_ge(lru_x_ready, CT)
                group_step(PKV, j, (0, 1, 2, 3), False)

        def cmp_hidden(w, b):
            pe.wait_ge(w1_in, 16 * (w + 1))
            pe.wait_ge(cx_ready, 8 * (w + 1))
            for m in range(2):
                for j in range(16):
                    var, j8 = j // 8, j % 8
                    last = mm(bank(b)[:, m * 2 * CW:m * 2 * CW + 2 * NCMP], w1[:, j, m * P:(m + 1) * P],
                              cmp_x[w][:, var, j8, :, var:var + NCMP], start=(j == 0), stop=(j == 15))
            last.then_inc(hid_mm, 1)

        kv_steps(0, 16)
        cmp_hidden(0, 6)
        kv_steps(16, 22)
        pe.wait_ge(gl_ready, 1)
        pe.wait_ge(w2_in, 48)
        for m in range(2):
            last = mm(bank(6)[:, 0:2 * NCMP], w2k[:, m, :], gl_g[:, m, 0:2 * NCMP], start=(m == 0), stop=(m == 1))
        last.then_inc(cw2_mm, 1)
        kv_steps(22, 25)
        pe.wait_ge(kc_sq, 1)
        mm(bank(6)[:, 64:64 + 2 * NCMP], ones[:], gl_t[:, 0:2 * NCMP], start=True, stop=True).then_inc(kc_ss, 1)
        kv_steps(25, 32)
        pe.wait_ge(cx_ready, 16)
        pe.wait_ge(g24_tanh, 1)
        pe.wait_ge(kc_full, 1)
        pe.wait_ge(kc_hi, 1)
        for j in range(16):
            group_step(PQ, j, (4, 5, 6, 7), False)
        pe.wait_ge(xc_ready, CT)
        pe.wait_ge(bd_in, 64)
        pe.wait_ge(v_ready, 2 * T)
        for ct in range(CT):
            for m in range(2):
                if ct >= 2:
                    pe.wait_ge(rg_tanh, 2 * (ct - 2) + m + 1)
                mm(bank(ct % 2 * 2 + m), bd[:, m, ct, :], lru_h[:, ct, :], start=True, stop=True).then_inc(rg_mm, 1)
        for b in range(2):
            pe.wait_ge(rg_tanh, 2 * (CT - 2) + b + 1)
            for t in range(T):
                pe.wait_ge(kn_ready, 2 * (t + 1))
                last = tr(bank(b)[:, t * P:(t + 1) * P], kn[:, t, b * P:(b + 1) * P], ident[:])
            last.then_inc(kt_mm, 1)
        pe.wait_ge(rg_tanh, 2 * CT)
        cmp_hidden(1, 2)
        for j in range(16, 32):
            group_step(PQ, j, (4, 5, 6, 7), False)

        def value_weights():
            pe.wait_ge(gl_ready, 2)
            for g in range(G):
                for kv in range(KV):
                    for m in range(2):
                        last = mm(ps[g * CW:(g + 1) * CW, 3, kv * HD:(kv + 1) * HD], gl_g[:, m, kv * CW:(kv + 1) * CW],
                                  w2v[:, m, :], start=(m == 0), stop=(m == 1))
            last.then_inc(cw2_mm, 1)

        def lru_squares():
            pe.wait_ge(lru_sum, 2)
            pe.wait_ge(o_init, 1)
            for t in range(T):
                last = mm(bank(6)[:, t:t + 1], lru_c[:, 0, t * P:(t + 1) * P], ones[:, 0:1], start=True, stop=True)
            last.then_inc(lru_ss, 1)

        def q_turn(i):
            pe.wait_ge(qn_ready, 3)
            if i >= 1:
                pe.wait_ge(o_init, i)
            if i == 1:
                pe.wait_ge(ssl_ready, 1)
            for a in range(H // 2):
                last = tr(bank(6)[:, a * P:(a + 1) * P], qn[:, i, a * P:(a + 1) * P], ident[:])
            last.then_inc(qt_mm, 1)

        def cmp_scores(i):
            pe.wait_ge(q_st_ready, 2 * (i + 1))
            pe.wait_ge(kc_ready, 1)
            for h in range(H):
                last = mm(bank(6)[:, h * 2 * CW:(h + 1) * 2 * CW], q_st[i % 2][:, h, :],
                          kc_st[:, h // G].rearrange("p s n -> p (s n)"), start=True, stop=True)
            last.then_inc(cs_mm, 1)

        def cmp_turn(i):
            pe.wait_ge(cp_ready, i + 1)
            for kv in range(KV):
                last = tr(bank(6)[:, kv * P:(kv + 1) * P], c_s[:, kv * G:(kv + 1) * G, :].rearrange("p g n -> p (g n)"), ident[:])
            last.then_inc(ct_mm, 1)

        def cmp_values(i):
            pe.wait_ge(cpt_ready, i + 1)
            pe.wait_ge(vc_ready, 2 * G)
            for kv in range(KV):
                last = mm(bank(6)[:, kv * 256:(kv + 1) * 256], c_pt[:, kv, :], v_blk[:, kv, :], start=True, stop=True)
            last.then_inc(cpv_mm, 1)

        def scores(u):
            i, b, h = u // (2 * H), u % (2 * H) // H, u % H
            n = (i + 1) * P
            if u == 0:
                pe.wait_ge(k_lo, 2 * KV)
                pe.wait_ge(k_ready, 16 * 2 * KV)
                pe.wait_ge(gate_bc, 2)
                pe.wait_ge(qn_ready, T)
            if u >= 2:
                pe.wait_ge(biased, u - 1)
            pe.wait_ge(q_st_ready, 2 * (i + 1))
            for part in range(2):
                last = mm(score_bank(u)[:, 0:n], q_st[i % 2][:, h, :], k_st[:, b, h // G, part, 0:n], start=(part == 0), stop=(part == 1))
            last.then_inc(scores_done, 1)

        def turn(u):
            pe.wait_ge(probs, u + 1)
            if u == 1:
                pe.wait_ge(vc_ready, 2 * G)
            if u >= 2:
                pe.wait_ge(pt_lo_done, u - 1)
            for kt in range(u // (2 * H) + 1):
                last = tr(turned_bank(u)[:, kt * P:(kt + 1) * P], sc_sb[u % 3][:, kt * P:(kt + 1) * P], ident[:])
            last.then_inc(pt_done, 1)

        def values(u):
            i, b, h = u // (2 * H), u % (2 * H) // H, u % H
            pe.wait_ge(pt_lo_done, u + 1)
            if u % 4 == 0 and u >= 4:
                pe.wait_ge(o_scaled, u // 4)
            for kt in range(i + 1):
                for n, part in enumerate((pt_lo, pt_hi)):
                    last = mm(bank(7)[:, h % G * P:(h % G + 1) * P], part[u % 2][:, kt * P:(kt + 1) * P],
                              v_hl[:, b, h // G, kt, :], start=(kt == 0 and n == 0), stop=(kt == i and n == 1))
            last.then_inc(pv_done, 1)

        def filler(j):
            if j < 2 * KC:
                g, k = j // 4 % 2, j // 8 * 4 + j % 4
            else:
                g, k = j // KC, j % KC
            if g < 2 * T:
                t, p = g % T, (PZN if g < T else PZL) + k // 4
                if k == 0:
                    if g == 0:
                        pe.wait_ge(k_lo, 2 * KV)
                    elif g == 1:
                        pe.wait_ge(gate_bc, 2)
                    elif g < T + 2:
                        pe.wait_ge(zn_ready, g - 1)
                    else:
                        pe.wait_ge(yl_full, g - T - 1)
                if t == 0:
                    piece_in(p)
                ins = triple(p, k % 4, t % 2, k, (h_hi[:, k, :], h_lo[:, k, :]), t, k == 0, k == KC - 1, g >= T)
                if t == T - 1 and k == 3:
                    ins.then_inc(piece_done, 1)
                if k == KC - 1:
                    ins.then_inc(piece_done if t == T - 1 else z_done, 1)
            else:
                n, kk = (j - 64) // CT, j % CT
                half, t = n // T, n % T
                if kk == 0:
                    if n < 2:
                        pe.wait_ge(yl_ready, CT)
                    else:
                        pe.wait_ge(part_ready, n - 1)
                    if t == 0:
                        piece_in(PO + half)
                ins = triple(PO + half, kk, n % 2, kk, (yl_hi[:, kk, :], yl_lo[:, kk, :]), t, kk == 0, kk == CT - 1, False)
                if kk == CT - 1:
                    ins.then_inc(part_mm, 1)

        def y_turn(t):
            pe.wait_ge(y_ready, t + 1)
            if t >= 1:
                pe.wait_ge(yn_ready, CT * t)
            else:
                pe.wait_ge(o_init, T)
            for ct in range(CT):
                last = tr(bank(6)[:, ct * P:(ct + 1) * P], z_silu[:, t, ct * P:(ct + 1) * P], ident[:])
            last.then_inc(yt_mm, 1)

        def out_nsa(n, kk):
            half, t = OUT_ORDER[n]
            if kk == 0:
                if n < 2:
                    pe.wait_ge(part_ready, 2 * T - 1 + n)
                if n == 2 * T - 1:
                    pe.wait_ge(out_gated, 1)
                pe.wait_ge(yn_ready, CT * (t + 1))
                piece_in(PO + 2 + half)
            ins = triple(PO + 2 + half, kk, OUT_BANKS[n], kk, (yn_hi[:, kk, :], yn_lo[:, kk, :]), t, kk == 0, kk == CT - 1, False)
            if kk == CT - 1:
                ins.then_inc(out_mm, 1)

        def attention_step(u):
            i, r = u // (2 * H), u % (2 * H)
            if u < UNITS:
                scores(u)
            if u >= 4:
                values(u - 4)
            for j in FILL_OF.get(u, ()):
                if j < FILLS:
                    filler(j)
                else:
                    out_nsa((j - FILLS) // CT, (j - FILLS) % CT)
            if 2 <= u < UNITS + 2:
                turn(u - 2)
            if u == 0:
                cmp_turn(0)
            if u == 2:
                cmp_values(0)
            if u == LSS_AT:
                lru_squares()
            if u - 1 in Y_AT:
                y_turn(Y_AT.index(u - 1))
            if i + 1 < T and u < UNITS:
                if r == AT_Q_TURN:
                    q_turn(i + 1)
                if r == AT_C_SCORES:
                    cmp_scores(i + 1)
                if r == AT_C_TURN:
                    cmp_turn(i + 1)
                if r == AT_C_VALUES:
                    cmp_values(i + 1)

        pe.wait_ge(gate_used, 4)
        pe.wait_ge(k_lo, 2 * KV)
        pe.wait_ge(gl_ready, 2)
        for half in range(2):
            mm(bank(2 - half), ones[:], gacc[:, half * 512:half * 512 + 512], start=True, stop=True).then_inc(gate_mm, 1)
        for j in range(4):
            filler(j)
        value_weights()
        for j in range(4, 8):
            filler(j)
        q_turn(0)
        for j in range(8, 12):
            filler(j)
        cmp_scores(0)
        for j in range(12, FILL0):
            filler(j)
        for u in range(UNITS + 4):
            attention_step(u)

        for n in range(2, 2 * T):
            if n == 2:
                pe.wait_ge(biased, UNITS)
                pe.wait_ge(pt_lo_done, UNITS)
            if n == 4:
                y_turn(T - 1)
            if n == 6:
                pe.wait_ge(o_scaled, 4 * T)
            for kk in range(CT):
                out_nsa(n, kk)

    FILL0 = 16
    FILLS = 2 * T * (KC + CT)
    FILL_OF = {}
    for g, start, span in zip(range(2, 2 * T), (1, 9, 16, 21, 26, 34), (7, 7, 6, 6, 6, 6)):
        for k in range(KC):
            FILL_OF.setdefault(start + k * span // KC, []).append(g * KC + k)
    for n in range(2 * T):
        for kk in range(CT):
            FILL_OF.setdefault(44 + (CT * n + kk) // 2, []).append(2 * T * KC + n * CT + kk)
    for j in range(2 * CT):
        FILL_OF.setdefault(61 + j // 2, []).append(FILLS + j)
    ZN_AT, ZL_AT, PART_AT = [-1, 0, 8, 18], [22, 27, 34, 38], [47, 48, 51, 53, 55, 57, 59, 61]
    HI_AT = {11: 9, 14: 10, 37: 11, 41: 12, 56: 13, 61: 14}
    LO_AT = {2: 9, 3: 10, 9: 11, 10: 12, 13: 13, 15: 14}
    RSL_AT, LSS_AT = 45, 4
    SQ_AT, Y_AT = [28, 43, 58], [48, 51, 60]
    AT_Q_TURN, AT_Q_HI, AT_Q_LO = 6, 7, 8
    AT_C_SCORES, AT_C_SOFT, AT_C_MAX, AT_C_EXP = 9, 10, 11, 11
    AT_C_FACTOR, AT_C_TURN, AT_C_PT, AT_C_VALUES, AT_C_OUT = 12, 13, 13, 14, 15
    OUT_ORDER = [(0, 0), (0, 1), (0, 2), (1, 0), (1, 1), (1, 2), (0, 3), (1, 3)]
    OUT_BANKS = [0, 1, 2, 3, 4, 5, 7, 0]
    tail = [sb(f"tail{n}", [P, S], r_sb + 2048 * n) for n in range(2)]
    o_sq = sb("o_sq", [P, S], r_x1)

    with nc.Block() as block:
        block.sync(sync_program)
        block.gpsimd(pool_program)
        block.scalar(act_program)
        block.vector(dve_program)
        block.tensor(pe_program)


_INS = ['x', 'c', 'w_ada', 'b_ada', 'norm_g', 'w_in', 'conv_w', 'conv_b', 'w_rg_a', 'b_rg_a', 'w_rg_x', 'b_rg_x',
        'lru_lambda', 'cmp_pos_k', 'cmp_w1_k', 'cmp_w2_k', 'cmp_pos_v', 'cmp_w1_v', 'cmp_w2_v', 'g_q', 'g_k_cmp',
        'g_k_slc', 'g_k_win', 'g_out_lru', 'g_out_nsa', 'w_out']
_OUTS = [((1, 512, 1024), 'float32')]


def kernel(**inputs):
    import numpy as _np
    import concourse.bacc as _bacc
    from concourse import mybir as _mybir
    from concourse.bass_utils import run_bass_kernel_spmd as _run

    nc = _bacc.Bacc("TRN2", target_bir_lowering=False, num_devices=1)
    arrays, args = {}, []
    for name in _INS:
        a = _np.ascontiguousarray(inputs[name])
        arrays[f"in_{name}_dram"] = a
        args.append(nc.dram_tensor(f"in_{name}_dram", a.shape, _mybir.dt.from_np(a.dtype), kind="ExternalInput").ap())
    for i, (shape, dtype) in enumerate(_OUTS):
        dt = _mybir.dt.from_np(_np.dtype(dtype))
        args.append(nc.dram_tensor(f"out_{i}_dram", shape, dt, kind="ExternalOutput").ap())
    build(nc, *args)
    r = _run(nc, [arrays], core_ids=[0])
    got = tuple(r.results[0][f"out_{i}_dram"] for i in range(len(_OUTS)))
    return got[0]
```
